# Optimizing a Trainium2 kernel written in Bass

```python
import math
import jax, jax.numpy as jnp
from jax import lax
import numpy as np

D_MODEL = 2048
BATCH = 1
SEQ = 256
DEPTH = 1

GRID_W = 64
CTX_LEN = 256
N_MIXERS = 3
N_MOD = 6
MLP_HIDDEN = 4 * D_MODEL
NORM_EPS = 1e-6
FNET_GROUPS = 8
FNET_GROUP_DIM = D_MODEL // FNET_GROUPS
HGRN_EXPAND = 128
HGRN_HEADS = D_MODEL // HGRN_EXPAND
HGRN_DK = HGRN_EXPAND
HGRN_DV = D_MODEL // HGRN_HEADS
HGRN_F = HGRN_HEADS * HGRN_DK
HGRN_CHUNK = 16
DIFF_HEAD_DIM = 128
DIFF_HEADS = D_MODEL // (2 * DIFF_HEAD_DIM)
DIFF_V_DIM = 2 * DIFF_HEAD_DIM
Q_BLOCK = 128
ROPE_BASE = 10000.0


F32 = jnp.float32

def rms_norm(x, g):
    xf = x.astype(F32)
    y = xf * lax.rsqrt(jnp.mean(xf * xf, axis=-1, keepdims=True) + NORM_EPS)
    return (y * g.astype(F32)).astype(x.dtype)

def modulate(h, shift, scale):
    return h * (1 + scale) + shift

def sqrelu_mlp(h, w1, w2):
    return jnp.square(jax.nn.relu(h @ w1)) @ w2

def axial_rope_tables(n_tokens, dim):
    rows = n_tokens // GRID_W
    row = jnp.broadcast_to(jnp.arange(rows)[:, None], (rows, GRID_W)).reshape(-1).astype(F32)
    col = jnp.broadcast_to(jnp.arange(GRID_W)[None, :], (rows, GRID_W)).reshape(-1).astype(F32)
    n_freq = dim // 4
    inv = ROPE_BASE ** (-jnp.arange(n_freq, dtype=F32) / n_freq)
    ang = jnp.concatenate([row[:, None] * inv, col[:, None] * inv], axis=-1)
    return jnp.cos(ang), jnp.sin(ang)

def apply_rope(x, cos, sin):
    xf = x.astype(F32)
    x1, x2 = jnp.split(xf, 2, axis=-1)
    return jnp.concatenate([x1 * cos - x2 * sin, x1 * sin + x2 * cos], axis=-1).astype(x.dtype)

def fourier_mix(h):
    B, L, D = h.shape
    hg = h.astype(F32).reshape(B, L, FNET_GROUPS, FNET_GROUP_DIM)
    return jnp.fft.fftn(hg, axes=(1, 3)).real.reshape(B, L, D).astype(h.dtype)

def hgrn_lower_bounds(p):
    cs = jnp.cumsum(jax.nn.softmax(p.astype(F32), axis=0), axis=0)
    return cs - cs[0:1]

def chunk_gla(q, k, v, logf, s0):
    B, H, L, dk = q.shape
    C = HGRN_CHUNK
    N = L // C
    r = lambda t: jnp.moveaxis(t.astype(F32).reshape(B, H, N, C, t.shape[-1]), 2, 0)
    bcum = jnp.cumsum(logf.astype(F32).reshape(B, H, N, C, dk), axis=3)
    xs = (r(q), r(k), r(v), jnp.moveaxis(bcum, 2, 0))
    mask = jnp.tril(jnp.ones((C, C), dtype=bool))[:, :, None]

    def step(s, inp):
        qc, kc, vc, bc = inp
        bl = bc[:, :, -1:, :]
        decay = jnp.exp(jnp.where(mask, bc[:, :, :, None, :] - bc[:, :, None, :, :], -jnp.inf))
        a = jnp.einsum('bhtd,bhsd,bhtsd->bhts', qc, kc, decay)
        o = jnp.einsum('bhts,bhsv->bhtv', a, vc) + jnp.einsum('bhtd,bhdv->bhtv', qc * jnp.exp(bc), s)
        s = jnp.exp(bl[:, :, 0, :])[..., None] * s + jnp.einsum('bhsd,bhsv->bhdv', kc * jnp.exp(bl - bc), vc)
        return s, o

    s_final, o = lax.scan(step, s0.astype(F32), xs)
    return jnp.moveaxis(o, 0, 2).reshape(B, H, L, v.shape[-1]), s_final

def hgrn2_mixer(h_lat, h_ctx, w_in, lb, gnorm, w_out, ctx_out):
    lb = lb.reshape(2, HGRN_HEADS, HGRN_DK)

    def project(h):
        B, L, _ = h.shape
        q, zf, zb, v, g = jnp.split(h @ w_in, [HGRN_F, 2 * HGRN_F, 3 * HGRN_F, 3 * HGRN_F + D_MODEL], axis=-1)
        hd = lambda t: t.reshape(B, L, HGRN_HEADS, -1).transpose(0, 2, 1, 3)
        return hd(q), hd(zf), hd(zb), hd(v), hd(g)

    def forget(z, lbd):
        zf = z.astype(F32)
        l = lbd[None, :, None, :]
        logf = jnp.logaddexp(jnp.log(l), jnp.log1p(-l) + jax.nn.log_sigmoid(zf))
        key = (1 - l) * jax.nn.sigmoid(-zf)
        return logf, key

    def readout(o, g, dtype):
        B, H, L, _ = o.shape
        y = rms_norm(o, gnorm) * jax.nn.silu(g.astype(F32))
        return y.transpose(0, 2, 1, 3).reshape(B, L, H * HGRN_DV).astype(dtype) @ w_out

    flip = lambda t: jnp.flip(t, axis=2)
    qc, zfc, zbc, vc, gc = project(h_ctx)
    ql, zfl, zbl, vl, gl = project(h_lat)
    s0 = jnp.zeros((qc.shape[0], HGRN_HEADS, HGRN_DK, HGRN_DV), F32)
    lfc, kfc = forget(zfc, lb[0])
    o_cf, s_f = chunk_gla(qc, kfc, vc, lfc, s0)
    lfl, kfl = forget(zfl, lb[0])
    o_lf, _ = chunk_gla(ql, kfl, vl, lfl, s_f)
    lbc, kbc = forget(zbc, lb[1])
    o_cb, s_b = chunk_gla(flip(qc), flip(kbc), flip(vc), flip(lbc), s0)
    lbl, kbl = forget(zbl, lb[1])
    o_lb, _ = chunk_gla(flip(ql), flip(kbl), flip(vl), flip(lbl), s_b)
    y_lat = readout(o_lf + flip(o_lb), gl, h_lat.dtype)
    y_ctx = readout(o_cf + flip(o_cb), gc, h_ctx.dtype) if ctx_out else None
    return y_lat, y_ctx

def diff_core(q, k, v, lam):
    s = jnp.einsum('bhmqd,bhmkd->bhmqk', q, k).astype(F32) * (DIFF_HEAD_DIM ** -0.5)
    p = jax.nn.softmax(s, axis=-1)
    a = p[:, :, 0] - lam * p[:, :, 1]
    return jnp.einsum('bhqk,bhkv->bhqv', a.astype(v.dtype), v)

def diff_attention(h_lat, h_ctx, w_qkv, lam_p, subln, w_out, lambda_init, cos, sin, ctx_out):
    def project(h):
        B, L, _ = h.shape
        q, k, v = jnp.split(h @ w_qkv, 3, axis=-1)
        q = q.reshape(B, L, DIFF_HEADS, 2, DIFF_HEAD_DIM).transpose(0, 2, 3, 1, 4)
        k = k.reshape(B, L, DIFF_HEADS, 2, DIFF_HEAD_DIM).transpose(0, 2, 3, 1, 4)
        v = v.reshape(B, L, DIFF_HEADS, DIFF_V_DIM).transpose(0, 2, 1, 3)
        return q, k, v

    def merge(o, dtype):
        B, H, L, _ = o.shape
        o = rms_norm(o, subln) * (1 - lambda_init)
        return o.transpose(0, 2, 1, 3).reshape(B, L, H * DIFF_V_DIM).astype(dtype) @ w_out

    lp = lam_p.astype(F32)
    lam = jnp.exp(jnp.sum(lp[0] * lp[1])) - jnp.exp(jnp.sum(lp[2] * lp[3])) + lambda_init
    q_c, k_c, v_c = project(h_ctx)
    q_l, k_l, v_l = project(h_lat)
    q_l, k_l = apply_rope(q_l, cos, sin), apply_rope(k_l, cos, sin)
    k_all = jnp.concatenate([k_c, k_l], axis=3)
    v_all = jnp.concatenate([v_c, v_l], axis=2)
    B, H, _, L, d = q_l.shape
    nb = L // Q_BLOCK
    q_blocks = jnp.moveaxis(q_l.reshape(B, H, 2, nb, Q_BLOCK, d), 3, 0)
    o_blocks = lax.map(lambda qb: diff_core(qb, k_all, v_all, lam), q_blocks)
    o_l = jnp.moveaxis(o_blocks, 0, 2).reshape(B, H, L, DIFF_V_DIM)
    y_lat = merge(o_l, h_lat.dtype)
    y_ctx = merge(diff_core(q_c, k_c, v_c, lam), h_ctx.dtype) if ctx_out else None
    return y_lat, y_ctx

def first_inputs(seed: int = 0) -> dict:
    key = jax.random.key(seed)
    ks = jax.random.split(key, 20)
    n_slot = lambda m: len(range(m, DEPTH, N_MIXERS))
    n_a, n_b, n_c = n_slot(0), n_slot(1), n_slot(2)
    D = D_MODEL
    nrm = lambda k, shape, s: jax.random.normal(k, shape, F32) * s
    return {
        'x': nrm(ks[0], (BATCH, SEQ, D), 1.0),
        'c': nrm(ks[1], (BATCH, D), 1.0),
        'ctx': nrm(ks[2], (BATCH, CTX_LEN, D), 1.0),
        'c_ctx': nrm(ks[3], (D,), 1.0),
        'w_mod': nrm(ks[4], (DEPTH, D, N_MOD * D), D ** -0.5),
        'b_mod': nrm(ks[5], (DEPTH, N_MOD * D), 0.01),
        'norm_g': 1.0 + nrm(ks[6], (DEPTH, 4, D), 0.02),
        'w_mlp_in': nrm(ks[7], (DEPTH, D, MLP_HIDDEN), D ** -0.5),
        'w_mlp_out': nrm(ks[8], (DEPTH, MLP_HIDDEN, D), MLP_HIDDEN ** -0.5),
        'fnet_w_out': nrm(ks[9], (n_a, D, D), D ** -0.5),
        'hgrn_w_in': nrm(ks[10], (n_b, D, 3 * HGRN_F + 2 * D), D ** -0.5),
        'hgrn_lb': nrm(ks[11], (DEPTH, 2, HGRN_F), 0.1),
        'hgrn_gnorm': 1.0 + nrm(ks[12], (n_b, HGRN_DV), 0.02),
        'hgrn_w_out': nrm(ks[13], (n_b, D, D), D ** -0.5),
        'diff_w_qkv': nrm(ks[14], (n_c, D, 3 * D), D ** -0.5),
        'diff_lambda': nrm(ks[15], (n_c, 4, DIFF_HEAD_DIM), 0.1),
        'diff_subln': 1.0 + nrm(ks[16], (n_c, DIFF_V_DIM), 0.02),
        'diff_w_out': nrm(ks[17], (n_c, D, D), D ** -0.5),
    }

def first_block(x, c, ctx, c_ctx, w_mod, b_mod, norm_g, w_mlp_in, w_mlp_out, fnet_w_out, hgrn_w_in, hgrn_lb, hgrn_gnorm, hgrn_w_out, diff_w_qkv, diff_lambda, diff_subln, diff_w_out):
    L = x.shape[1]
    cos, sin = axial_rope_tables(L, DIFF_HEAD_DIM)
    lower_bounds = hgrn_lower_bounds(hgrn_lb)
    silu_c = jax.nn.silu(c)
    silu_cc = jax.nn.silu(c_ctx)
    for i in range(DEPTH):
        mixer, slot = i % N_MIXERS, i // N_MIXERS
        ctx_out = i < DEPTH - 1
        ctx_in = ctx_out or mixer != 0
        sh1, sc1, g1, sh2, sc2, g2 = jnp.split((silu_c @ w_mod[i] + b_mod[i])[:, None, :], N_MOD, axis=-1)
        h_lat = modulate(rms_norm(x, norm_g[i, 0]), sh1, sc1)
        h_ctx = None
        if ctx_in:
            csh1, csc1, cg1, csh2, csc2, cg2 = jnp.split(silu_cc @ w_mod[i] + b_mod[i], N_MOD, axis=-1)
            h_ctx = modulate(rms_norm(ctx, norm_g[i, 0]), csh1, csc1)
        if mixer == 0:
            y_lat = fourier_mix(h_lat) @ fnet_w_out[slot]
            y_ctx = fourier_mix(h_ctx) @ fnet_w_out[slot] if ctx_out else None
        elif mixer == 1:
            y_lat, y_ctx = hgrn2_mixer(h_lat, h_ctx, hgrn_w_in[slot], lower_bounds[i], hgrn_gnorm[slot], hgrn_w_out[slot], ctx_out)
        else:
            lambda_init = 0.8 - 0.6 * math.exp(-0.3 * i)
            y_lat, y_ctx = diff_attention(h_lat, h_ctx, diff_w_qkv[slot], diff_lambda[slot], diff_subln[slot], diff_w_out[slot], lambda_init, cos, sin, ctx_out)
        x = x + g1 * rms_norm(y_lat, norm_g[i, 1])
        x = x + g2 * rms_norm(sqrelu_mlp(modulate(rms_norm(x, norm_g[i, 2]), sh2, sc2), w_mlp_in[i], w_mlp_out[i]), norm_g[i, 3])
        if ctx_out:
            ctx = ctx + cg1 * rms_norm(y_ctx, norm_g[i, 1])
            ctx = ctx + cg2 * rms_norm(sqrelu_mlp(modulate(rms_norm(ctx, norm_g[i, 2]), csh2, csc2), w_mlp_in[i], w_mlp_out[i]), norm_g[i, 3])
    return x


CHUNK = 64
HEAD_DIM = 128
N_HEADS_SB = 8
N_HEADS_FOX = 8
W_SB = N_HEADS_SB * HEAD_DIM
W_FOX = N_HEADS_FOX * HEAD_DIM
MIX_WIDTH = W_SB + W_FOX
IN_COLS = 3 * W_SB + 3 * W_FOX + N_HEADS_FOX
D_FF = 4 * D_MODEL
EPS = 1e-6


def rmsnorm(x, g):
    xf = x.astype(jnp.float32)
    var = jnp.mean(xf * xf, axis=-1, keepdims=True)
    return (xf * lax.rsqrt(var + EPS) * g.astype(jnp.float32)).astype(x.dtype)

def head_rmsnorm(o, g):
    of = o.astype(jnp.float32)
    of = of * lax.rsqrt(jnp.mean(of * of, axis=-1, keepdims=True) + EPS)
    b, h, s, d = o.shape
    of = jnp.transpose(of, (0, 2, 1, 3)).reshape(b, s, h * d)
    return (of * g.astype(jnp.float32)).astype(o.dtype)

def split_heads(t, n_heads):
    b, s, _ = t.shape
    return jnp.transpose(t.reshape(b, s, n_heads, HEAD_DIM), (0, 2, 1, 3))

def stick_breaking_attention(q, k, v):
    seq = q.shape[2]
    scale = HEAD_DIM ** -0.5
    outs = []
    for i in range(seq // Q_BLOCK):
        end = (i + 1) * Q_BLOCK
        qb = q[:, :, i * Q_BLOCK:end]
        kb = k[:, :, :end]
        vb = v[:, :, :end]
        z = jnp.einsum('bhqd,bhkd->bhqk', qb, kb).astype(jnp.float32) * scale
        t_pos = i * Q_BLOCK + jnp.arange(Q_BLOCK)
        s_pos = jnp.arange(end)
        causal = s_pos[None, :] < t_pos[:, None]
        log_beta = jax.nn.log_sigmoid(z)
        log_keep = jnp.where(causal, jax.nn.log_sigmoid(-z), 0.0)
        rest = lax.cumsum(log_keep, axis=3, reverse=True) - log_keep
        a = jnp.where(causal, jnp.exp(log_beta + rest), 0.0)
        outs.append(jnp.einsum('bhqk,bhkd->bhqd', a.astype(v.dtype), vb))
    return jnp.concatenate(outs, axis=2)

def forgetting_attention(q, k, v, log_f):
    seq = q.shape[2]
    scale = HEAD_DIM ** -0.5
    c = lax.cumsum(log_f.astype(jnp.float32), axis=2)
    outs = []
    for i in range(seq // Q_BLOCK):
        end = (i + 1) * Q_BLOCK
        qb = q[:, :, i * Q_BLOCK:end]
        kb = k[:, :, :end]
        vb = v[:, :, :end]
        z = jnp.einsum('bhqd,bhkd->bhqk', qb, kb).astype(jnp.float32) * scale
        z = z + c[:, :, i * Q_BLOCK:end, None] - c[:, :, None, :end]
        t_pos = i * Q_BLOCK + jnp.arange(Q_BLOCK)
        s_pos = jnp.arange(end)
        causal = s_pos[None, :] <= t_pos[:, None]
        p = jax.nn.softmax(jnp.where(causal, z, -jnp.inf), axis=-1)
        outs.append(jnp.einsum('bhqk,bhkd->bhqd', p.astype(v.dtype), vb))
    return jnp.concatenate(outs, axis=2)

def second_inputs(seed: int = 0) -> dict:
    key = jax.random.key(seed)
    ks = jax.random.split(key, 12)
    f32 = jnp.float32
    x = jax.random.normal(ks[0], (BATCH, SEQ, D_MODEL), f32)
    g_attn = 1.0 + 0.05 * jax.random.normal(ks[1], (DEPTH, D_MODEL), f32)
    w_in = jax.random.normal(ks[2], (DEPTH, D_MODEL, IN_COLS), f32) * D_MODEL ** -0.5
    b_f = jax.random.uniform(ks[3], (DEPTH, N_HEADS_FOX), f32, 1.0, 4.0)
    g_out_sb = 1.0 + 0.05 * jax.random.normal(ks[4], (DEPTH, W_SB), f32)
    g_out_fox = 1.0 + 0.05 * jax.random.normal(ks[5], (DEPTH, W_FOX), f32)
    w_out = jax.random.normal(ks[6], (DEPTH, MIX_WIDTH, D_MODEL), f32) * MIX_WIDTH ** -0.5
    g_mlp = 1.0 + 0.05 * jax.random.normal(ks[7], (DEPTH, D_MODEL), f32)
    w_up = jax.random.normal(ks[8], (DEPTH, D_MODEL, D_FF), f32) * D_MODEL ** -0.5
    w_down = jax.random.normal(ks[9], (DEPTH, D_FF, D_MODEL), f32) * D_FF ** -0.5
    g_final = 1.0 + 0.05 * jax.random.normal(ks[10], (D_MODEL,), f32)
    return {"x": x, "g_attn": g_attn, "w_in": w_in, "b_f": b_f,
            "g_out_sb": g_out_sb, "g_out_fox": g_out_fox, "w_out": w_out,
            "g_mlp": g_mlp, "w_up": w_up, "w_down": w_down, "g_final": g_final}

def second_block(x, g_attn, w_in, b_f, g_out_sb, g_out_fox, w_out, g_mlp, w_up, w_down, g_final):
    o0 = 3 * W_SB
    o1 = o0 + 3 * W_FOX
    for l in range(DEPTH):
        h = rmsnorm(x, g_attn[l])
        proj = jnp.einsum('bsd,de->bse', h, w_in[l])
        qa = split_heads(proj[..., 0:W_SB], N_HEADS_SB)
        ka = split_heads(proj[..., W_SB:2 * W_SB], N_HEADS_SB)
        va = split_heads(proj[..., 2 * W_SB:o0], N_HEADS_SB)
        qf = split_heads(proj[..., o0:o0 + W_FOX], N_HEADS_FOX)
        kf = split_heads(proj[..., o0 + W_FOX:o0 + 2 * W_FOX], N_HEADS_FOX)
        vf = split_heads(proj[..., o0 + 2 * W_FOX:o1], N_HEADS_FOX)
        f_logit = proj[..., o1:].astype(jnp.float32) + b_f[l].astype(jnp.float32)
        log_f = jnp.transpose(jax.nn.log_sigmoid(f_logit), (0, 2, 1))

        o_sb = stick_breaking_attention(qa, ka, va)
        o_fox = forgetting_attention(qf, kf, vf, log_f)
        mixed = jnp.concatenate([head_rmsnorm(o_sb, g_out_sb[l]),
                                 head_rmsnorm(o_fox, g_out_fox[l])], axis=-1)
        x = x + jnp.einsum('bse,ed->bsd', mixed, w_out[l])

        h2 = rmsnorm(x, g_mlp[l])
        u = jax.nn.relu(jnp.einsum('bsd,df->bsf', h2, w_up[l]))
        x = x + jnp.einsum('bsf,fd->bsd', u * u, w_down[l])
    return rmsnorm(x, g_final)


def setup_inputs(seed=0):
    out = dict(first_inputs(seed))
    for name, value in second_inputs(seed + 1).items():
        if name != "x":
            out[name + "_2"] = value
    return out


def reference(
    x, c, ctx, c_ctx, w_mod, b_mod, norm_g, w_mlp_in, w_mlp_out, fnet_w_out, hgrn_w_in, hgrn_lb,
    hgrn_gnorm, hgrn_w_out, diff_w_qkv, diff_lambda, diff_subln, diff_w_out, g_attn_2, w_in_2,
    b_f_2, g_out_sb_2, g_out_fox_2, w_out_2, g_mlp_2, w_up_2, w_down_2, g_final_2,
):
    x = first_block(
        x, c, ctx, c_ctx, w_mod, b_mod, norm_g, w_mlp_in, w_mlp_out, fnet_w_out, hgrn_w_in,
        hgrn_lb, hgrn_gnorm, hgrn_w_out, diff_w_qkv, diff_lambda, diff_subln, diff_w_out,
    )
    return second_block(
        x, g_attn_2, w_in_2, b_f_2, g_out_sb_2, g_out_fox_2, w_out_2, g_mlp_2, w_up_2, w_down_2,
        g_final_2,
    )


_drawn_inputs = setup_inputs


def setup_inputs(seed=0):
    import zlib

    import numpy as np

    out = dict(_drawn_inputs(seed))
    spreads = {}
    factors = {'b_mod': 3.573}
    for name, (base, spread) in spreads.items():
        noise = np.random.default_rng([zlib.crc32(name.encode()), seed]).standard_normal(out[name].shape)
        drawn = base * np.exp(spread * noise) if base else spread * noise
        out[name] = __import__('jax').numpy.asarray(drawn.astype(out[name].dtype))
    for name, factor in factors.items():
        out[name] = (out[name] * factor).astype(out[name].dtype)
    return out
```

```python
from collections import defaultdict
from contextlib import ExitStack, contextmanager

import numpy as np

import concourse.bass as bass
from concourse import mybir

P = 128
SEQ = 256
D = 2048
TT = SEQ // P
KT = D // P
CW = 512
NC = D // CW
HALVES = KT // 2
LEAD = 4
RAW = 4
QUARTERS = 4
HD = 128
HEADS = 8
GH = 4
GROUPS = 4
EPS = 1e-6
GROUP_DIM = 256
FG = D // GROUP_DIM
MASKED = -1e30

C_ID, C_GE, C_LE, C_ONE, C_SB, C_FOX = 0, 128, 256, 384, 512, 896
C_ALL = 1280

V_C, V_G0, V_G2, V_GA, V_GM, V_GO = (KT * i for i in range(6))
V_ALL = 6 * KT

MOD_AFTER = (6, 14, 22, 30)

SLOTS = {5: (("z", 0),), 7: (("z", 1), ("mid", 0)), 10: (("z", 2), ("mid", 1), ("out", 0)),
         13: (("z", 3), ("mid", 2), ("out", 1)), 15: (("mid", 3), ("out", 2)), 18: (("out", 3),),
         21: (("turn", 0),), 23: (("turn", 1),)}
LAST_SLOTS = {0: (("z", 0),), 2: (("z", 1), ("mid", 0)), 4: (("z", 2), ("mid", 1), ("out", 0)),
              6: (("z", 3), ("mid", 2), ("out", 1)), 8: (("mid", 3), ("out", 2)), 9: (("out", 3),),
              11: (("turn", 0), ("turn", 1))}
OUT_ORDER = [(0, 0), (0, 1), (0, 2), (1, 0), (1, 1), (1, 2), (0, 3), (1, 3)] + \
            [(c, j) for c in (2, 3) for j in range(4)]


class Tally:

    def __init__(self):
        self.c = defaultdict(int)
        self.q, self.start, self.per = None, 0, {}

    def at(self, name, d=0):
        v = self.c[name] + d
        per = self.per.get(name, 0)
        return v if self.q is None or per == 0 else self.q * per + (v - self.start * per)

    def add(self, name, k=1):
        self.c[name] += k

    def arrived(self):
        v = 16 * (self.c["raw"] // RAW + 1)
        per = 16 * (self.per.get("raw", 0) // RAW)
        return v if self.q is None or per == 0 else self.q * per + (v - self.start * per)

    @contextmanager
    def loop(self, eng, start, stop, **per):
        before = dict(self.c)
        with eng.Fori(start, stop) as q:
            self.q, self.start, self.per = q, start, per
            yield q
        self.q, self.start, self.per = None, 0, {}
        for name in set(self.c) | set(per):
            one = self.c[name] - before.get(name, 0)
            assert one == per.get(name, 0), (name, one)
            self.c[name] = before.get(name, 0) + one * (stop - start)


def in_column(g, r):
    kind, part = divmod(g, 2)
    return kind * 3 * HEADS * HD + r * HEADS * HD + part * CW


def program(nc, x, c_in, w_mod, b_mod, norm_g, w_mlp_in, w_mlp_out, fnet_w, g_attn, w_in, b_f,
            g_out_sb, g_out_fox, w_out, g_mlp, w_up, w_down, g_final, consts, dft, select, out):
    dt = mybir.dt
    f32, f32r = dt.float32, dt.float32r
    ACT = mybir.ActivationFunctionType
    ALU = mybir.AluOpType
    AX = mybir.AxisListType

    ctx = ExitStack()
    with ctx:
        def sb(name, shape, dtype=f32):
            return ctx.enter_context(nc.sbuf_tensor(name, shape, dtype))

        def sem(name):
            return ctx.enter_context(nc.semaphore(name))

        raw = sb("raw", [P, RAW, 4 * CW])
        w_high = sb("w_high", [P, LEAD, 2 * CW], f32r)
        w_low = sb("w_low", [P, LEAD, 2 * CW], f32r)
        h_high = sb("h_high", [P, KT, SEQ], f32r)
        h_low = sb("h_low", [P, KT, SEQ], f32r)
        u_high = sb("u_high", [P, KT, SEQ], f32r)
        u_low = sb("u_low", [P, KT, SEQ], f32r)
        xs = sb("xs", [P, TT, D])
        acc = sb("acc", [P, TT, D])
        grow = sb("grow", [P, D])
        scr = sb("scr", [P, 2 * D])
        extra = sb("extra", [P, 1536])
        junk = sb("junk", [P, CW])
        probs = sb("probs", [P, 2, 384])
        fin = sb("fin", [P, CW])
        cst = sb("cst", [P, C_ALL])
        cols = sb("cols", [P, V_ALL])
        silu_t = sb("silu_t", [P, 2 * KT])
        silu_c = sb("silu_c", [P, KT])
        mcol = sb("mcol", [P, 4 * KT])
        scale1 = sb("scale1", [P, KT])
        scale2 = sb("scale2", [P, KT])
        shift1 = sb("shift1", [P, KT])
        ssq = sb("ssq", [P, TT * NC])
        ms = sb("ms", [P, TT])
        sd = sb("sd", [P, TT])
        rstd = sb("rstd", [P, TT])
        wf = sb("wf", [P, KT * HEADS])
        wf_high = sb("wf_high", [P, KT * HEADS], f32r)
        wf_low = sb("wf_low", [P, KT * HEADS], f32r)
        bf = sb("bf", [P, TT * HEADS])
        fl = sb("fl", [P, TT * HEADS])
        fe = sb("fe", [P, TT * HEADS])
        csum = sb("csum", [P, TT * HEADS])
        negmax = sb("negmax", [P, TT * GH])
        psums = sb("psums", [P, TT * GH])
        precip = sb("precip", [P, TT * GH])
        hms = sb("hms", [P, TT * GH])
        hsd = sb("hsd", [P, TT * GH])
        hrs = sb("hrs", [P, TT * GH])
        ps = ctx.enter_context(nc.psum_tensor("ps", [P, 8, CW], f32))

        def lin(n):
            return ps[:, 2 * (n % 2):2 * (n % 2) + 2, :]

        def side(b):
            return ps[:, 4 + b, :]

        ident = cst[:, C_ID:C_ID + P]
        ones = cst[:, C_ONE:C_ONE + P]
        mod_acc = scr[:, D:2 * D]
        xn = scr[:, :].rearrange("p (t n) -> p t n", t=TT)
        relu = scr[:, 0:TT * CW].rearrange("p (t n) -> p t n", t=TT)
        hidden = scr[:, TT * CW:2 * TT * CW].rearrange("p (t n) -> p t n", t=TT)
        seq_dft = scr[:, 0:D].rearrange("p (b d n) -> p b d n", b=2, d=2)
        tables = extra[:, :].rearrange("p (t n) -> p t n", t=2)
        turned = extra[:, 0:2 * CW].rearrange("p (b n) -> p b n", b=2)
        qT = acc[:, 0, :].rearrange("p (b h s) -> p b h s", b=2, h=GH)
        kT = acc[:, 1, :].rearrange("p (b h s) -> p b h s", b=2, h=GH)
        vv = grow[:, :].rearrange("p (b t n) -> p b t n", b=2, t=TT)
        stage = scr[:, 0:TT * CW].rearrange("p (t n) -> p t n", t=TT)
        heads = scr[:, TT * CW:2 * TT * CW].rearrange("p (t n) -> p t n", t=TT)
        normed = scr[:, 2 * TT * CW:3 * TT * CW].rearrange("p (t n) -> p t n", t=TT)
        sel = scr[0:HEADS, 3 * TT * CW:4 * TT * CW].rearrange("p (h n) -> p h n", h=HEADS)
        zs = extra[:, 0:768].rearrange("p (b n) -> p b n", b=2)
        ew = extra[:, 768:1536].rearrange("p (b n) -> p b n", b=2)
        negc = sb("negc", [HEADS, SEQ])

        raw_loaded = [sem(f"raw_loaded{i}") for i in range(RAW)]
        raw_used = sem("raw_used")
        high_ready = sem("high_ready")
        low_ready = sem("low_ready")
        half_used = sem("half_used")
        x_in, cst_in, dft_in, vec_in = sem("x_in"), sem("cst_in"), sem("dft_in"), sem("vec_in")
        grow_in, gate_in, sel_in = sem("grow_in"), sem("gate_in"), sem("sel_in")
        vec_turned, vec_ready = sem("vec_turned"), sem("vec_ready")
        act_link, vec_link, pool_link = sem("act_link"), sem("vec_link"), sem("pool_link")
        silu_exp, silu_ready = sem("silu_exp"), sem("silu_ready")
        acc_init = sem("acc_init")
        mod_step = sem("mod_step")
        mod_read = sem("mod_read")
        mod_cols = sem("mod_cols")
        squared = sem("squared")
        ms_ready, sd_ready, rstd_ready = sem("ms_ready"), sem("sd_ready"), sem("rstd_ready")
        yn_ready = sem("yn_ready")
        seq_done, scaled, dft_done = sem("seq_done"), sem("scaled"), sem("dft_done")
        dft_high, dft_low = sem("dft_high"), sem("dft_low")
        acc_zero = sem("acc_zero")
        summed = sem("summed")
        up_taken, up_ready = sem("up_taken"), sem("up_ready")
        t_posed, t_high, t_low = sem("t_posed"), sem("t_high"), sem("t_low")
        xn_ready, n_posed = sem("xn_ready"), sem("n_posed")
        n_scaled, n_high, n_low = sem("n_scaled"), sem("n_high"), sem("n_low")
        gated = sem("gated")
        x_updated = sem("x_updated")
        qkv_taken = sem("qkv_taken")
        a_posed, a_turned = sem("a_posed"), sem("a_turned")
        f_raw, f_high, f_low = sem("f_raw"), sem("f_high"), sem("f_low")
        f_sum, f_exp, f_logit, f_ready = sem("f_sum"), sem("f_exp"), sem("f_logit"), sem("f_ready")
        c_sum, c_ready = sem("c_sum"), sem("c_ready")
        z_ready, z_taken, z_logs = sem("z_ready"), sem("z_taken"), sem("z_logs")
        mid_in, mid_ready, mid_taken = sem("mid_in"), sem("mid_ready"), sem("mid_taken")
        fox_exp = sem("fox_exp")
        probs_ready = sem("probs_ready")
        o_ready, o_taken = sem("o_ready"), sem("o_taken")
        hms_ready, hsd_ready, mixed_ready = sem("hms_ready"), sem("hsd_ready"), sem("mixed_ready")
        m_posed, m_scaled, m_high, m_low = sem("m_posed"), sem("m_scaled"), sem("m_high"), sem("m_low")
        final_scaled, final_ready, out_done = sem("final_scaled"), sem("final_ready"), sem("out_done")

        block = ctx.enter_context(nc.Block())

        @block.sync
        def _(eng):
            t = Tally()

            def load(src, shape=None):
                slot = t.c["raw"] % RAW
                if t.c["raw"] >= RAW or t.q is not None:
                    eng.wait_ge(raw_used, t.at("raw", 1 - RAW))
                dst = raw[:, slot, :]
                if shape is not None:
                    dst = dst.rearrange("p (k n) -> p k n", k=4)
                eng.dma_start(dst, src).then_inc(raw_loaded[slot], 16)
                t.add("raw")

            def chunk(w, row, col):
                load(w[bass.ds(row, 4 * P), bass.ds(col, CW)].rearrange("(k p) n -> p k n", p=P), 4)

            def mod_tile(unit, kk):
                load(w_mod[bass.ds(kk * P, P), unit * D:(unit + 1) * D])

            for i in range(RAW):
                mod_tile(0, i)
            for unit in range(3):
                with t.loop(eng, 1 if unit == 0 else 0, KT // RAW, raw=RAW) as q:
                    for i in range(RAW):
                        mod_tile(unit, q * RAW + i)
            with t.loop(eng, 0, NC, raw=8) as c:
                for j in range(4):
                    chunk(fnet_w, j * 4 * P, c * CW)
                    mod_tile(3, c * 4 + j)
            with t.loop(eng, 0, KT // RAW, raw=RAW) as q:
                for i in range(RAW):
                    mod_tile(4, q * RAW + i)

            def mlp_chunk(w1, w2, q, ch):
                step, j = divmod(ch, 4)
                if step < NC:
                    chunk(w1, j * 4 * P, q * D + step * CW)
                else:
                    chunk(w2, q * D + j * 4 * P, (step - NC) * CW)

            chunk(w_mlp_in, 0, 0)
            chunk(w_mlp_in, 4 * P, 0)

            def mlp1_body(q, then):
                for pos in range(32):
                    if pos < 30:
                        mlp_chunk(w_mlp_in, w_mlp_out, q, pos + 2)
                    else:
                        then(pos - 30)
                    if pos in MOD_AFTER:
                        mod_tile(5, q * 4 + MOD_AFTER.index(pos))

            with t.loop(eng, 0, QUARTERS - 1, raw=36) as q:
                mlp1_body(q, lambda j: chunk(w_mlp_in, j * 4 * P, (q + 1) * D))
            mlp1_body(QUARTERS - 1, lambda j: chunk(w_in, j * 4 * P, in_column(0, 0)))
            for g in range(GROUPS):
                for r in range(3):
                    for j in range(2 if g == r == 0 else 0, 4):
                        chunk(w_in, j * 4 * P, in_column(g, r))
            for c, j in OUT_ORDER:
                chunk(w_out, j * 4 * P, c * CW)
            chunk(w_up, 0, 0)
            chunk(w_up, 4 * P, 0)
            with t.loop(eng, 0, QUARTERS - 1, raw=32) as q:
                for ch in range(2, 32):
                    mlp_chunk(w_up, w_down, q, ch)
                for j in range(2):
                    chunk(w_up, j * 4 * P, (q + 1) * D)
            for ch in range(2, 32):
                mlp_chunk(w_up, w_down, QUARTERS - 1, ch)
            outv = out.rearrange("(t p) n -> p t n", p=P)
            for i in range(TT * NC):
                tt, j = divmod(i, NC)
                eng.wait_ge(final_ready, i + 1)
                eng.dma_start(outv[:, tt, j * CW:(j + 1) * CW], acc[:, tt, j * CW:(j + 1) * CW])\
                   .then_inc(out_done, 16)
            eng.wait_ge(out_done, 16 * TT * NC)

        @block.gpsimd
        def _(eng):
            for v in range(6):
                if v:
                    eng.wait_ge(mod_read, v)
                if v == 5:
                    eng.wait_ge(n_posed, TT * NC)
                eng.memset(mod_acc, 0.0).then_inc(pool_link, 1)
                eng.wait_ge(pool_link, v + 1)
                eng.dma_start(scr[0:1, D:2 * D], b_mod[0:1, v * D:(v + 1) * D]).then_inc(acc_init, 16)
                if v == 0:
                    eng.dma_start(grow[:, :], norm_g[1:2, :].broadcast_to([P, D])).then_inc(grow_in, 16)
                    eng.dma_start(wf[:, :].rearrange("p (k n) -> p k n", k=KT),
                                  w_in[:, 6 * HEADS * HD:6 * HEADS * HD + HEADS]
                                  .rearrange("(k p) n -> p k n", p=P)).then_inc(f_raw, 16)
                    for tt in range(TT):
                        eng.dma_start(bf[:, tt * HEADS:(tt + 1) * HEADS],
                                      b_f.broadcast_to([P, HEADS])).then_inc(f_raw, 16)
                if v == 2:
                    eng.wait_ge(seq_done, FG)
                    eng.memset(acc[:, :, :], 0.0).then_inc(acc_zero, 1)
                if v == 5:
                    eng.wait_ge(x_updated, TT * NC)
                    eng.memset(acc[:, :, :], 0.0).then_inc(acc_zero, 1)
                    eng.dma_start(grow[:, :], norm_g[3:4, :].broadcast_to([P, D])).then_inc(grow_in, 16)
            eng.wait_ge(n_posed, 2 * TT * NC)
            eng.dma_start(sel, select).then_inc(sel_in, 16)
            eng.wait_ge(o_ready, GROUPS * GH)
            eng.dma_start(grow[:, :], g_final.broadcast_to([P, D])).then_inc(grow_in, 16)

        @block.tensor
        def _(eng):
            t = Tally()

            def half(n, hh, high, low):
                slot = t.c["half"] % LEAD
                eng.wait_ge(low_ready, t.at("half", 1))
                for tt in range(TT):
                    for kk in range(2):
                        k = 2 * hh + kk
                        wh = w_high[:, slot, kk * CW:(kk + 1) * CW]
                        wl = w_low[:, slot, kk * CW:(kk + 1) * CW]
                        ah = high[:, k, tt * P:(tt + 1) * P]
                        al = low[:, k, tt * P:(tt + 1) * P]
                        dst = lin(n)[:, tt, :]
                        eng.matmul(dst, ah, wh, start=(k == 0), stop=False)
                        eng.matmul(dst, ah, wl, start=False, stop=False)
                        last = eng.matmul(dst, al, wh, start=False, stop=(k == KT - 1))
                last.then_inc(half_used, 1)
                t.add("half")

            def sum_partitions_to_columns(v, place):
                eng.wait_ge(mod_step, KT * (v + 1))
                if place:
                    eng.wait_ge(mod_cols, t.c["mod_cols"])
                for j in range(KT):
                    last = eng.matmul(side(3)[:, place * KT + j:place * KT + j + 1],
                                      mod_acc[:, j * P:(j + 1) * P], ones[:, 0:1], start=True, stop=True)
                last.then_inc(mod_read, 1)
                t.add("mod_cols")

            def sum_partitions_to_rows(v):
                eng.wait_ge(mod_step, KT * (v + 1))
                for j in range(NC):
                    last = eng.matmul(side(j), ones, mod_acc[:, j * CW:(j + 1) * CW], start=True, stop=True)
                last.then_inc(mod_read, 1)

            def turn(dst, src):
                for b in range(4):
                    last = eng.transpose(dst[:, b * P:(b + 1) * P], src[:, b * P:(b + 1) * P], ident)
                return last

            def norm_turn():
                base = t.c["norm"]
                for i in range(TT * NC):
                    tt, j = divmod(i, NC)
                    eng.wait_ge(xn_ready, base + i + 1)
                    if i >= 4:
                        eng.wait_ge(n_low, base + i - 3)
                    turn(side(i % 4), xn[:, tt, j * CW:(j + 1) * CW]).then_inc(n_posed, 1)
                t.add("norm", TT * NC)

            def h_ready(hh):
                if hh % 2 == 0:
                    eng.wait_ge(n_low, t.c["norm"] - 3 + hh // 2)

            def mlp():
                with t.loop(eng, 0, QUARTERS, half=64, summed=NC, up=NC, t=2 * NC):
                    for c in range(NC):
                        if c < 2:
                            eng.wait_ge(summed, t.at("summed", c - 1))
                        else:
                            eng.wait_ge(up_taken, t.at("up", -1))
                        for hh in range(HALVES):
                            if c == 0:
                                h_ready(hh)
                            half(c, hh, h_high, h_low)
                            if c and hh in (1, 3):
                                turn_hidden(hh // 2)
                        t.add("up")
                    for c in range(NC):
                        if c < 2:
                            eng.wait_ge(up_taken, t.at("up", c - 1))
                        else:
                            eng.wait_ge(summed, t.at("summed", -1))
                        for hh in range(HALVES):
                            if c == 0 and hh % 2 == 0:
                                eng.wait_ge(t_low, t.at("t", -(2 * NC - 2) + hh) if hh < 6 else t.at("t", 0))
                            half(c, hh, u_high, u_low)
                            if c == 0 and hh in (1, 3):
                                turn_hidden(hh // 2)
                        t.add("summed")

            def turn_hidden(tt):
                if tt == 0:
                    eng.wait_ge(up_ready, t.at("up", 0))
                if (t.c["t"] - t_base[0]) % (2 * NC):
                    eng.wait_ge(t_low, t.at("t", 0))
                turn(side(0), hidden[:, tt, :]).then_inc(t_posed, 1)
                t.add("t")

            t_base = [0]

            eng.wait_ge(cst_in, 16)
            eng.wait_ge(vec_in, 16 * 7)
            eng.transpose(side(0)[:, 0:V_ALL], junk[0:V_ALL, 0:P], cst[0:V_ALL, C_ID:C_ID + V_ALL])\
               .then_inc(vec_turned, 1)
            sum_partitions_to_columns(0, 0)
            sum_partitions_to_columns(1, 1)
            eng.wait_ge(mod_cols, 2)
            eng.wait_ge(yn_ready, TT)
            eng.wait_ge(dft_in, 16)

            def over_sequence(g):
                if g >= 2:
                    eng.wait_ge(scaled, g - 1)
                for d in range(2):
                    k = 2 * g + d
                    for tt in range(TT):
                        last = eng.matmul(side(2 * (g % 2) + d), acc[:, tt, k * P:(k + 1) * P],
                                          tables[:, tt, 0:2 * SEQ], start=(tt == 0), stop=(tt == 1))
                last.then_inc(seq_done, 1)

            over_sequence(0)
            for g in range(FG):
                if g + 1 < FG:
                    over_sequence(g + 1)
                eng.wait_ge(scaled, g + 1)
                if g >= 2:
                    eng.wait_ge(dft_low, g - 1)
                for e in range(2):
                    dst = lin(g)[:, 0, e * SEQ:(e + 1) * SEQ]
                    for d in range(2):
                        eng.matmul(dst, tables[:, d, e * P:(e + 1) * P], seq_dft[:, g % 2, d, 0:SEQ],
                                   start=(d == 0), stop=False)
                        last = eng.matmul(dst, tables[:, d, 2 * SEQ + e * P:2 * SEQ + (e + 1) * P],
                                          seq_dft[:, g % 2, d, SEQ:2 * SEQ], start=False, stop=(d == 1))
                last.then_inc(dft_done, 1)
            sum_partitions_to_rows(2)
            eng.wait_ge(dft_low, FG)
            for c in range(NC):
                if c >= 2:
                    eng.wait_ge(summed, c - 1)
                for hh in range(HALVES):
                    half(c, hh, h_high, h_low)
                t.add("summed")
            eng.wait_ge(mod_cols, 3)
            sum_partitions_to_columns(3, 2)
            t.add("mod_cols")
            sum_partitions_to_columns(4, 3)
            eng.wait_ge(mod_cols, 5)
            norm_turn()
            mlp()
            sum_partitions_to_rows(5)
            norm_turn()

            def forget_logits():
                eng.wait_ge(f_low, 1)
                for tt in range(TT):
                    dst = side(3)[:, tt * HEADS:(tt + 1) * HEADS]
                    for k in range(KT):
                        ah = h_high[:, k, tt * P:(tt + 1) * P]
                        al = h_low[:, k, tt * P:(tt + 1) * P]
                        fh = wf_high[:, k * HEADS:(k + 1) * HEADS]
                        f_l = wf_low[:, k * HEADS:(k + 1) * HEADS]
                        eng.matmul(dst, ah, fh, start=(k == 0), stop=False)
                        eng.matmul(dst, ah, f_l, start=False, stop=False)
                        last = eng.matmul(dst, al, fh, start=False, stop=(k == KT - 1))
                last.then_inc(f_sum, 1)

            def forget_sums():
                eng.wait_ge(f_ready, 1)
                lf = [fl[:, tt * HEADS:(tt + 1) * HEADS] for tt in range(TT)]
                le, one = cst[:, C_LE:C_LE + P], ones
                eng.matmul(side(3)[0:HEADS, 0:SEQ], lf[0], cst[:, C_LE:C_LE + SEQ], start=True, stop=False)
                eng.matmul(side(3)[0:HEADS, P:SEQ], lf[1], le, start=False, stop=True)
                col = side(3)[:, SEQ:SEQ + 2 * HEADS]
                eng.matmul(col[:, 0:HEADS], le, lf[0], start=True, stop=True)
                eng.matmul(col[:, HEADS:2 * HEADS], one, lf[0], start=True, stop=False)
                eng.matmul(col[:, HEADS:2 * HEADS], le, lf[1], start=False, stop=True).then_inc(c_sum, 1)

            def scores(g, i):
                n = t.c["z"]
                q_h, k_h = qT[:, g % 2, i, :], kT[:, g % 2, i, :]
                eng.wait_ge(a_turned, 4 * (g + 1))
                if n:
                    eng.wait_ge(z_taken, n)
                bank = side(1)
                if g < 2:
                    eng.matmul(bank[:, 0:SEQ], k_h[:, 0:P], q_h, start=True, stop=True)
                    eng.matmul(bank[:, SEQ:384], k_h[:, P:SEQ], q_h[:, P:SEQ], start=True, stop=True)\
                       .then_inc(z_ready, 1)
                else:
                    if g == 2 and i == 0:
                        eng.wait_ge(c_ready, 1)
                        eng.wait_ge(sel_in, 16)
                    s_h = sel[:, GH * (g - 2) + i, :]
                    eng.matmul(bank[:, 0:P], q_h[:, 0:P], k_h[:, 0:P], start=True, stop=False)
                    eng.matmul(bank[:, 0:P], s_h, negc[:, 0:P], start=False, stop=True)
                    eng.matmul(bank[:, P:384], q_h[:, P:SEQ], k_h, start=True, stop=False)
                    eng.matmul(bank[:, P:384], s_h, negc[:, :], start=False, stop=True)\
                       .then_inc(z_ready, 1)
                t.add("z")

            def middle(g, i):
                n = t.c["mid"]
                e = ew[:, n % 2, :]
                if n:
                    eng.wait_ge(mid_taken, n) if g < 2 or n == 2 * GH else eng.wait_ge(probs_ready, n)
                bank = side(2)
                if g < 2:
                    eng.wait_ge(mid_in, n + 1)
                    eng.matmul(bank[:, 0:384], cst[:, C_GE:C_GE + P], e, start=True, stop=False)
                    eng.matmul(bank[:, P:SEQ], ones, e[:, SEQ:384], start=False, stop=True)\
                       .then_inc(mid_ready, 1)
                else:
                    eng.wait_ge(fox_exp, n + 1 - 2 * GH)
                    for b in range(3):
                        last = eng.transpose(bank[:, b * P:(b + 1) * P], e[:, b * P:(b + 1) * P], ident)
                    last.then_inc(mid_ready, 1)
                t.add("mid")

            def weigh_values(g, i):
                n = t.c["o"]
                a = probs[:, n % 2, :]
                v_h = [vv[:, g % 2, tt, i * HD:(i + 1) * HD] for tt in range(TT)]
                eng.wait_ge(probs_ready, n + 1)
                if n == 0 or i == 0:
                    eng.wait_ge(qkv_taken, 3 * (g + 1))
                if n:
                    eng.wait_ge(o_taken, n)
                else:
                    eng.wait_ge(c_ready, 1)
                eng.matmul(side(3)[:, 0:HD], a[:, 0:P], v_h[0], start=True, stop=True)
                eng.matmul(side(3)[:, HD:2 * HD], a[:, P:SEQ], v_h[0], start=True, stop=False)
                eng.matmul(side(3)[:, HD:2 * HD], a[:, SEQ:384], v_h[1], start=False, stop=True)\
                   .then_inc(o_ready, 1)
                t.add("o")

            def turn_mixed(g, tt):
                if tt == 0:
                    eng.wait_ge(mixed_ready, g + 1)
                    eng.wait_ge(a_turned, min(4 * (g + 2), 4 * GROUPS))
                else:
                    eng.wait_ge(m_scaled, 2 * g + 1)
                turn(side(0), normed[:, tt, :]).then_inc(m_posed, 1)

            def attention(g, jobs):
                for job, i in jobs:
                    {"z": scores, "mid": middle, "out": weigh_values, "turn": turn_mixed}[job](g, i)

            def turn_qk(n, tt):
                g, r = divmod(n, 3)
                done = 4 * g + 2 * r + tt
                if tt == 0:
                    eng.wait_ge(qkv_taken, n + 1)
                if done:
                    eng.wait_ge(a_turned, done)
                if r == 0 and tt == 0 and g >= 2:
                    eng.wait_ge(m_scaled, 2 * (g - 1))
                turn(side(0), stage[:, tt, :]).then_inc(a_posed, 1)

            for n in range(3 * GROUPS):
                if n < 2:
                    eng.wait_ge(summed, t.c["summed"] - 1 + n)
                else:
                    eng.wait_ge(qkv_taken, n - 1)
                g, r = divmod(n, 3)
                for hh in range(HALVES):
                    if n == 0:
                        h_ready(hh)
                    half(n, hh, h_high, h_low)
                    if hh in (1, 3) and n % 3:
                        turn_qk(n - 1, hh // 2)
                    if n == 0 and hh == 7:
                        forget_logits()
                    if n == 1 and hh == 5:
                        forget_sums()
                    if g:
                        attention(g - 1, SLOTS.get(r * HALVES + hh, ()))
            for y, (c, j) in enumerate([o for o in OUT_ORDER for _ in range(2)]):
                hh = 2 * j + y % 2
                if hh == 0:
                    if c < 2:
                        eng.wait_ge(qkv_taken, 3 * GROUPS - 1 + c)
                    else:
                        eng.wait_ge(summed, t.c["summed"] - 1)
                if y % 2 == 0 and (y < 6 or j == 3):
                    eng.wait_ge(m_low, 2 * (j + 1))
                half(c, hh, u_high, u_low)
                if hh == 7:
                    t.add("summed")
                attention(GROUPS - 1, LAST_SLOTS.get(y, ()))
            norm_turn()
            t_base[0] = t.c["t"]
            mlp()

        @block.scalar
        def _(eng):
            t = Tally()

            def link(ins):
                ins.then_inc(act_link, 1)
                t.add("link")
                eng.wait_ge(act_link, t.at("link", 0))

            def high_part():
                h = t.c["high"]
                slot = t.c["raw"] % RAW
                if h % 2 == 0:
                    eng.wait_ge(raw_loaded[slot], t.arrived())
                if h >= LEAD or t.q is not None:
                    eng.wait_ge(half_used, t.at("high", 1 - LEAD))
                eng.activation(w_high[:, h % LEAD, :], raw[:, slot, (h % 2) * 2 * CW:(h % 2 + 1) * 2 * CW],
                               ACT.Copy).then_inc(high_ready, 1)
                t.add("high")
                if h % 2:
                    t.add("raw")

            def square_sum(src, column):
                if t.c["squared"] or t.q is not None:
                    eng.wait_ge(squared, t.at("squared", 0))
                t.add("squared")
                eng.activation(junk[:, :], src, ACT.Square, accum_out=ssq[:, column:column + 1])\
                   .then_inc(squared, 1)

            def step_squares(target, c, done):
                eng.wait_ge(summed, done)
                for tt in range(TT):
                    square_sum(target[:, tt, c * CW:(c + 1) * CW], tt * NC + c)

            def root():
                t.add("root")
                eng.wait_ge(ms_ready, t.c["root"])
                eng.activation(sd[:, :], ms[:, :], ACT.Sqrt).then_inc(sd_ready, 1)

            def norm(scale, shift):
                base = t.c["norm"]
                root()
                eng.wait_ge(rstd_ready, t.c["root"])

                def scale_turned(i):
                    tt, j = divmod(i, NC)
                    eng.wait_ge(n_posed, base + i + 1)
                    if i >= 2:
                        eng.wait_ge(n_low, base + i - 1)
                    for b in range(4):
                        k = 4 * j + b
                        src, dst = side(i % 4)[:, b * P:(b + 1) * P], turned[:, i % 2, b * P:(b + 1) * P]
                        if shift is None:
                            last = eng.activation(dst, src, ACT.Copy, scale=scale[:, k:k + 1])
                        else:
                            last = eng.activation(dst, src, ACT.Identity, scale=scale[:, k:k + 1],
                                                  bias=shift[:, k:k + 1])
                    last.then_inc(n_scaled, 1)

                if shift is not None:
                    eng.wait_ge(mod_cols, 5)
                for i in range(TT * NC + 2):
                    if i < TT * NC:
                        tt, j = divmod(i, NC)
                        eng.activation(xn[:, tt, j * CW:(j + 1) * CW], xs[:, tt, j * CW:(j + 1) * CW],
                                       ACT.Copy, scale=rstd[:, tt:tt + 1]).then_inc(xn_ready, 1)
                    if i >= 2:
                        scale_turned(i - 2)
                t.add("norm", TT * NC)

            def residual_squares():
                for i in range(TT * NC):
                    tt, j = divmod(i, NC)
                    t.add("x_updated")
                    eng.wait_ge(x_updated, t.c["x_updated"])
                    square_sum(xs[:, tt, j * CW:(j + 1) * CW], i)

            def mlp_body(target, mods, ahead):
                for y in range(64):
                    if y < 60 or ahead:
                        high_part()
                        if t.c["high"] % 2 == 0 and (y // 2) in mods:
                            t.add("raw")
                    c, hh = divmod(y, HALVES)
                    if 1 <= c <= NC and hh in (1, 3):
                        tt = hh // 2
                        t.add("t")
                        eng.wait_ge(t_posed, t.at("t", 0))
                        eng.activation(u_high[:, 4 * (c - 1):4 * c, tt * P:(tt + 1) * P],
                                       side(0).rearrange("p (b n) -> p b n", b=4), ACT.Copy).then_inc(t_high, 1)
                    if hh == 7:
                        t.add("done", 8)
                        eng.wait_ge(half_used, t.at("done", 0))
                        if c < NC:
                            t.add("up")
                            eng.activation(relu, lin(c), ACT.Relu).then_inc(up_taken, 1)
                            eng.wait_ge(up_taken, t.at("up", 0))
                            eng.activation(hidden, relu, ACT.Square).then_inc(up_ready, 1)
                        else:
                            t.add("summed")
                            step_squares(target, c - NC, t.at("summed", 0))

            eng.dma_start(xs[:, :, :], x.rearrange("(t p) n -> p t n", p=P)).then_inc(x_in, 16)
            eng.dma_start(cst[:, :], consts).then_inc(cst_in, 16)
            for src, row, rows in ((c_in, V_C, KT), (norm_g[0:1, :], V_G0, KT), (norm_g[2:3, :], V_G2, KT),
                                   (g_attn, V_GA, KT), (g_mlp, V_GM, KT), (g_out_sb, V_GO, HEADS),
                                   (g_out_fox, V_GO + HEADS, HEADS)):
                eng.dma_start(junk[row:row + rows, 0:P], src.rearrange("o (r n) -> (o r) n", n=P))\
                   .then_inc(vec_in, 16)
            eng.dma_start(extra[:, :], dft.rearrange("(t p) n -> p t n", p=P)).then_inc(dft_in, 16)
            eng.wait_ge(vec_ready, 1)
            eng.activation(silu_t[:, 0:KT], cols[:, V_C:V_C + KT], ACT.Exp, scale=-1.0).then_inc(silu_exp, 1)
            eng.wait_ge(x_in, 16)
            for i in range(TT * NC):
                tt, j = divmod(i, NC)
                square_sum(xs[:, tt, j * CW:(j + 1) * CW], i)
            root()
            eng.wait_ge(rstd_ready, 1)
            for tt in range(TT):
                eng.activation(acc[:, tt, :], xs[:, tt, :], ACT.Copy, scale=rstd[:, tt:tt + 1])\
                   .then_inc(yn_ready, 1)
            eng.wait_ge(mod_cols, 2)

            def scale_and_shift(g):
                eng.wait_ge(seq_done, g + 1)
                if g >= 2:
                    eng.wait_ge(dft_done, g - 1)
                for d in range(2):
                    k = 2 * g + d
                    ins = eng.activation(seq_dft[:, g % 2, d, :], side(2 * (g % 2) + d), ACT.Copy,
                                         scale=scale1[:, k:k + 1])
                link(ins)
                for d in range(2):
                    k = 2 * g + d
                    at0 = seq_dft[:, g % 2, d, 0:1]
                    last = eng.activation(at0, at0, ACT.Identity, bias=shift1[:, k:k + 1])
                last.then_inc(scaled, 1)

            scale_and_shift(0)
            for g in range(FG):
                if g + 1 < FG:
                    scale_and_shift(g + 1)
                eng.wait_ge(dft_done, g + 1)
                eng.activation(h_high[:, 2 * g:2 * g + 2, :],
                               lin(g)[:, 0, :].rearrange("p (e s) -> p e s", e=2), ACT.Copy).then_inc(dft_high, 1)
            t.add("raw", 3 * KT)

            def fnet_high():
                high_part()
                if t.c["high"] % 2 == 0:
                    t.add("raw")

            for _ in range(LEAD):
                fnet_high()
            for y in range(NC * HALVES):
                if y < NC * HALVES - LEAD:
                    fnet_high()
                if y % HALVES == 7:
                    t.add("done", 8)
                    t.add("summed")
                    step_squares(acc, y // HALVES, t.c["summed"])
            root()
            t.add("raw", KT)
            for _ in range(LEAD):
                high_part()
            residual_squares()
            norm(scale2, mcol[:, 2 * KT:3 * KT])
            with t.loop(eng, 0, QUARTERS, high=64, raw=36, t=2 * NC, done=64, up=NC, summed=NC,
                        squared=TT * NC):
                mlp_body(acc, MOD_AFTER, True)
            root()
            residual_squares()
            norm(cols[:, V_GA:V_GA + KT], None)

            def take_qkv(n):
                g, r = divmod(n, 3)
                t.add("done", 8)
                eng.wait_ge(half_used, t.c["done"])
                if r < 2:
                    if n:
                        eng.wait_ge(a_posed, 4 * g + 2 * r)
                    eng.activation(stage, lin(n), ACT.Copy, scale=(float(HD) ** -0.5 if r == 0 else 1.0))\
                       .then_inc(qkv_taken, 1)
                else:
                    if g >= 2:
                        eng.wait_ge(o_ready, GH * (g - 1))
                    eng.activation(vv[:, g % 2, :, :], lin(n), ACT.Copy).then_inc(qkv_taken, 1)

            def forget_high():
                eng.wait_ge(f_raw, 48)
                eng.activation(wf_high[:, :], wf[:, :], ACT.Copy).then_inc(f_high, 1)

            def forget_gate():
                eng.wait_ge(f_logit, 1)
                link(eng.activation(fe[:, :], fl[:, :], ACT.Abs))
                link(eng.activation(fe[:, :], fe[:, :], ACT.Exp, scale=-1.0))
                eng.activation(fe[:, :], fe[:, :], ACT.Ln, bias=1.0).then_inc(f_exp, 1)

            def score_logs(g, i):
                n = t.c["z"]
                t.add("z")
                z, e = zs[:, n % 2, :], ew[:, n % 2, :]
                eng.wait_ge(z_taken, n + 1)
                if g < 2:
                    link(eng.activation(e, z, ACT.Abs))
                    link(eng.activation(e, e, ACT.Exp, scale=-1.0))
                    eng.activation(e, e, ACT.Ln, bias=1.0).then_inc(z_logs, 1)
                else:
                    eng.wait_ge(mid_in, n + 1)
                    for tt, (a, b) in enumerate(((0, P), (P, 384))):
                        last = eng.activation(e[:, a:b], z[:, a:b], ACT.Exp,
                                              bias=negmax[:, tt * GH + i:tt * GH + i + 1],
                                              accum_out=psums[:, tt * GH + i:tt * GH + i + 1])
                    last.then_inc(fox_exp, 1)

            def take_middle(g, i):
                n = t.c["mid"]
                t.add("mid")
                if n >= 2:
                    eng.wait_ge(o_ready, n - 1)
                if g < 2:
                    eng.wait_ge(mid_taken, n + 1)
                    eng.activation(probs[:, n % 2, :], ew[:, n % 2, :], ACT.Exp).then_inc(probs_ready, 1)
                else:
                    eng.wait_ge(mid_ready, n + 1)
                    eng.activation(probs[:, n % 2, :], side(2)[:, 0:384], ACT.Copy).then_inc(probs_ready, 1)

            def head_root(g, i):
                if i == 3:
                    eng.wait_ge(hms_ready, g + 1)
                    eng.activation(hsd[:, :], hms[:, :], ACT.Sqrt).then_inc(hsd_ready, 1)

            def take_mixed(g, tt):
                eng.wait_ge(m_posed, 2 * g + tt + 1)
                if 2 * g + tt:
                    eng.wait_ge(m_low, 2 * g + tt)
                for b in range(4):
                    k = V_GO + 4 * g + b
                    last = eng.activation(fin[:, b * P:(b + 1) * P], side(0)[:, b * P:(b + 1) * P],
                                          ACT.Copy, scale=cols[:, k:k + 1])
                last.then_inc(m_scaled, 1)

            def attention(g, jobs):
                for job, i in jobs:
                    {"z": score_logs, "mid": take_middle, "out": head_root, "turn": take_mixed}[job](g, i)

            forget_high()
            for n in range(3 * GROUPS):
                g, r = divmod(n, 3)
                for hh in range(HALVES):
                    high_part()
                    if hh == 7:
                        take_qkv(n)
                    if n == 0 and hh == 7:
                        forget_gate()
                    if g:
                        attention(g - 1, SLOTS.get(r * HALVES + hh, ()))
            for y, (c, j) in enumerate([o for o in OUT_ORDER for _ in range(2)]):
                high_part()
                if j == 3 and y % 2:
                    t.add("summed")
                    step_squares(xs, c, t.c["summed"])
                attention(GROUPS - 1, LAST_SLOTS.get(y, ()))
            t.add("done", 8 * NC)
            norm(cols[:, V_GM:V_GM + KT], None)
            with t.loop(eng, 0, QUARTERS - 1, high=64, raw=32, t=2 * NC, done=64, up=NC, summed=NC,
                        squared=TT * NC):
                mlp_body(xs, (), True)
            mlp_body(xs, (), False)
            root()
            eng.wait_ge(rstd_ready, t.c["root"])
            for i in range(TT * NC):
                tt, j = divmod(i, NC)
                eng.activation(acc[:, tt, j * CW:(j + 1) * CW], xs[:, tt, j * CW:(j + 1) * CW], ACT.Copy,
                               scale=rstd[:, tt:tt + 1]).then_inc(final_scaled, 1)

        @block.vector
        def _(eng):
            t = Tally()

            def link(ins):
                ins.then_inc(vec_link, 1)
                t.add("link")
                eng.wait_ge(vec_link, t.at("link", 0))

            def low_part():
                h = t.c["low"]
                slot = t.c["raw"] % RAW
                piece = slice((h % 2) * 2 * CW, (h % 2 + 1) * 2 * CW)
                eng.wait_ge(high_ready, t.at("low", 1))
                ins = eng.tensor_tensor(w_low[:, h % LEAD, :], raw[:, slot, piece],
                                        w_high[:, h % LEAD, :].bitcast(f32), ALU.subtract)
                ins.then_inc(low_ready, 1)
                t.add("low")
                if h % 2:
                    free_raw()

            def free_raw():
                eng.wait_ge(low_ready, t.at("low", 0))
                eng.sem_inc(raw_used, 1)
                t.add("raw")

            def mod_tile(kk):
                slot = t.c["raw"] % RAW
                eng.wait_ge(raw_loaded[slot], t.arrived())
                if t.c["mod"] or t.q is not None:
                    eng.wait_ge(mod_step, t.at("mod", 0))
                eng.scalar_tensor_tensor(out=mod_acc, in0=raw[:, slot, :], scalar=silu_c[:, bass.ds(kk, 1)],
                                         in1=mod_acc, op0=ALU.mult, op1=ALU.add).then_inc(mod_step, 1)
                t.add("mod")
                eng.wait_ge(mod_step, t.at("mod", 0))
                eng.sem_inc(raw_used, 1)
                t.add("raw")

            def mod_columns(v, place):
                eng.wait_ge(mod_read, v + 1)
                col = mcol[:, place * KT:(place + 1) * KT]
                src = side(3)[:, place * KT:(place + 1) * KT]
                if place == 0:
                    link(eng.tensor_copy(col, src))
                    eng.tensor_scalar(shift1[:, :], col, float(SEQ), None, ALU.mult).then_inc(mod_cols, 1)
                elif place == 2:
                    eng.tensor_copy(col, src).then_inc(mod_cols, 1)
                else:
                    dst, gain = (scale1, V_G0) if place == 1 else (scale2, V_G2)
                    eng.scalar_tensor_tensor(out=dst[:, :], in0=src, scalar=1.0, in1=cols[:, gain:gain + KT],
                                             op0=ALU.add, op1=ALU.mult).then_inc(mod_cols, 1)

            def mod_rows(v, loads):
                eng.wait_ge(mod_read, v + 1)
                eng.wait_ge(grow_in, 16 * loads)
                for j in range(NC):
                    piece = grow[:, j * CW:(j + 1) * CW]
                    ins = eng.tensor_tensor(piece, side(j), piece, ALU.mult)
                return ins

            def inverse_root():
                t.add("root")
                eng.wait_ge(squared, t.c["squared"])
                link(eng.tensor_reduce(ms[:, :], ssq[:, :].rearrange("p (t c) -> p t c", t=TT), AX.X, ALU.add))
                eng.tensor_scalar(ms[:, :], ms[:, :], 1.0 / D, EPS, ALU.mult, ALU.add).then_inc(ms_ready, 1)
                eng.wait_ge(sd_ready, t.c["root"])
                eng.reciprocal(rstd[:, :], sd[:, :]).then_inc(rstd_ready, 1)
                eng.wait_ge(rstd_ready, t.c["root"])

            def gate(i):
                tt, j = divmod(i, NC)
                a = acc[:, tt, j * CW:(j + 1) * CW]
                eng.scalar_tensor_tensor(out=a, in0=a, scalar=rstd[:, tt:tt + 1], in1=grow[:, j * CW:(j + 1) * CW],
                                         op0=ALU.mult, op1=ALU.mult).then_inc(gated, 1)
                t.add("gated")

            def update(i):
                tt, j = divmod(i, NC)
                piece = xs[:, tt, j * CW:(j + 1) * CW]
                t.add("updated")
                eng.wait_ge(gated, t.c["updated"])
                eng.tensor_tensor(piece, piece, acc[:, tt, j * CW:(j + 1) * CW], ALU.add).then_inc(x_updated, 1)

            def residual():
                for i in range(TT * NC + 1):
                    if i < TT * NC:
                        gate(i)
                    if i:
                        update(i - 1)

            def norm():
                t.add("squared", TT * NC)
                inverse_root()
                for i in range(TT * NC):
                    tt, j = divmod(i, NC)
                    t.add("norm")
                    src = turned[:, i % 2, :].rearrange("p (b n) -> p b n", b=4)
                    high = h_high[:, 4 * j:4 * j + 4, tt * P:(tt + 1) * P]
                    eng.wait_ge(n_scaled, t.c["norm"])
                    eng.tensor_copy(high, src).then_inc(n_high, 1)
                    eng.wait_ge(n_high, t.c["norm"])
                    eng.tensor_tensor(h_low[:, 4 * j:4 * j + 4, tt * P:(tt + 1) * P], src, high.bitcast(f32),
                                      ALU.subtract).then_inc(n_low, 1)

            def add_step(target, n, c):
                eng.wait_ge(half_used, t.at("done", 0))
                piece = target[:, :, c * CW:(c + 1) * CW]
                eng.tensor_tensor(piece, lin(n), piece, ALU.add).then_inc(summed, 1)
                t.add("squared", TT)

            def mlp_body(target, mods, q, ahead):
                for y in range(64):
                    if y < 60 or ahead:
                        low_part()
                        if t.c["low"] % 2 == 0 and (y // 2) in mods:
                            mod_tile(q * 4 + mods.index(y // 2))
                    c, hh = divmod(y, HALVES)
                    if 1 <= c <= NC and hh in (1, 3):
                        tt = hh // 2
                        t.add("t")
                        eng.wait_ge(t_high, t.at("t", 0))
                        high = u_high[:, 4 * (c - 1):4 * c, tt * P:(tt + 1) * P]
                        eng.tensor_tensor(u_low[:, 4 * (c - 1):4 * c, tt * P:(tt + 1) * P],
                                          side(0).rearrange("p (b n) -> p b n", b=4), high.bitcast(f32),
                                          ALU.subtract).then_inc(t_low, 1)
                    if hh == 7:
                        t.add("done", 8)
                        if c >= NC:
                            add_step(target, c, c - NC)

            eng.wait_ge(vec_turned, 1)
            eng.tensor_copy(cols[:, :], side(0)[:, 0:V_ALL]).then_inc(vec_ready, 1)
            eng.wait_ge(silu_exp, 1)
            eng.wait_ge(vec_ready, 1)
            link(eng.tensor_scalar(silu_t[:, KT:2 * KT], silu_t[:, 0:KT], 1.0, None, ALU.add))
            link(eng.reciprocal(silu_t[:, 0:KT], silu_t[:, KT:2 * KT]))
            link(eng.tensor_tensor(silu_c[:, :], silu_t[:, 0:KT], cols[:, V_C:V_C + KT], ALU.mult))
            t.add("squared", TT * NC)
            inverse_root()
            for unit in range(2):
                eng.wait_ge(acc_init, 16 * (unit + 1))
                mod_tile(0) if unit == 0 else None
                if unit == 0:
                    for i in range(1, RAW):
                        mod_tile(i)
                with t.loop(eng, 1 if unit == 0 else 0, KT // RAW, raw=RAW, mod=RAW) as q:
                    for i in range(RAW):
                        mod_tile(q * RAW + i)
                mod_columns(unit, unit)
            eng.wait_ge(acc_init, 16 * 3)
            for g in range(FG):
                mod_tile(2 * g)
                mod_tile(2 * g + 1)
                eng.wait_ge(dft_high, g + 1)
                eng.tensor_tensor(h_low[:, 2 * g:2 * g + 2, :], lin(g)[:, 0, :].rearrange("p (e s) -> p e s", e=2),
                                  h_high[:, 2 * g:2 * g + 2, :].bitcast(f32), ALU.subtract).then_inc(dft_low, 1)
            mod_rows(2, 1).then_inc(mod_cols, 1)
            def fnet_low():
                low_part()
                if t.c["low"] % 2 == 0:
                    if t.c["low"] == 2:
                        eng.wait_ge(acc_init, 16 * 4)
                    mod_tile(t.c["low"] // 2 - 1)

            for _ in range(LEAD):
                fnet_low()
            eng.wait_ge(acc_zero, 1)
            for y in range(NC * HALVES):
                if y < NC * HALVES - LEAD:
                    fnet_low()
                if y % HALVES == 7:
                    t.add("done", 8)
                    add_step(acc, y // HALVES, y // HALVES)
            inverse_root()
            mod_columns(3, 2)
            eng.wait_ge(acc_init, 16 * 5)
            for i in range(KT):
                mod_tile(i)
                if i % 2 == 0:
                    gate(i // 2)
                else:
                    update(i // 2)
            mod_columns(4, 3)
            for _ in range(LEAD):
                low_part()
            norm()
            eng.wait_ge(acc_init, 16 * 6)
            eng.wait_ge(acc_zero, 2)
            with t.loop(eng, 0, QUARTERS, low=64, raw=36, mod=4, t=2 * NC, done=64, squared=TT * NC) as q:
                mlp_body(acc, MOD_AFTER, q, True)
            t.c["squared"] -= TT * NC
            t.add("squared", TT * NC)
            inverse_root()
            link(mod_rows(5, 2))
            residual()
            norm()

            def forget_low():
                eng.wait_ge(f_high, 1)
                eng.tensor_tensor(wf_low[:, :], wf[:, :], wf_high[:, :].bitcast(f32), ALU.subtract)\
                   .then_inc(f_low, 1)

            def forget_logit():
                eng.wait_ge(f_sum, 1)
                eng.tensor_tensor(fl[:, :], side(3)[:, 0:TT * HEADS], bf[:, :], ALU.add).then_inc(f_logit, 1)

            def forget_gate():
                eng.wait_ge(f_exp, 1)
                eng.scalar_tensor_tensor(out=fl[:, :], in0=fl[:, :], scalar=0.0, in1=fe[:, :],
                                         op0=ALU.min, op1=ALU.subtract).then_inc(f_ready, 1)

            def forget_sums():
                eng.wait_ge(c_sum, 1)
                eng.tensor_scalar(negc[:, :], side(3)[0:HEADS, 0:SEQ], -1.0, None, ALU.mult)
                eng.tensor_copy(csum[:, :], side(3)[:, SEQ:SEQ + TT * HEADS]).then_inc(c_ready, 1)

            def turned_qk(n, tt):
                g, r = divmod(n, 3)
                t.add("a")
                eng.wait_ge(a_posed, t.c["a"])
                dst = (qT, kT)[r][:, g % 2, :, tt * P:(tt + 1) * P]
                eng.tensor_copy(dst, side(0).rearrange("p (h n) -> p h n", h=GH)).then_inc(a_turned, 1)

            def mask_scores(g, i):
                n = t.c["z"]
                t.add("z")
                z = zs[:, n % 2, :]
                eng.wait_ge(z_ready, n + 1)
                if g < 2:
                    eng.tensor_tensor(z, side(1)[:, 0:384], cst[:, C_SB:C_SB + 384], ALU.add).then_inc(z_taken, 1)
                    return
                head = GH * (g - 2) + i
                for tt, (a, b) in enumerate(((0, P), (P, 384))):
                    last = eng.scalar_tensor_tensor(
                        out=z[:, a:b], in0=side(1)[:, a:b], scalar=csum[:, tt * HEADS + head:tt * HEADS + head + 1],
                        in1=cst[:, C_FOX + a:C_FOX + b], op0=ALU.add, op1=ALU.add)
                last.then_inc(z_taken, 1)
                eng.wait_ge(z_taken, n + 1)
                for tt, (a, b) in enumerate(((0, P), (P, 384))):
                    last = eng.tensor_reduce(negmax[:, tt * GH + i:tt * GH + i + 1], z[:, a:b], AX.X, ALU.max,
                                             negate=True)
                last.then_inc(mid_in, 1)

            def keep_logs(g, i):
                n = t.c["z"] - 1
                if g < 2:
                    e = ew[:, n % 2, :]
                    eng.wait_ge(z_logs, n + 1)
                    eng.scalar_tensor_tensor(out=e, in0=zs[:, n % 2, :], scalar=0.0, in1=e, op0=ALU.max,
                                             op1=ALU.add).then_inc(mid_in, 1)

            def take_middle(g, i):
                n = t.c["mid"]
                t.add("mid")
                eng.wait_ge(mid_ready, n + 1)
                if g < 2:
                    eng.tensor_tensor(ew[:, n % 2, :], zs[:, n % 2, :], side(2)[:, 0:384], ALU.subtract)\
                       .then_inc(mid_taken, 1)

            def take_out(g, i):
                n = t.c["o"]
                t.add("o")
                eng.wait_ge(o_ready, n + 1)
                if g < 2:
                    eng.tensor_copy(heads[:, :, i * HD:(i + 1) * HD],
                                    side(3)[:, 0:TT * HD].rearrange("p (t n) -> p t n", t=TT)).then_inc(o_taken, 1)
                else:
                    for tt in range(TT):
                        s = slice(tt * GH + i, tt * GH + i + 1)
                        ins = eng.reciprocal(precip[:, s], psums[:, s])
                    link(ins)
                    for tt in range(TT):
                        last = eng.tensor_scalar(heads[:, tt, i * HD:(i + 1) * HD], side(3)[:, tt * HD:(tt + 1) * HD],
                                                 precip[:, tt * GH + i:tt * GH + i + 1], None, ALU.mult)
                    last.then_inc(o_taken, 1)
                if i == GH - 1:
                    eng.wait_ge(o_taken, n + 1)
                    if g:
                        eng.wait_ge(m_posed, 2 * g)
                    flat = normed.rearrange("p t (h n) -> p (t h) n", n=HD)
                    src = heads.rearrange("p t (h n) -> p (t h) n", n=HD)
                    link(eng.tensor_tensor(flat, src, src, ALU.mult))
                    link(eng.tensor_reduce(hms[:, :], flat, AX.X, ALU.add))
                    eng.tensor_scalar(hms[:, :], hms[:, :], 1.0 / HD, EPS, ALU.mult, ALU.add).then_inc(hms_ready, 1)
                    eng.wait_ge(hsd_ready, g + 1)
                    link(eng.reciprocal(hrs[:, :], hsd[:, :]))
                    eng.tensor_tensor(flat, src, hrs[:, :].unsqueeze(2).to_broadcast([P, TT * GH, HD]), ALU.mult)\
                       .then_inc(mixed_ready, 1)

            def take_mixed(g, tt):
                src = fin[:, :].rearrange("p (b n) -> p b n", b=4)
                high = u_high[:, 4 * g:4 * g + 4, tt * P:(tt + 1) * P]
                eng.wait_ge(m_scaled, 2 * g + tt + 1)
                eng.tensor_copy(high, src).then_inc(m_high, 1)
                eng.wait_ge(m_high, 2 * g + tt + 1)
                eng.tensor_tensor(u_low[:, 4 * g:4 * g + 4, tt * P:(tt + 1) * P], src, high.bitcast(f32),
                                  ALU.subtract).then_inc(m_low, 1)

            def attention(g, jobs):
                for job, i in jobs:
                    {"z": mask_scores, "mid": take_middle, "out": take_out, "turn": take_mixed}[job](g, i)
                for job, i in jobs:
                    if job == "z":
                        keep_logs(g, i)

            forget_low()
            for n in range(3 * GROUPS):
                g, r = divmod(n, 3)
                for hh in range(HALVES):
                    low_part()
                    if hh in (1, 3) and n % 3:
                        turned_qk(n - 1, hh // 2)
                    if n == 0 and hh == 7:
                        forget_logit()
                        forget_gate()
                    if n == 1 and hh == 5:
                        forget_sums()
                    if g:
                        attention(g - 1, SLOTS.get(r * HALVES + hh, ()))
            t.add("done", 8 * 3 * GROUPS)
            done = t.c["done"]
            for y, (c, j) in enumerate([o for o in OUT_ORDER for _ in range(2)]):
                low_part()
                if j == 3 and y % 2:
                    t.c["done"] = done + y + 1
                    add_step(xs, c, c)
                attention(GROUPS - 1, LAST_SLOTS.get(y, ()))
            t.c["squared"] -= TT * NC
            norm()
            with t.loop(eng, 0, QUARTERS - 1, low=64, raw=32, t=2 * NC, done=64, squared=TT * NC) as q:
                mlp_body(xs, (), q, True)
            mlp_body(xs, (), QUARTERS - 1, False)
            inverse_root()
            eng.wait_ge(grow_in, 48)
            for i in range(TT * NC):
                tt, j = divmod(i, NC)
                piece = acc[:, tt, j * CW:(j + 1) * CW]
                eng.wait_ge(final_scaled, i + 1)
                eng.tensor_tensor(piece, piece, grow[:, j * CW:(j + 1) * CW], ALU.mult).then_inc(final_ready, 1)


def shape_constants():
    i, j = np.arange(P)[:, None], np.arange(P)[None, :]
    f = np.float32
    tri = lambda ok: np.where(ok, f(0), f(MASKED))
    zero = np.zeros((P, P), f)
    later, upto = tri(i < j), tri(j <= i)
    consts = np.concatenate([np.eye(P, dtype=f), (i >= j).astype(f), (i <= j).astype(f), np.ones((P, P), f),
                             later, zero, later, upto, zero, upto], axis=1)
    n = np.arange(SEQ)
    angle = 2.0 * np.pi * ((n[:, None] * n[None, :]) % SEQ) / SEQ
    cos, sin = np.cos(angle), np.sin(angle)
    dft = np.concatenate([cos, sin, -sin], axis=1).astype(f)
    select = np.repeat(np.eye(HEADS, dtype=f)[:, :, None], P, axis=2)
    return consts.astype(f), dft, select


def kernel(x, c, ctx, c_ctx, w_mod, b_mod, norm_g, w_mlp_in, w_mlp_out, fnet_w_out, hgrn_w_in, hgrn_lb,
           hgrn_gnorm, hgrn_w_out, diff_w_qkv, diff_lambda, diff_subln, diff_w_out, g_attn_2, w_in_2,
           b_f_2, g_out_sb_2, g_out_fox_2, w_out_2, g_mlp_2, w_up_2, w_down_2, g_final_2):
    import concourse.bacc as bacc
    from concourse.bass_utils import run_bass_kernel_spmd

    consts, dft, select = shape_constants()
    two_d = lambda a: np.ascontiguousarray(np.asarray(a)).reshape(-1, np.asarray(a).shape[-1])
    given = [("x", two_d(x)), ("c", two_d(c)), ("w_mod", two_d(w_mod)), ("b_mod", two_d(b_mod)),
             ("norm_g", two_d(norm_g)), ("w_mlp_in", two_d(w_mlp_in)), ("w_mlp_out", two_d(w_mlp_out)),
             ("fnet_w", two_d(fnet_w_out)), ("g_attn", two_d(g_attn_2)), ("w_in", two_d(w_in_2)),
             ("b_f", two_d(b_f_2)), ("g_out_sb", two_d(g_out_sb_2)), ("g_out_fox", two_d(g_out_fox_2)),
             ("w_out", two_d(w_out_2)), ("g_mlp", two_d(g_mlp_2)), ("w_up", two_d(w_up_2)),
             ("w_down", two_d(w_down_2)), ("g_final", two_d(g_final_2)), ("consts", consts), ("dft", dft),
             ("select", select)]
    nc = bacc.Bacc("TRN2", target_bir_lowering=False, num_devices=1)
    arrays, args = {}, []
    for name, a in given:
        arrays[f"in_{name}"] = a
        args.append(nc.dram_tensor(f"in_{name}", a.shape, mybir.dt.from_np(a.dtype), kind="ExternalInput").ap())
    args.append(nc.dram_tensor("out_x", (SEQ, D), mybir.dt.float32, kind="ExternalOutput").ap())
    program(nc, *args)
    r = run_bass_kernel_spmd(nc, [arrays], core_ids=[0])
    return r.results[0]["out_x"].reshape(1, SEQ, D)
```

```python
from collections import defaultdict
from contextlib import ExitStack, contextmanager

import numpy as np

import concourse.bass as bass
from concourse import mybir

P = 128
SEQ = 256
D = 2048
TT = SEQ // P
KT = D // P
CW = 512
NC = D // CW
HALVES = KT // 2
LEAD = 4
RAW = 4
QUARTERS = 4
HD = 128
HEADS = 8
GH = 4
GROUPS = 4
EPS = 1e-6
GROUP_DIM = 256
FG = D // GROUP_DIM
MASKED = -1e30

C_ID, C_GE, C_LE, C_ONE, C_SB, C_FOX = 0, 128, 256, 384, 512, 896
C_ALL = 1280

V_C, V_G0, V_G2, V_GA, V_GM, V_GO = (KT * i for i in range(6))
V_ALL = 6 * KT

MOD_AFTER = (2, 5, 8, 11, 14, 18, 22, 26)
MOD_LOOPS = KT // len(MOD_AFTER)
TURN_BANKS = (0, 1, 4, 5, 6, 7, 2, 3)

SLOTS = {5: (("z", 0),), 7: (("z", 1), ("mid", 0)), 10: (("z", 2), ("mid", 1), ("out", 0)),
         13: (("z", 3), ("mid", 2), ("out", 1)), 15: (("mid", 3), ("out", 2)), 18: (("out", 3),),
         21: (("turn", 0),), 23: (("turn", 1),)}
LAST_SLOTS = {0: (("z", 0),), 2: (("z", 1), ("mid", 0)), 4: (("z", 2), ("mid", 1), ("out", 0)),
              6: (("z", 3), ("mid", 2), ("out", 1)), 8: (("mid", 3), ("out", 2)), 9: (("out", 3),),
              11: (("turn", 0), ("turn", 1))}
OUT_ORDER = [(0, 0), (0, 1), (0, 2), (1, 0), (1, 1), (1, 2), (0, 3), (1, 3)] + \
            [(c, j) for c in (2, 3) for j in range(4)]


class Tally:

    def __init__(self):
        self.c = defaultdict(int)
        self.q, self.start, self.per = None, 0, {}

    def at(self, name, d=0):
        v = self.c[name] + d
        per = self.per.get(name, 0)
        return v if self.q is None or per == 0 else self.q * per + (v - self.start * per)

    def add(self, name, k=1):
        self.c[name] += k

    def arrived(self):
        v = 16 * (self.c["raw"] // RAW + 1)
        per = 16 * (self.per.get("raw", 0) // RAW)
        return v if self.q is None or per == 0 else self.q * per + (v - self.start * per)

    @contextmanager
    def loop(self, eng, start, stop, **per):
        before = dict(self.c)
        with eng.Fori(start, stop) as q:
            self.q, self.start, self.per = q, start, per
            yield q
        self.q, self.start, self.per = None, 0, {}
        for name in set(self.c) | set(per):
            one = self.c[name] - before.get(name, 0)
            assert one == per.get(name, 0), (name, one)
            self.c[name] = before.get(name, 0) + one * (stop - start)


def in_column(g, r):
    kind, part = divmod(g, 2)
    return kind * 3 * HEADS * HD + r * HEADS * HD + part * CW


def program(nc, x, c_in, w_mod, b_mod, norm_g, w_mlp_in, w_mlp_out, fnet_w, g_attn, w_in, b_f,
            g_out_sb, g_out_fox, w_out, g_mlp, w_up, w_down, g_final, consts, dft, select, out):
    dt = mybir.dt
    f32, f32r = dt.float32, dt.float32r
    ACT = mybir.ActivationFunctionType
    ALU = mybir.AluOpType
    AX = mybir.AxisListType

    ctx = ExitStack()
    with ctx:
        def sb(name, shape, dtype=f32):
            return ctx.enter_context(nc.sbuf_tensor(name, shape, dtype))

        def sem(name):
            return ctx.enter_context(nc.semaphore(name))

        raw = sb("raw", [P, RAW, 4 * CW])
        w_high = sb("w_high", [P, LEAD, 2 * CW], f32r)
        w_low = sb("w_low", [P, LEAD, 2 * CW], f32r)
        h_high = sb("h_high", [P, KT, SEQ], f32r)
        h_low = sb("h_low", [P, KT, SEQ], f32r)
        u_high = sb("u_high", [P, KT, SEQ], f32r)
        u_low = sb("u_low", [P, KT, SEQ], f32r)
        xs = sb("xs", [P, TT, D])
        acc = sb("acc", [P, TT, D])
        grow = sb("grow", [P, D])
        scr = sb("scr", [P, 2 * D])
        extra = sb("extra", [P, 1536])
        junk = sb("junk", [P, CW])
        probs = sb("probs", [P, 2, 384])
        fin = sb("fin", [P, CW])
        cst = sb("cst", [P, C_ALL])
        cols = sb("cols", [P, V_ALL])
        silu_t = sb("silu_t", [P, 2 * KT])
        silu_c = sb("silu_c", [P, KT])
        mcol = sb("mcol", [P, 4 * KT])
        scale1 = sb("scale1", [P, KT])
        scale2 = sb("scale2", [P, KT])
        shift1 = sb("shift1", [P, KT])
        ssq = sb("ssq", [P, TT * NC])
        ms = sb("ms", [P, TT])
        sd = sb("sd", [P, TT])
        rstd = sb("rstd", [P, TT])
        wf = sb("wf", [P, KT * HEADS])
        wf_high = sb("wf_high", [P, KT * HEADS], f32r)
        wf_low = sb("wf_low", [P, KT * HEADS], f32r)
        bf = sb("bf", [P, TT * HEADS])
        fl = sb("fl", [P, TT * HEADS])
        fe = sb("fe", [P, TT * HEADS])
        csum = sb("csum", [P, TT * HEADS])
        negmax = sb("negmax", [P, TT * GH])
        psums = sb("psums", [P, TT * GH])
        precip = sb("precip", [P, TT * GH])
        hms = sb("hms", [P, TT * GH])
        hsd = sb("hsd", [P, TT * GH])
        hrs = sb("hrs", [P, TT * GH])
        ps = ctx.enter_context(nc.psum_tensor("ps", [P, 8, CW], f32))

        def lin(n):
            return ps[:, 2 * (n % 2):2 * (n % 2) + 2, :]

        def side(b):
            return ps[:, 4 + b, :]

        ident = cst[:, C_ID:C_ID + P]
        ones = cst[:, C_ONE:C_ONE + P]

        def mod_acc(v):
            return scr[:, 0:D] if v in (1, 3) else scr[:, D:2 * D]

        relu = scr[:, 0:TT * CW].rearrange("p (t n) -> p t n", t=TT)
        hidden = scr[:, TT * CW:2 * TT * CW].rearrange("p (t n) -> p t n", t=TT)
        seq_dft = scr[:, 0:D].rearrange("p (b d n) -> p b d n", b=2, d=2)
        tables = extra[:, :].rearrange("p (t n) -> p t n", t=2)
        turned = extra[:, 0:2 * CW].rearrange("p (b n) -> p b n", b=2)
        qT = acc[:, 0, :].rearrange("p (b h s) -> p b h s", b=2, h=GH)
        kT = acc[:, 1, :].rearrange("p (b h s) -> p b h s", b=2, h=GH)
        vv = grow[:, :].rearrange("p (b t n) -> p b t n", b=2, t=TT)
        stage = scr[:, 0:TT * CW].rearrange("p (t n) -> p t n", t=TT)
        heads = scr[:, TT * CW:2 * TT * CW].rearrange("p (t n) -> p t n", t=TT)
        normed = scr[:, 2 * TT * CW:3 * TT * CW].rearrange("p (t n) -> p t n", t=TT)
        sel = scr[0:HEADS, 3 * TT * CW:4 * TT * CW].rearrange("p (h n) -> p h n", h=HEADS)
        zs = extra[:, 0:768].rearrange("p (b n) -> p b n", b=2)
        ew = extra[:, 768:1536].rearrange("p (b n) -> p b n", b=2)
        negc = sb("negc", [HEADS, SEQ])

        raw_loaded = [sem(f"raw_loaded{i}") for i in range(RAW)]
        raw_used = sem("raw_used")
        high_ready = sem("high_ready")
        low_first = sem("low_first")
        half_used = sem("half_used")
        x_in, cst_in, dft_in, vec_in = sem("x_in"), sem("cst_in"), sem("dft_in"), sem("vec_in")
        grow_in, gate_in, sel_in = sem("grow_in"), sem("gate_in"), sem("sel_in")
        vec_turned, vec_ready = sem("vec_turned"), sem("vec_ready")
        act_link, vec_link, pool_link = sem("act_link"), sem("vec_link"), sem("pool_link")
        silu_exp, silu_ready = sem("silu_exp"), sem("silu_ready")
        acc_init = [sem("acc_init0"), sem("acc_init1")]
        mod_read = sem("mod_read")
        mod_cols = sem("mod_cols")
        squared = sem("squared")
        ms_ready, sd_ready, rstd_ready = sem("ms_ready"), sem("sd_ready"), sem("rstd_ready")
        yn_ready = sem("yn_ready")
        seq_done, scaled, dft_done = sem("seq_done"), sem("scaled"), sem("dft_done")
        dft_high, dft_low = sem("dft_high"), sem("dft_low")
        acc_zero = sem("acc_zero")
        summed = sem("summed")
        up_taken, up_ready = sem("up_taken"), sem("up_ready")
        t_posed, t_high, t_low = sem("t_posed"), sem("t_high"), sem("t_low")
        xn_ready, n_posed = sem("xn_ready"), sem("n_posed")
        n_scaled, n_high, n_low = sem("n_scaled"), sem("n_high"), sem("n_low")
        gated = sem("gated")
        x_updated = sem("x_updated")
        qkv_taken = sem("qkv_taken")
        a_posed, a_turned = sem("a_posed"), sem("a_turned")
        f_raw, f_high, f_low = sem("f_raw"), sem("f_high"), sem("f_low")
        f_sum, f_exp, f_logit, f_ready = sem("f_sum"), sem("f_exp"), sem("f_logit"), sem("f_ready")
        c_sum, c_ready = sem("c_sum"), sem("c_ready")
        z_ready, z_taken, z_logs = sem("z_ready"), sem("z_taken"), sem("z_logs")
        mid_in, mid_ready, mid_taken = sem("mid_in"), sem("mid_ready"), sem("mid_taken")
        fox_exp = sem("fox_exp")
        probs_ready = sem("probs_ready")
        o_ready, o_taken = sem("o_ready"), sem("o_taken")
        hms_ready, hsd_ready, mixed_ready = sem("hms_ready"), sem("hsd_ready"), sem("mixed_ready")
        m_posed, m_scaled, m_high, m_low = sem("m_posed"), sem("m_scaled"), sem("m_high"), sem("m_low")
        final_gained = sem("final_gained")
        final_first, final_second, out_done = sem("final_first"), sem("final_second"), sem("out_done")

        block = ctx.enter_context(nc.Block())

        @block.sync
        def _(eng):
            t = Tally()

            def load(src, shape=None):
                slot = t.c["raw"] % RAW
                if t.c["raw"] >= RAW or t.q is not None:
                    eng.wait_ge(raw_used, t.at("raw", 1 - RAW))
                dst = raw[:, slot, :]
                if shape is not None:
                    dst = dst.rearrange("p (k n) -> p k n", k=4)
                eng.dma_start(dst, src).then_inc(raw_loaded[slot], 16)
                t.add("raw")

            def chunk(w, row, col):
                load(w[bass.ds(row, 4 * P), bass.ds(col, CW)].rearrange("(k p) n -> p k n", p=P), 4)

            def mod_tile(unit, kk):
                load(w_mod[bass.ds(kk * P, P), unit * D:(unit + 1) * D])

            eng.wait_ge(vec_in, 16 * 8)
            for i in range(RAW):
                mod_tile(0, i)
            for unit in range(3):
                with t.loop(eng, 1 if unit == 0 else 0, KT // RAW, raw=RAW) as q:
                    for i in range(RAW):
                        mod_tile(unit, q * RAW + i)
            for ch in range(4 * NC):
                chunk(fnet_w, ch % 4 * 4 * P, ch // 4 * CW)
                if ch >= 2:
                    mod_tile(3, ch - 2)
            mod_tile(3, KT - 2)
            mod_tile(3, KT - 1)
            with t.loop(eng, 0, KT // RAW, raw=RAW) as q:
                for i in range(RAW):
                    mod_tile(4, q * RAW + i)

            def mlp_chunk(w1, w2, q, ch):
                step, j = divmod(ch, 4)
                if step < NC:
                    chunk(w1, j * 4 * P, q * D + step * CW)
                else:
                    chunk(w2, q * D + j * 4 * P, (step - NC) * CW)

            chunk(w_mlp_in, 0, 0)
            chunk(w_mlp_in, 4 * P, 0)

            with t.loop(eng, 0, MOD_LOOPS, raw=32 + len(MOD_AFTER)) as q:
                for pos in range(32):
                    if pos < 30:
                        mlp_chunk(w_mlp_in, w_mlp_out, q, pos + 2)
                    else:
                        chunk(w_mlp_in, (pos - 30) * 4 * P, (q + 1) * D)
                    if pos in MOD_AFTER:
                        mod_tile(5, q * len(MOD_AFTER) + MOD_AFTER.index(pos))
            for q in range(MOD_LOOPS, QUARTERS):
                for ch in range(2, 32):
                    mlp_chunk(w_mlp_in, w_mlp_out, q, ch)
                for j in range(2):
                    if q < QUARTERS - 1:
                        chunk(w_mlp_in, j * 4 * P, (q + 1) * D)
                    else:
                        chunk(w_in, j * 4 * P, in_column(0, 0))
            for g in range(GROUPS):
                for r in range(3):
                    for j in range(2 if g == r == 0 else 0, 4):
                        chunk(w_in, j * 4 * P, in_column(g, r))
            for c, j in OUT_ORDER:
                chunk(w_out, j * 4 * P, c * CW)
            chunk(w_up, 0, 0)
            chunk(w_up, 4 * P, 0)
            with t.loop(eng, 0, QUARTERS - 1, raw=32) as q:
                for ch in range(2, 32):
                    mlp_chunk(w_up, w_down, q, ch)
                for j in range(2):
                    chunk(w_up, j * 4 * P, (q + 1) * D)
            for ch in range(2, 32):
                mlp_chunk(w_up, w_down, QUARTERS - 1, ch)
            outv = out.rearrange("(t p) n -> p t n", p=P)
            for part in range(2):
                piece = slice(part * D // 2, (part + 1) * D // 2)
                for tt, ready in ((1, final_second), (0, final_first)):
                    eng.wait_ge(ready, part + 1)
                    eng.dma_start(outv[:, tt, piece], acc[:, tt, piece]).then_inc(out_done, 16)
            eng.wait_ge(out_done, 16 * 4)

        @block.gpsimd
        def _(eng):
            for v in range(6):
                if v == 3:
                    eng.wait_ge(dft_done, FG)
                if v >= 2:
                    eng.wait_ge(mod_read, v if v == 5 else v - 1)
                eng.memset(mod_acc(v), 0.0).then_inc(pool_link, 1)
                eng.wait_ge(pool_link, v + 1)
                eng.dma_start(mod_acc(v)[0:1, :], b_mod[0:1, v * D:(v + 1) * D]).then_inc(acc_init[v % 2], 16)
                if v == 1:
                    eng.dma_start(grow[:, :], norm_g[1:2, :].broadcast_to([P, D])).then_inc(grow_in, 16)
                    eng.dma_start(wf[:, :].rearrange("p (k n) -> p k n", k=KT),
                                  w_in[:, 6 * HEADS * HD:6 * HEADS * HD + HEADS]
                                  .rearrange("(k p) n -> p k n", p=P)).then_inc(f_raw, 16)
                    for tt in range(TT):
                        eng.dma_start(bf[:, tt * HEADS:(tt + 1) * HEADS],
                                      b_f.broadcast_to([P, HEADS])).then_inc(f_raw, 16)
                if v == 2:
                    eng.wait_ge(seq_done, FG)
                    eng.memset(acc[:, :, :], 0.0).then_inc(acc_zero, 1)
            eng.wait_ge(x_updated, TT * NC)
            eng.dma_start(grow[:, :], norm_g[3:4, :].broadcast_to([P, D])).then_inc(grow_in, 16)
            eng.wait_ge(n_posed, TT * NC)
            eng.memset(acc[:, :, :], 0.0).then_inc(acc_zero, 1)
            eng.wait_ge(mod_read, 6)
            eng.wait_ge(n_posed, 2 * TT * NC)
            eng.dma_start(sel, select).then_inc(sel_in, 16)
            eng.wait_ge(o_ready, GROUPS * GH)
            eng.dma_start(grow[:, :], g_final.broadcast_to([P, D])).then_inc(grow_in, 16)

        @block.tensor
        def _(eng):
            t = Tally()

            def half(n, hh, high, low):
                slot = t.c["half"] % LEAD
                if t.c["half"] % 2 == 0:
                    t.add("chunk")
                    eng.wait_ge(low_first, t.at("chunk", 0))
                else:
                    t.add("raw")
                    eng.wait_ge(raw_used, t.at("raw", 0))
                for tt in range(TT):
                    for kk in range(2):
                        k = 2 * hh + kk
                        wh = w_high[:, slot, kk * CW:(kk + 1) * CW]
                        wl = w_low[:, slot, kk * CW:(kk + 1) * CW]
                        ah = high[:, k, tt * P:(tt + 1) * P]
                        al = low[:, k, tt * P:(tt + 1) * P]
                        dst = lin(n)[:, tt, :]
                        eng.matmul(dst, ah, wh, start=(k == 0), stop=False)
                        eng.matmul(dst, ah, wl, start=False, stop=False)
                        last = eng.matmul(dst, al, wh, start=False, stop=(k == KT - 1))
                last.then_inc(half_used, 1)
                t.add("half")

            def sum_partitions_to_columns(v, place):
                if place:
                    eng.wait_ge(mod_cols, t.c["mod_cols"])
                for j in range(KT):
                    last = eng.matmul(ps[:, 3, place * KT + j:place * KT + j + 1],
                                      mod_acc(v)[:, j * P:(j + 1) * P], ones[:, 0:1], start=True, stop=True)
                last.then_inc(mod_read, 1)
                t.add("mod_cols")

            def sum_partitions_to_rows(v):
                for j in range(NC):
                    last = eng.matmul(side(j), ones, mod_acc(v)[:, j * CW:(j + 1) * CW], start=True, stop=True)
                last.then_inc(mod_read, 1)
                t.add("mod_cols")

            def turn(dst, src):
                for b in range(4):
                    last = eng.transpose(dst[:, b * P:(b + 1) * P], src[:, b * P:(b + 1) * P], ident)
                return last

            def norm_turn(first, stop):
                for i in range(first, stop):
                    j, tt = divmod(i, TT)
                    t.add("norm")
                    eng.wait_ge(xn_ready, t.c["norm"])
                    turn(ps[:, TURN_BANKS[i], :], acc[:, tt, j * CW:(j + 1) * CW]).then_inc(n_posed, 1)

            def h_ready(hh):
                if hh % 2 == 0:
                    eng.wait_ge(n_low, t.c["norm"] - 6 + hh)

            def turn_hidden(tt, mods_read):
                if tt == 0:
                    eng.wait_ge(up_ready, t.at("up", 0))
                if t.c["t"] % (2 * NC):
                    eng.wait_ge(t_low, t.at("t", 0))
                elif mods_read:
                    eng.wait_ge(mod_cols, mods_read)
                turn(side(0), hidden[:, tt, :]).then_inc(t_posed, 1)
                t.add("t")

            def mlp(start, stop, mods=(), mods_read=0):
                def step(n, c, high, low, first):
                    for hh in range(HALVES):
                        first(hh)
                        half(n, hh, high, low)
                        if t.c["half"] % 2 == 0 and (4 * n + hh // 2) - 2 in mods:
                            t.add("raw")
                        if 1 <= n <= NC and hh in (1, 3):
                            turn_hidden(hh // 2, mods_read)

                with t.loop(eng, start, stop, half=64, chunk=32, raw=32 + len(mods), summed=NC, up=NC, t=2 * NC):
                    for c in range(NC):
                        if c < 2:
                            eng.wait_ge(summed, t.at("summed", c - 1))
                        else:
                            eng.wait_ge(up_taken, t.at("up", -1))
                        step(c, c, h_high, h_low, h_ready if c == 0 else lambda hh: None)
                        t.add("up")
                    for c in range(NC):
                        if c < 2:
                            eng.wait_ge(up_taken, t.at("up", c - 1))
                        else:
                            eng.wait_ge(summed, t.at("summed", -1))

                        def hidden_ready(hh):
                            if c == 0 and hh % 2 == 0:
                                eng.wait_ge(t_low, t.at("t", hh + 2 - 2 * NC) if hh < 6 else t.at("t", 0))

                        step(NC + c, c, u_high, u_low, hidden_ready)
                        t.add("summed")

            eng.wait_ge(vec_in, 16 * 8)
            eng.transpose(side(0)[:, 0:V_ALL], junk[0:V_ALL, 0:P], cst[0:V_ALL, C_ID:C_ID + V_ALL])\
               .then_inc(vec_turned, 1)
            eng.wait_ge(cst_in, 16)
            for v in range(2):
                t.add("raw", KT)
                eng.wait_ge(raw_used, t.c["raw"])
                sum_partitions_to_columns(v, v)
            eng.wait_ge(mod_cols, 2)
            eng.wait_ge(yn_ready, TT)
            eng.wait_ge(dft_in, 16)

            def over_sequence(g):
                if g >= 2:
                    eng.wait_ge(scaled, g - 1)
                for d in range(2):
                    k = 2 * g + d
                    for tt in range(TT):
                        last = eng.matmul(side(2 * (g % 2) + d), acc[:, tt, k * P:(k + 1) * P],
                                          tables[:, tt, 0:2 * SEQ], start=(tt == 0), stop=(tt == 1))
                last.then_inc(seq_done, 1)

            over_sequence(0)
            for g in range(FG):
                if g + 1 < FG:
                    over_sequence(g + 1)
                eng.wait_ge(scaled, g + 1)
                if g >= 2:
                    eng.wait_ge(dft_low, g - 1)
                for e in range(2):
                    dst = lin(g)[:, 0, e * SEQ:(e + 1) * SEQ]
                    for d in range(2):
                        eng.matmul(dst, tables[:, d, e * P:(e + 1) * P], seq_dft[:, g % 2, d, 0:SEQ],
                                   start=(d == 0), stop=False)
                        last = eng.matmul(dst, tables[:, d, 2 * SEQ + e * P:2 * SEQ + (e + 1) * P],
                                          seq_dft[:, g % 2, d, SEQ:2 * SEQ], start=False, stop=(d == 1))
                last.then_inc(dft_done, 1)
            t.add("raw", KT)
            eng.wait_ge(raw_used, t.c["raw"])
            sum_partitions_to_rows(2)
            eng.wait_ge(dft_low, FG)
            for c in range(NC):
                if c >= 2:
                    eng.wait_ge(summed, c - 1)
                for hh in range(HALVES):
                    half(c, hh, h_high, h_low)
                    if hh % 2 and 4 * c + hh // 2 >= 2:
                        t.add("raw")
                t.add("summed")
            t.add("raw", 2)
            eng.wait_ge(raw_used, t.c["raw"])
            eng.wait_ge(summed, NC)
            sum_partitions_to_columns(3, 2)
            norm_turn(0, 7)
            t.add("raw", KT)
            eng.wait_ge(raw_used, t.c["raw"])
            sum_partitions_to_columns(4, 3)
            eng.wait_ge(mod_cols, 5)
            norm_turn(7, 8)
            mlp(0, MOD_LOOPS, MOD_AFTER)
            sum_partitions_to_rows(5)
            mlp(MOD_LOOPS, QUARTERS, mods_read=6)
            norm_turn(0, 8)

            def forget_logits():
                eng.wait_ge(f_low, 1)
                for tt in range(TT):
                    dst = side(3)[:, tt * HEADS:(tt + 1) * HEADS]
                    for k in range(KT):
                        ah = h_high[:, k, tt * P:(tt + 1) * P]
                        al = h_low[:, k, tt * P:(tt + 1) * P]
                        fh = wf_high[:, k * HEADS:(k + 1) * HEADS]
                        f_l = wf_low[:, k * HEADS:(k + 1) * HEADS]
                        eng.matmul(dst, ah, fh, start=(k == 0), stop=False)
                        eng.matmul(dst, ah, f_l, start=False, stop=False)
                        last = eng.matmul(dst, al, fh, start=False, stop=(k == KT - 1))
                last.then_inc(f_sum, 1)

            def forget_sums():
                eng.wait_ge(f_ready, 1)
                lf = [fl[:, tt * HEADS:(tt + 1) * HEADS] for tt in range(TT)]
                le, one = cst[:, C_LE:C_LE + P], ones
                eng.matmul(side(3)[0:HEADS, 0:SEQ], lf[0], cst[:, C_LE:C_LE + SEQ], start=True, stop=False)
                eng.matmul(side(3)[0:HEADS, P:SEQ], lf[1], le, start=False, stop=True)
                col = side(3)[:, SEQ:SEQ + 2 * HEADS]
                eng.matmul(col[:, 0:HEADS], le, lf[0], start=True, stop=True)
                eng.matmul(col[:, HEADS:2 * HEADS], one, lf[0], start=True, stop=False)
                eng.matmul(col[:, HEADS:2 * HEADS], le, lf[1], start=False, stop=True).then_inc(c_sum, 1)

            def scores(g, i):
                n = t.c["z"]
                q_h, k_h = qT[:, g % 2, i, :], kT[:, g % 2, i, :]
                eng.wait_ge(a_turned, 4 * (g + 1))
                if n:
                    eng.wait_ge(z_taken, n)
                bank = side(1)
                if g < 2:
                    eng.matmul(bank[:, 0:SEQ], k_h[:, 0:P], q_h, start=True, stop=True)
                    eng.matmul(bank[:, SEQ:384], k_h[:, P:SEQ], q_h[:, P:SEQ], start=True, stop=True)\
                       .then_inc(z_ready, 1)
                else:
                    if g == 2 and i == 0:
                        eng.wait_ge(c_ready, 1)
                        eng.wait_ge(sel_in, 16)
                    s_h = sel[:, GH * (g - 2) + i, :]
                    eng.matmul(bank[:, 0:P], q_h[:, 0:P], k_h[:, 0:P], start=True, stop=False)
                    eng.matmul(bank[:, 0:P], s_h, negc[:, 0:P], start=False, stop=True)
                    eng.matmul(bank[:, P:384], q_h[:, P:SEQ], k_h, start=True, stop=False)
                    eng.matmul(bank[:, P:384], s_h, negc[:, :], start=False, stop=True)\
                       .then_inc(z_ready, 1)
                t.add("z")

            def middle(g, i):
                n = t.c["mid"]
                e = ew[:, n % 2, :]
                if n:
                    eng.wait_ge(mid_taken, n) if g < 2 or n == 2 * GH else eng.wait_ge(probs_ready, n)
                bank = side(2)
                if g < 2:
                    eng.wait_ge(mid_in, n + 1)
                    eng.matmul(bank[:, 0:384], cst[:, C_GE:C_GE + P], e, start=True, stop=False)
                    eng.matmul(bank[:, P:SEQ], ones, e[:, SEQ:384], start=False, stop=True)\
                       .then_inc(mid_ready, 1)
                else:
                    eng.wait_ge(fox_exp, n + 1 - 2 * GH)
                    for b in range(3):
                        last = eng.transpose(bank[:, b * P:(b + 1) * P], e[:, b * P:(b + 1) * P], ident)
                    last.then_inc(mid_ready, 1)
                t.add("mid")

            def weigh_values(g, i):
                n = t.c["o"]
                a = probs[:, n % 2, :]
                v_h = [vv[:, g % 2, tt, i * HD:(i + 1) * HD] for tt in range(TT)]
                eng.wait_ge(probs_ready, n + 1)
                if n == 0 or i == 0:
                    eng.wait_ge(qkv_taken, 3 * (g + 1))
                if n:
                    eng.wait_ge(o_taken, n)
                else:
                    eng.wait_ge(c_ready, 1)
                eng.matmul(side(3)[:, 0:HD], a[:, 0:P], v_h[0], start=True, stop=True)
                eng.matmul(side(3)[:, HD:2 * HD], a[:, P:SEQ], v_h[0], start=True, stop=False)
                eng.matmul(side(3)[:, HD:2 * HD], a[:, SEQ:384], v_h[1], start=False, stop=True)\
                   .then_inc(o_ready, 1)
                t.add("o")

            def turn_mixed(g, tt):
                if tt == 0:
                    eng.wait_ge(mixed_ready, g + 1)
                    eng.wait_ge(a_turned, min(4 * (g + 2), 4 * GROUPS))
                else:
                    eng.wait_ge(m_scaled, 2 * g + 1)
                turn(side(0), normed[:, tt, :]).then_inc(m_posed, 1)

            def attention(g, jobs):
                for job, i in jobs:
                    {"z": scores, "mid": middle, "out": weigh_values, "turn": turn_mixed}[job](g, i)

            def turn_qk(n, tt):
                g, r = divmod(n, 3)
                done = 4 * g + 2 * r + tt
                if tt == 0:
                    eng.wait_ge(qkv_taken, n + 1)
                if done:
                    eng.wait_ge(a_turned, done)
                if r == 0 and tt == 0 and g >= 2:
                    eng.wait_ge(m_scaled, 2 * (g - 1))
                turn(side(0), stage[:, tt, :]).then_inc(a_posed, 1)

            for n in range(3 * GROUPS):
                if n < 2:
                    eng.wait_ge(summed, t.c["summed"] - 1 + n)
                else:
                    eng.wait_ge(qkv_taken, n - 1)
                g, r = divmod(n, 3)
                for hh in range(HALVES):
                    if n == 0:
                        h_ready(hh)
                    half(n, hh, h_high, h_low)
                    if hh in (1, 3) and n % 3:
                        turn_qk(n - 1, hh // 2)
                    if n == 0 and hh == 7:
                        forget_logits()
                    if n == 1 and hh == 5:
                        forget_sums()
                    if g:
                        attention(g - 1, SLOTS.get(r * HALVES + hh, ()))
            for y, (c, j) in enumerate([o for o in OUT_ORDER for _ in range(2)]):
                hh = 2 * j + y % 2
                if hh == 0:
                    if c < 2:
                        eng.wait_ge(qkv_taken, 3 * GROUPS - 1 + c)
                    else:
                        eng.wait_ge(summed, t.c["summed"] - 1)
                if y % 2 == 0 and (y < 6 or j == 3):
                    eng.wait_ge(m_low, 2 * (j + 1))
                half(c, hh, u_high, u_low)
                if hh == 7:
                    t.add("summed")
                attention(GROUPS - 1, LAST_SLOTS.get(y, ()))
            norm_turn(0, 8)
            mlp(0, QUARTERS)

        @block.scalar
        def _(eng):
            t = Tally()

            def link(ins):
                ins.then_inc(act_link, 1)
                t.add("link")
                eng.wait_ge(act_link, t.at("link", 0))

            def high_part():
                h = t.c["high"]
                slot = t.c["raw"] % RAW
                if h % 2 == 0:
                    eng.wait_ge(raw_loaded[slot], t.arrived())
                if h >= LEAD or t.q is not None:
                    eng.wait_ge(half_used, t.at("high", 1 - LEAD))
                eng.activation(w_high[:, h % LEAD, :], raw[:, slot, (h % 2) * 2 * CW:(h % 2 + 1) * 2 * CW],
                               ACT.Copy).then_inc(high_ready, 1)
                t.add("high")
                if h % 2:
                    t.add("raw")

            def square_sum(src, column):
                if t.c["squared"] or t.q is not None:
                    eng.wait_ge(squared, t.at("squared", 0))
                t.add("squared")
                eng.activation(junk[:, :], src, ACT.Square, accum_out=ssq[:, column:column + 1])\
                   .then_inc(squared, 1)

            def step_squares(target, c, done):
                eng.wait_ge(summed, done)
                for tt in range(TT):
                    square_sum(target[:, tt, c * CW:(c + 1) * CW], tt * NC + c)

            def root():
                t.add("root")
                eng.wait_ge(ms_ready, t.c["root"])
                eng.activation(sd[:, :], ms[:, :], ACT.Sqrt).then_inc(sd_ready, 1)

            def scale_turned(i, scale, shift):
                j = i // TT
                t.add("norm")
                eng.wait_ge(n_posed, t.c["norm"])
                if t.c["norm"] > 2:
                    eng.wait_ge(n_low, t.c["norm"] - 2)
                for b in range(4):
                    k = 4 * j + b
                    src, dst = ps[:, TURN_BANKS[i], b * P:(b + 1) * P], turned[:, i % 2, b * P:(b + 1) * P]
                    if shift is None:
                        last = eng.activation(dst, src, ACT.Copy, scale=scale[:, k:k + 1])
                    else:
                        last = eng.activation(dst, src, ACT.Identity, scale=scale[:, k:k + 1],
                                              bias=shift[:, k:k + 1])
                last.then_inc(n_scaled, 1)

            def residual_squares():
                for i in range(TT * NC):
                    tt, j = divmod(i, NC)
                    t.add("x_updated")
                    eng.wait_ge(x_updated, t.c["x_updated"])
                    square_sum(xs[:, tt, j * CW:(j + 1) * CW], i)

            def mlp_body(target, mods=(), ahead=True):
                for y in range(64):
                    if y < 60 or ahead:
                        high_part()
                        if t.c["high"] % 2 == 0 and (y // 2) in mods:
                            t.add("raw")
                    c, hh = divmod(y, HALVES)
                    if 1 <= c <= NC and hh in (1, 3):
                        tt = hh // 2
                        t.add("t")
                        eng.wait_ge(t_posed, t.at("t", 0))
                        eng.activation(u_high[:, 4 * (c - 1):4 * c, tt * P:(tt + 1) * P],
                                       side(0).rearrange("p (b n) -> p b n", b=4), ACT.Copy).then_inc(t_high, 1)
                    if hh == 7:
                        t.add("done", 8)
                        eng.wait_ge(half_used, t.at("done", 0))
                        if c < NC:
                            t.add("up")
                            eng.activation(relu, lin(c), ACT.Relu).then_inc(up_taken, 1)
                            eng.wait_ge(up_taken, t.at("up", 0))
                            eng.activation(hidden, relu, ACT.Square).then_inc(up_ready, 1)
                        else:
                            t.add("summed")
                            step_squares(target, c - NC, t.at("summed", 0))

            eng.dma_start(ident, consts[:, C_ID:C_ID + P]).then_inc(vec_in, 16)
            for src, row, rows in ((c_in, V_C, KT), (norm_g[0:1, :], V_G0, KT), (norm_g[2:3, :], V_G2, KT),
                                   (g_attn, V_GA, KT), (g_mlp, V_GM, KT), (g_out_sb, V_GO, HEADS),
                                   (g_out_fox, V_GO + HEADS, HEADS)):
                eng.dma_start(junk[row:row + rows, 0:P], src.rearrange("o (r n) -> (o r) n", n=P))\
                   .then_inc(vec_in, 16)
            eng.dma_start(cst[:, C_GE:C_ALL], consts[:, C_GE:C_ALL]).then_inc(cst_in, 16)
            eng.dma_start(xs[:, :, :], x.rearrange("(t p) n -> p t n", p=P)).then_inc(x_in, 16)
            eng.dma_start(extra[:, :].rearrange("p (t n) -> p t n", t=TT), dft.rearrange("(t p) n -> p t n", p=P))\
               .then_inc(dft_in, 16)
            eng.wait_ge(vec_ready, 1)
            eng.activation(silu_t[:, 0:KT], cols[:, V_C:V_C + KT], ACT.Exp, scale=-1.0).then_inc(silu_exp, 1)
            eng.wait_ge(x_in, 16)
            for i in range(TT * NC):
                tt, j = divmod(i, NC)
                square_sum(xs[:, tt, j * CW:(j + 1) * CW], i)
            root()
            eng.wait_ge(rstd_ready, 1)
            for tt in range(TT):
                eng.activation(acc[:, tt, :], xs[:, tt, :], ACT.Copy, scale=rstd[:, tt:tt + 1])\
                   .then_inc(yn_ready, 1)
            eng.wait_ge(mod_cols, 2)

            def scale_and_shift(g):
                eng.wait_ge(seq_done, g + 1)
                if g >= 2:
                    eng.wait_ge(dft_done, g - 1)
                for d in range(2):
                    k = 2 * g + d
                    ins = eng.activation(seq_dft[:, g % 2, d, :], side(2 * (g % 2) + d), ACT.Copy,
                                         scale=scale1[:, k:k + 1])
                link(ins)
                for d in range(2):
                    k = 2 * g + d
                    at0 = seq_dft[:, g % 2, d, 0:1]
                    last = eng.activation(at0, at0, ACT.Identity, bias=shift1[:, k:k + 1])
                last.then_inc(scaled, 1)

            scale_and_shift(0)
            for g in range(FG):
                if g + 1 < FG:
                    scale_and_shift(g + 1)
                eng.wait_ge(dft_done, g + 1)
                eng.activation(h_high[:, 2 * g:2 * g + 2, :],
                               lin(g)[:, 0, :].rearrange("p (e s) -> p e s", e=2), ACT.Copy).then_inc(dft_high, 1)
            t.add("raw", 3 * KT)

            def fnet_high():
                high_part()
                if t.c["high"] % 2 == 0 and t.c["high"] >= 6:
                    t.add("raw")

            for _ in range(LEAD):
                fnet_high()
            for y in range(NC * HALVES):
                if y < NC * HALVES - LEAD:
                    fnet_high()
                if y % HALVES == 7:
                    t.add("done", 8)
                    t.add("summed")
                    step_squares(acc, y // HALVES, t.c["summed"])
            t.add("raw", 2 + KT)
            root()
            residual_squares()
            root()
            eng.wait_ge(mod_cols, 5)
            for i in range(TT * NC):
                scale_turned(i, scale2, mcol[:, 2 * KT:3 * KT])
                if i % 2:
                    high_part()
            with t.loop(eng, 0, MOD_LOOPS, high=64, raw=32 + len(MOD_AFTER), t=2 * NC, done=64, up=NC, summed=NC,
                        squared=TT * NC):
                mlp_body(acc, MOD_AFTER)
            for q in range(MOD_LOOPS, QUARTERS):
                mlp_body(acc)
            root()
            residual_squares()
            root()
            for i in range(TT * NC):
                scale_turned(i, cols[:, V_GA:V_GA + KT], None)

            def take_qkv(n):
                g, r = divmod(n, 3)
                t.add("done", 8)
                eng.wait_ge(half_used, t.c["done"])
                if r < 2:
                    if n:
                        eng.wait_ge(a_posed, 4 * g + 2 * r)
                    eng.activation(stage, lin(n), ACT.Copy, scale=(float(HD) ** -0.5 if r == 0 else 1.0))\
                       .then_inc(qkv_taken, 1)
                else:
                    if g >= 2:
                        eng.wait_ge(o_ready, GH * (g - 1))
                    eng.activation(vv[:, g % 2, :, :], lin(n), ACT.Copy).then_inc(qkv_taken, 1)

            def forget_high():
                eng.wait_ge(f_raw, 48)
                eng.activation(wf_high[:, :], wf[:, :], ACT.Copy).then_inc(f_high, 1)

            def forget_gate():
                eng.wait_ge(f_logit, 1)
                link(eng.activation(fe[:, :], fl[:, :], ACT.Abs))
                link(eng.activation(fe[:, :], fe[:, :], ACT.Exp, scale=-1.0))
                eng.activation(fe[:, :], fe[:, :], ACT.Ln, bias=1.0).then_inc(f_exp, 1)

            def score_logs(g, i):
                n = t.c["z"]
                t.add("z")
                z, e = zs[:, n % 2, :], ew[:, n % 2, :]
                eng.wait_ge(z_taken, n + 1)
                if g < 2:
                    link(eng.activation(e, z, ACT.Abs))
                    link(eng.activation(e, e, ACT.Exp, scale=-1.0))
                    eng.activation(e, e, ACT.Ln, bias=1.0).then_inc(z_logs, 1)
                else:
                    eng.wait_ge(mid_in, n + 1)
                    for tt, (a, b) in enumerate(((0, P), (P, 384))):
                        last = eng.activation(e[:, a:b], z[:, a:b], ACT.Exp,
                                              bias=negmax[:, tt * GH + i:tt * GH + i + 1],
                                              accum_out=psums[:, tt * GH + i:tt * GH + i + 1])
                    last.then_inc(fox_exp, 1)

            def take_middle(g, i):
                n = t.c["mid"]
                t.add("mid")
                if n >= 2:
                    eng.wait_ge(o_ready, n - 1)
                if g < 2:
                    eng.wait_ge(mid_taken, n + 1)
                    eng.activation(probs[:, n % 2, :], ew[:, n % 2, :], ACT.Exp).then_inc(probs_ready, 1)
                else:
                    eng.wait_ge(mid_ready, n + 1)
                    eng.activation(probs[:, n % 2, :], side(2)[:, 0:384], ACT.Copy).then_inc(probs_ready, 1)

            def head_root(g, i):
                if i == 3:
                    eng.wait_ge(hms_ready, g + 1)
                    eng.activation(hsd[:, :], hms[:, :], ACT.Sqrt).then_inc(hsd_ready, 1)

            def take_mixed(g, tt):
                eng.wait_ge(m_posed, 2 * g + tt + 1)
                if 2 * g + tt:
                    eng.wait_ge(m_low, 2 * g + tt)
                for b in range(4):
                    k = V_GO + 4 * g + b
                    last = eng.activation(fin[:, b * P:(b + 1) * P], side(0)[:, b * P:(b + 1) * P],
                                          ACT.Copy, scale=cols[:, k:k + 1])
                last.then_inc(m_scaled, 1)

            def attention(g, jobs):
                for job, i in jobs:
                    {"z": score_logs, "mid": take_middle, "out": head_root, "turn": take_mixed}[job](g, i)

            forget_high()
            for n in range(3 * GROUPS):
                g, r = divmod(n, 3)
                for hh in range(HALVES):
                    high_part()
                    if hh == 7:
                        take_qkv(n)
                    if n == 0 and hh == 7:
                        forget_gate()
                    if g:
                        attention(g - 1, SLOTS.get(r * HALVES + hh, ()))
            for y, (c, j) in enumerate([o for o in OUT_ORDER for _ in range(2)]):
                high_part()
                if j == 3 and y % 2:
                    t.add("summed")
                    step_squares(xs, c, t.c["summed"])
                attention(GROUPS - 1, LAST_SLOTS.get(y, ()))
            t.add("done", 8 * NC)
            root()
            for i in range(TT * NC):
                scale_turned(i, cols[:, V_GM:V_GM + KT], None)
            with t.loop(eng, 0, QUARTERS - 1, high=64, raw=32, t=2 * NC, done=64, up=NC, summed=NC,
                        squared=TT * NC):
                mlp_body(xs)
            mlp_body(xs, ahead=False)
            root()
            eng.wait_ge(rstd_ready, t.c["root"])
            eng.wait_ge(final_gained, NC)
            for part in range(2):
                piece = acc[:, 0, part * D // 2:(part + 1) * D // 2]
                eng.activation(piece, piece, ACT.Copy, scale=rstd[:, 0:1]).then_inc(final_first, 1)

        @block.vector
        def _(eng):
            t = Tally()

            def link(ins):
                ins.then_inc(vec_link, 1)
                t.add("link")
                eng.wait_ge(vec_link, t.at("link", 0))

            def low_part():
                h = t.c["low"]
                slot = t.c["raw"] % RAW
                piece = slice((h % 2) * 2 * CW, (h % 2 + 1) * 2 * CW)
                eng.wait_ge(high_ready, t.at("low", 1))
                eng.tensor_tensor(w_low[:, h % LEAD, :], raw[:, slot, piece], w_high[:, h % LEAD, :].bitcast(f32),
                                  ALU.subtract).then_inc(raw_used if h % 2 else low_first, 1)
                t.add("low")
                if h % 2:
                    t.add("raw")

            def mod_tile(v, kk):
                slot = t.c["raw"] % RAW
                eng.wait_ge(raw_loaded[slot], t.arrived())
                if t.c["raw"]:
                    eng.wait_ge(raw_used, t.at("raw", 0))
                eng.scalar_tensor_tensor(out=mod_acc(v), in0=raw[:, slot, :], scalar=silu_c[:, bass.ds(kk, 1)],
                                         in1=mod_acc(v), op0=ALU.mult, op1=ALU.add).then_inc(raw_used, 1)
                t.add("raw")

            def mod_columns(v, place):
                eng.wait_ge(mod_read, v + 1)
                col = mcol[:, place * KT:(place + 1) * KT]
                src = ps[:, 3, place * KT:(place + 1) * KT]
                if place == 0:
                    link(eng.tensor_copy(col, src))
                    eng.tensor_scalar(shift1[:, :], col, float(SEQ), None, ALU.mult).then_inc(mod_cols, 1)
                elif place == 2:
                    eng.tensor_copy(col, src).then_inc(mod_cols, 1)
                else:
                    dst, gain = (scale1, V_G0) if place == 1 else (scale2, V_G2)
                    eng.scalar_tensor_tensor(out=dst[:, :], in0=src, scalar=1.0, in1=cols[:, gain:gain + KT],
                                             op0=ALU.add, op1=ALU.mult).then_inc(mod_cols, 1)

            def mod_rows(v, loads):
                eng.wait_ge(mod_read, v + 1)
                eng.wait_ge(grow_in, 16 * loads)
                for j in range(NC):
                    piece = grow[:, j * CW:(j + 1) * CW]
                    ins = eng.tensor_tensor(piece, side(j), piece, ALU.mult)
                return ins

            def mean_square():
                t.add("root")
                eng.wait_ge(squared, t.c["squared"])
                link(eng.tensor_reduce(ms[:, :], ssq[:, :].rearrange("p (t c) -> p t c", t=TT), AX.X, ALU.add))
                eng.tensor_scalar(ms[:, :], ms[:, :], 1.0 / D, EPS, ALU.mult, ALU.add).then_inc(ms_ready, 1)

            def invert():
                eng.wait_ge(sd_ready, t.c["root"])
                eng.reciprocal(rstd[:, :], sd[:, :]).then_inc(rstd_ready, 1)
                eng.wait_ge(rstd_ready, t.c["root"])

            def gate(c):
                eng.wait_ge(squared, t.c["squared"])
                if t.c["gated"]:
                    eng.wait_ge(gated, t.c["gated"])
                piece = acc[:, :, c * CW:(c + 1) * CW]
                row = grow[:, c * CW:(c + 1) * CW].unsqueeze(1).to_broadcast([P, TT, CW])
                eng.tensor_tensor(piece, piece, row, ALU.mult).then_inc(gated, 1)
                t.add("gated")

            def update(i):
                tt, j = divmod(i, NC)
                piece = xs[:, tt, j * CW:(j + 1) * CW]
                if i == 0:
                    eng.wait_ge(gated, t.c["gated"])
                eng.scalar_tensor_tensor(out=piece, in0=acc[:, tt, j * CW:(j + 1) * CW], scalar=rstd[:, tt:tt + 1],
                                         in1=piece, op0=ALU.mult, op1=ALU.add).then_inc(x_updated, 1)
                t.add("squared")
                t.add("updated")

            def normalize(i):
                j, tt = divmod(i, TT)
                piece = slice(j * CW, (j + 1) * CW)
                if i == 0 and t.c["updated"]:
                    eng.wait_ge(x_updated, t.c["updated"])
                eng.tensor_scalar(acc[:, tt, piece], xs[:, tt, piece], rstd[:, tt:tt + 1], None, ALU.mult)\
                   .then_inc(xn_ready, 1)

            def split_h(i):
                j, tt = divmod(i, TT)
                t.add("norm")
                src = turned[:, i % 2, :].rearrange("p (b n) -> p b n", b=4)
                high = h_high[:, 4 * j:4 * j + 4, tt * P:(tt + 1) * P]
                eng.wait_ge(n_scaled, t.c["norm"])
                eng.tensor_copy(high, src).then_inc(n_high, 1)
                eng.wait_ge(n_high, t.c["norm"])
                eng.tensor_tensor(h_low[:, 4 * j:4 * j + 4, tt * P:(tt + 1) * P], src, high.bitcast(f32),
                                  ALU.subtract).then_inc(n_low, 1)

            def norm():
                mean_square()
                invert()
                for i in range(TT * NC):
                    normalize(i)
                for i in range(TT * NC):
                    split_h(i)

            def add_step(target, n, c):
                eng.wait_ge(half_used, t.at("done", 0))
                piece = target[:, :, c * CW:(c + 1) * CW]
                eng.tensor_tensor(piece, lin(n), piece, ALU.add).then_inc(summed, 1)
                t.add("summed")
                t.add("squared", TT)

            def gain(c):
                eng.wait_ge(summed, t.at("summed", 0))
                row = grow[:, c * CW:(c + 1) * CW].unsqueeze(1).to_broadcast([P, TT, CW])
                eng.tensor_tensor(acc[:, :, c * CW:(c + 1) * CW], xs[:, :, c * CW:(c + 1) * CW], row, ALU.mult)\
                   .then_inc(final_gained, 1)

            def mlp_body(target, q=0, mods=(), ahead=True, after=None):
                for y in range(64):
                    if y < 60 or ahead:
                        low_part()
                        if t.c["low"] % 2 == 0 and (y // 2) in mods:
                            mod_tile(5, q * len(mods) + mods.index(y // 2))
                    c, hh = divmod(y, HALVES)
                    if 1 <= c <= NC and hh in (1, 3):
                        tt = hh // 2
                        t.add("t")
                        eng.wait_ge(t_high, t.at("t", 0))
                        high = u_high[:, 4 * (c - 1):4 * c, tt * P:(tt + 1) * P]
                        eng.tensor_tensor(u_low[:, 4 * (c - 1):4 * c, tt * P:(tt + 1) * P],
                                          side(0).rearrange("p (b n) -> p b n", b=4), high.bitcast(f32),
                                          ALU.subtract).then_inc(t_low, 1)
                    if hh == 7:
                        t.add("done", 8)
                        if c >= NC:
                            add_step(target, c, c - NC)
                    if after is not None and hh == 1 and c > NC:
                        after(c - 1 - NC)
                if after is not None:
                    after(NC - 1)

            eng.wait_ge(vec_turned, 1)
            eng.tensor_copy(cols[:, :], side(0)[:, 0:V_ALL]).then_inc(vec_ready, 1)
            eng.wait_ge(silu_exp, 1)
            eng.wait_ge(vec_ready, 1)
            link(eng.tensor_scalar(silu_t[:, KT:2 * KT], silu_t[:, 0:KT], 1.0, None, ALU.add))
            link(eng.reciprocal(silu_t[:, 0:KT], silu_t[:, KT:2 * KT]))
            link(eng.tensor_tensor(silu_c[:, :], silu_t[:, 0:KT], cols[:, V_C:V_C + KT], ALU.mult))
            for v in range(2):
                eng.wait_ge(acc_init[v], 16)
                if v == 0:
                    for i in range(RAW):
                        mod_tile(v, i)
                with t.loop(eng, 1 if v == 0 else 0, KT // RAW, raw=RAW) as q:
                    for i in range(RAW):
                        mod_tile(v, q * RAW + i)
                if v == 0:
                    t.add("squared", TT * NC)
                    mean_square()
                    invert()
                mod_columns(v, v)
            eng.wait_ge(acc_init[0], 16 * 2)

            def fnet_low():
                low_part()
                if t.c["low"] % 2 == 0 and t.c["low"] >= 6:
                    if t.c["low"] == 6:
                        eng.wait_ge(acc_init[1], 16 * 2)
                    mod_tile(3, t.c["low"] // 2 - 3)

            kk = 0
            for g in range(FG):
                for _ in range(4 if g == 0 else 2):
                    if kk < KT:
                        mod_tile(2, kk)
                        kk += 1
                if g == FG - 1:
                    for _ in range(LEAD):
                        fnet_low()
                eng.wait_ge(dft_high, g + 1)
                eng.tensor_tensor(h_low[:, 2 * g:2 * g + 2, :], lin(g)[:, 0, :].rearrange("p (e s) -> p e s", e=2),
                                  h_high[:, 2 * g:2 * g + 2, :].bitcast(f32), ALU.subtract).then_inc(dft_low, 1)
            mod_rows(2, 1).then_inc(mod_cols, 1)
            eng.wait_ge(acc_zero, 1)
            eng.wait_ge(mod_cols, 3)
            for y in range(NC * HALVES):
                if y < NC * HALVES - LEAD:
                    fnet_low()
                c, hh = divmod(y, HALVES)
                if hh == 7:
                    t.add("done", 8)
                    add_step(acc, c, c)
                if hh == 1 and c:
                    gate(c - 1)
            mod_tile(3, KT - 2)
            mod_tile(3, KT - 1)
            mod_columns(3, 2)
            eng.wait_ge(acc_init[0], 16 * 3)
            for i in range(KT):
                mod_tile(4, i)
                if i == 0:
                    gate(NC - 1)
                    mean_square()
                elif i == 1:
                    invert()
                elif 3 <= i < 11:
                    update(i - 3)
                elif i == 12:
                    mean_square()
                elif i == 13:
                    invert()
                    for piece in range(TT * NC):
                        normalize(piece)
            mod_columns(4, 3)
            for i in range(TT * NC):
                split_h(i)
                if i % 2:
                    low_part()
            eng.wait_ge(acc_init[1], 16 * 3)
            eng.wait_ge(acc_zero, 2)
            with t.loop(eng, 0, MOD_LOOPS, low=64, raw=32 + len(MOD_AFTER), t=2 * NC, done=64, squared=TT * NC,
                        summed=NC) as q:
                mlp_body(acc, q, MOD_AFTER)
            mod_rows(5, 2).then_inc(mod_cols, 1)
            for q in range(MOD_LOOPS, QUARTERS - 1):
                mlp_body(acc)
            eng.wait_ge(mod_cols, 6)
            mlp_body(acc, after=gate)
            mean_square()
            invert()
            for i in range(TT * NC):
                update(i)
            norm()

            def forget_low():
                eng.wait_ge(f_high, 1)
                eng.tensor_tensor(wf_low[:, :], wf[:, :], wf_high[:, :].bitcast(f32), ALU.subtract)\
                   .then_inc(f_low, 1)

            def forget_logit():
                eng.wait_ge(f_sum, 1)
                eng.tensor_tensor(fl[:, :], side(3)[:, 0:TT * HEADS], bf[:, :], ALU.add).then_inc(f_logit, 1)

            def forget_gate():
                eng.wait_ge(f_exp, 1)
                eng.scalar_tensor_tensor(out=fl[:, :], in0=fl[:, :], scalar=0.0, in1=fe[:, :],
                                         op0=ALU.min, op1=ALU.subtract).then_inc(f_ready, 1)

            def forget_sums():
                eng.wait_ge(c_sum, 1)
                eng.tensor_scalar(negc[:, :], side(3)[0:HEADS, 0:SEQ], -1.0, None, ALU.mult)
                eng.tensor_copy(csum[:, :], side(3)[:, SEQ:SEQ + TT * HEADS]).then_inc(c_ready, 1)

            def turned_qk(n, tt):
                g, r = divmod(n, 3)
                t.add("a")
                eng.wait_ge(a_posed, t.c["a"])
                dst = (qT, kT)[r][:, g % 2, :, tt * P:(tt + 1) * P]
                eng.tensor_copy(dst, side(0).rearrange("p (h n) -> p h n", h=GH)).then_inc(a_turned, 1)

            def mask_scores(g, i):
                n = t.c["z"]
                t.add("z")
                z = zs[:, n % 2, :]
                eng.wait_ge(z_ready, n + 1)
                if g < 2:
                    eng.tensor_tensor(z, side(1)[:, 0:384], cst[:, C_SB:C_SB + 384], ALU.add).then_inc(z_taken, 1)
                    return
                head = GH * (g - 2) + i
                for tt, (a, b) in enumerate(((0, P), (P, 384))):
                    last = eng.scalar_tensor_tensor(
                        out=z[:, a:b], in0=side(1)[:, a:b], scalar=csum[:, tt * HEADS + head:tt * HEADS + head + 1],
                        in1=cst[:, C_FOX + a:C_FOX + b], op0=ALU.add, op1=ALU.add)
                last.then_inc(z_taken, 1)
                eng.wait_ge(z_taken, n + 1)
                for tt, (a, b) in enumerate(((0, P), (P, 384))):
                    last = eng.tensor_reduce(negmax[:, tt * GH + i:tt * GH + i + 1], z[:, a:b], AX.X, ALU.max,
                                             negate=True)
                last.then_inc(mid_in, 1)

            def keep_logs(g, i):
                n = t.c["z"] - 1
                if g < 2:
                    e = ew[:, n % 2, :]
                    eng.wait_ge(z_logs, n + 1)
                    eng.scalar_tensor_tensor(out=e, in0=zs[:, n % 2, :], scalar=0.0, in1=e, op0=ALU.max,
                                             op1=ALU.add).then_inc(mid_in, 1)

            def take_middle(g, i):
                n = t.c["mid"]
                t.add("mid")
                eng.wait_ge(mid_ready, n + 1)
                if g < 2:
                    eng.tensor_tensor(ew[:, n % 2, :], zs[:, n % 2, :], side(2)[:, 0:384], ALU.subtract)\
                       .then_inc(mid_taken, 1)

            def take_out(g, i):
                n = t.c["o"]
                t.add("o")
                eng.wait_ge(o_ready, n + 1)
                if g < 2:
                    eng.tensor_copy(heads[:, :, i * HD:(i + 1) * HD],
                                    side(3)[:, 0:TT * HD].rearrange("p (t n) -> p t n", t=TT)).then_inc(o_taken, 1)
                else:
                    for tt in range(TT):
                        s = slice(tt * GH + i, tt * GH + i + 1)
                        ins = eng.reciprocal(precip[:, s], psums[:, s])
                    link(ins)
                    for tt in range(TT):
                        last = eng.tensor_scalar(heads[:, tt, i * HD:(i + 1) * HD], side(3)[:, tt * HD:(tt + 1) * HD],
                                                 precip[:, tt * GH + i:tt * GH + i + 1], None, ALU.mult)
                    last.then_inc(o_taken, 1)
                if i == GH - 1:
                    eng.wait_ge(o_taken, n + 1)
                    if g:
                        eng.wait_ge(m_posed, 2 * g)
                    flat = normed.rearrange("p t (h n) -> p (t h) n", n=HD)
                    src = heads.rearrange("p t (h n) -> p (t h) n", n=HD)
                    link(eng.tensor_tensor(flat, src, src, ALU.mult))
                    link(eng.tensor_reduce(hms[:, :], flat, AX.X, ALU.add))
                    eng.tensor_scalar(hms[:, :], hms[:, :], 1.0 / HD, EPS, ALU.mult, ALU.add).then_inc(hms_ready, 1)
                    eng.wait_ge(hsd_ready, g + 1)
                    link(eng.reciprocal(hrs[:, :], hsd[:, :]))
                    eng.tensor_tensor(flat, src, hrs[:, :].unsqueeze(2).to_broadcast([P, TT * GH, HD]), ALU.mult)\
                       .then_inc(mixed_ready, 1)

            def take_mixed(g, tt):
                src = fin[:, :].rearrange("p (b n) -> p b n", b=4)
                high = u_high[:, 4 * g:4 * g + 4, tt * P:(tt + 1) * P]
                eng.wait_ge(m_scaled, 2 * g + tt + 1)
                eng.tensor_copy(high, src).then_inc(m_high, 1)
                eng.wait_ge(m_high, 2 * g + tt + 1)
                eng.tensor_tensor(u_low[:, 4 * g:4 * g + 4, tt * P:(tt + 1) * P], src, high.bitcast(f32),
                                  ALU.subtract).then_inc(m_low, 1)

            def attention(g, jobs):
                for job, i in jobs:
                    {"z": mask_scores, "mid": take_middle, "out": take_out, "turn": take_mixed}[job](g, i)
                for job, i in jobs:
                    if job == "z":
                        keep_logs(g, i)

            forget_low()
            for n in range(3 * GROUPS):
                g, r = divmod(n, 3)
                for hh in range(HALVES):
                    low_part()
                    if hh in (1, 3) and n % 3:
                        turned_qk(n - 1, hh // 2)
                    if n == 0 and hh == 7:
                        forget_logit()
                        forget_gate()
                    if n == 1 and hh == 5:
                        forget_sums()
                    if g:
                        attention(g - 1, SLOTS.get(r * HALVES + hh, ()))
            t.add("done", 8 * 3 * GROUPS)
            done = t.c["done"]
            for y, (c, j) in enumerate([o for o in OUT_ORDER for _ in range(2)]):
                low_part()
                if j == 3 and y % 2:
                    t.c["done"] = done + y + 1
                    add_step(xs, c, c)
                attention(GROUPS - 1, LAST_SLOTS.get(y, ()))
            norm()
            with t.loop(eng, 0, QUARTERS - 1, low=64, raw=32, t=2 * NC, done=64, squared=TT * NC, summed=NC) as q:
                mlp_body(xs)
            eng.wait_ge(grow_in, 48)
            mlp_body(xs, ahead=False, after=gain)
            mean_square()
            invert()
            eng.wait_ge(final_gained, NC)
            for part in range(2):
                piece = acc[:, 1, part * D // 2:(part + 1) * D // 2]
                eng.tensor_scalar(piece, piece, rstd[:, 1:2], None, ALU.mult).then_inc(final_second, 1)


def shape_constants():
    i, j = np.arange(P)[:, None], np.arange(P)[None, :]
    f = np.float32
    tri = lambda ok: np.where(ok, f(0), f(MASKED))
    zero = np.zeros((P, P), f)
    later, upto = tri(i < j), tri(j <= i)
    consts = np.concatenate([np.eye(P, dtype=f), (i >= j).astype(f), (i <= j).astype(f), np.ones((P, P), f),
                             later, zero, later, upto, zero, upto], axis=1)
    n = np.arange(SEQ)
    angle = 2.0 * np.pi * ((n[:, None] * n[None, :]) % SEQ) / SEQ
    cos, sin = np.cos(angle), np.sin(angle)
    dft = np.concatenate([cos, sin, -sin], axis=1).astype(f)
    select = np.repeat(np.eye(HEADS, dtype=f)[:, :, None], P, axis=2)
    return consts.astype(f), dft, select


def kernel(x, c, ctx, c_ctx, w_mod, b_mod, norm_g, w_mlp_in, w_mlp_out, fnet_w_out, hgrn_w_in, hgrn_lb,
           hgrn_gnorm, hgrn_w_out, diff_w_qkv, diff_lambda, diff_subln, diff_w_out, g_attn_2, w_in_2,
           b_f_2, g_out_sb_2, g_out_fox_2, w_out_2, g_mlp_2, w_up_2, w_down_2, g_final_2):
    import concourse.bacc as bacc
    from concourse.bass_utils import run_bass_kernel_spmd

    consts, dft, select = shape_constants()
    two_d = lambda a: np.ascontiguousarray(np.asarray(a)).reshape(-1, np.asarray(a).shape[-1])
    given = [("x", two_d(x)), ("c", two_d(c)), ("w_mod", two_d(w_mod)), ("b_mod", two_d(b_mod)),
             ("norm_g", two_d(norm_g)), ("w_mlp_in", two_d(w_mlp_in)), ("w_mlp_out", two_d(w_mlp_out)),
             ("fnet_w", two_d(fnet_w_out)), ("g_attn", two_d(g_attn_2)), ("w_in", two_d(w_in_2)),
             ("b_f", two_d(b_f_2)), ("g_out_sb", two_d(g_out_sb_2)), ("g_out_fox", two_d(g_out_fox_2)),
             ("w_out", two_d(w_out_2)), ("g_mlp", two_d(g_mlp_2)), ("w_up", two_d(w_up_2)),
             ("w_down", two_d(w_down_2)), ("g_final", two_d(g_final_2)), ("consts", consts), ("dft", dft),
             ("select", select)]
    nc = bacc.Bacc("TRN2", target_bir_lowering=False, num_devices=1)
    arrays, args = {}, []
    for name, a in given:
        arrays[f"in_{name}"] = a
        args.append(nc.dram_tensor(f"in_{name}", a.shape, mybir.dt.from_np(a.dtype), kind="ExternalInput").ap())
    args.append(nc.dram_tensor("out_x", (SEQ, D), mybir.dt.float32, kind="ExternalOutput").ap())
    program(nc, *args)
    r = run_bass_kernel_spmd(nc, [arrays], core_ids=[0])
    return r.results[0]["out_x"].reshape(1, SEQ, D)
```

```python
from collections import defaultdict
from contextlib import ExitStack, contextmanager

import numpy as np

import concourse.bass as bass
from concourse import mybir

P = 128
SEQ = 256
D = 2048
TT = SEQ // P
KT = D // P
CW = 512
NC = D // CW
HALVES = KT // 2
LEAD = 4
RAW = 4
QUARTERS = 4
HD = 128
HEADS = 8
GH = 4
GROUPS = 4
EPS = 1e-6
GROUP_DIM = 256
FG = D // GROUP_DIM
MASKED = -1e30

C_ID, C_GE, C_LE, C_ONE, C_SB, C_FOX = 0, 128, 256, 384, 512, 896
C_ALL = 1280

V_C, V_G0, V_G2, V_GA, V_GM, V_GO = (KT * i for i in range(6))
V_ALL = 6 * KT

GATE_AHEAD = 15
FNET_AFTER = range(2, 14)
SEQ_AHEAD = 5
GATE_ROWS = 10
SHIFT_AT = GATE_AHEAD + len(FNET_AFTER) - KT
MOD_AFTER = (2, 5, 8, 11, 14, 18, 22, 26)
MOD_LOOPS = KT // len(MOD_AFTER)
TURN_BANKS = (0, 1, 4, 5, 6, 7, 2, 3)

SLOTS = {5: (("z", 0),), 7: (("z", 1), ("mid", 0)), 10: (("z", 2), ("mid", 1), ("out", 0)),
         13: (("z", 3), ("mid", 2), ("out", 1)), 15: (("mid", 3), ("out", 2)), 18: (("out", 3),),
         21: (("turn", 0),), 23: (("turn", 1),)}
LAST_SLOTS = {0: (("z", 0),), 1: (("z", 1),), 2: (("mid", 0),), 3: (("z", 2), ("mid", 1), ("out", 0)),
              5: (("z", 3), ("mid", 2), ("out", 1)), 7: (("mid", 3), ("out", 2)), 8: (("out", 3),),
              10: (("turn", 0), ("turn", 1))}
OUT_ORDER = [(0, 0), (0, 1), (0, 2), (1, 0), (1, 1), (1, 2), (0, 3), (1, 3)] + \
            [(c, j) for c in (2, 3) for j in range(4)]


PLAIN_TURNS = {15: 0, 17: 1, 25: 2}


class Tally:

    def __init__(self):
        self.c = defaultdict(int)
        self.q, self.start, self.per = None, 0, {}

    def at(self, name, d=0):
        v = self.c[name] + d
        per = self.per.get(name, 0)
        return v if self.q is None or per == 0 else self.q * per + (v - self.start * per)

    def add(self, name, k=1):
        self.c[name] += k

    def arrived(self):
        v = 16 * (self.c["raw"] // RAW + 1)
        per = 16 * (self.per.get("raw", 0) // RAW)
        return v if self.q is None or per == 0 else self.q * per + (v - self.start * per)

    @contextmanager
    def loop(self, eng, start, stop, **per):
        before = dict(self.c)
        with eng.Fori(start, stop) as q:
            self.q, self.start, self.per = q, start, per
            yield q
        self.q, self.start, self.per = None, 0, {}
        for name in set(self.c) | set(per):
            one = self.c[name] - before.get(name, 0)
            assert one == per.get(name, 0), (name, one)
            self.c[name] = before.get(name, 0) + one * (stop - start)


def in_column(g, r):
    kind, part = divmod(g, 2)
    return kind * 3 * HEADS * HD + r * HEADS * HD + part * CW


def program(nc, x, c_in, w_mod, b_mod, norm_g, w_mlp_in, w_mlp_out, fnet_w, g_attn, w_in, b_f,
            g_out_sb, g_out_fox, w_out, g_mlp, w_up, w_down, g_final, consts, dft, select, out):
    dt = mybir.dt
    f32, f32r = dt.float32, dt.float32r
    ACT = mybir.ActivationFunctionType
    ALU = mybir.AluOpType
    AX = mybir.AxisListType

    ctx = ExitStack()
    with ctx:
        def sb(name, shape, dtype=f32):
            return ctx.enter_context(nc.sbuf_tensor(name, shape, dtype))

        def sem(name):
            return ctx.enter_context(nc.semaphore(name))

        raw = sb("raw", [P, RAW, 4 * CW])
        w_high = sb("w_high", [P, LEAD, 2 * CW], f32r)
        w_low = sb("w_low", [P, LEAD, 2 * CW], f32r)
        h_both = sb("h_both", [P, KT, 2, SEQ], f32r)
        u_high = sb("u_high", [P, KT, SEQ], f32r)
        u_low = sb("u_low", [P, KT, SEQ], f32r)
        xs = sb("xs", [P, TT, D])
        acc = sb("acc", [P, TT, D])
        grow = sb("grow", [P, D])
        scr = sb("scr", [P, 2 * D])
        extra = sb("extra", [P, 1536])
        junk = sb("junk", [P, CW])
        probs = sb("probs", [P, 2, 384])
        fin = sb("fin", [P, CW])
        cst = sb("cst", [P, C_ALL])
        cols = sb("cols", [P, V_ALL])
        silu_t = sb("silu_t", [P, 2 * KT])
        silu_c = sb("silu_c", [P, KT])
        mcol = sb("mcol", [P, 4 * KT])
        scale1 = sb("scale1", [P, KT])
        scale2 = sb("scale2", [P, KT])
        shift1 = sb("shift1", [P, KT])
        ssq = sb("ssq", [P, TT * NC])
        ms = sb("ms", [P, TT])
        sd = sb("sd", [P, TT])
        rstd = sb("rstd", [P, TT])
        rstd_q = sb("rstd_q", [P, TT])
        wf = sb("wf", [P, KT * HEADS])
        wf_high = sb("wf_high", [P, KT * HEADS], f32r)
        wf_low = sb("wf_low", [P, KT * HEADS], f32r)
        bf = sb("bf", [P, TT * HEADS])
        fl = sb("fl", [P, TT * HEADS])
        fe = sb("fe", [P, TT * HEADS])
        csum = sb("csum", [P, TT * HEADS])
        negmax = sb("negmax", [P, TT * GH])
        psums = sb("psums", [P, TT * GH])
        precip = sb("precip", [P, TT * GH])
        hms = sb("hms", [P, TT * GH])
        hsd = sb("hsd", [P, TT * GH])
        hrs = sb("hrs", [P, TT * GH])
        ps = ctx.enter_context(nc.psum_tensor("ps", [P, 8, CW], f32))

        def lin(n):
            return ps[:, 2 * (n % 2):2 * (n % 2) + 2, :]

        def side(b):
            return ps[:, 4 + b, :]

        ident = cst[:, C_ID:C_ID + P]
        ones = cst[:, C_ONE:C_ONE + P]

        h_high, h_low = h_both[:, :, 0, :], h_both[:, :, 1, :]

        def mod_acc(v):
            return scr[:, 0:D] if v in (1, 3) else scr[:, D:2 * D]

        def seq_dft(g):
            g %= SEQ_AHEAD
            if g < 2:
                return grow[:, g * D // 2:(g + 1) * D // 2].rearrange("p (d n) -> p d n", d=2)
            return acc[:, :, (g - 2) * CW:(g - 1) * CW]

        gated_last = scr[:, 0:TT * CW].rearrange("p (t n) -> p t n", t=TT)
        relu = scr[:, 0:TT * CW].rearrange("p (t n) -> p t n", t=TT)
        hidden = scr[:, TT * CW:2 * TT * CW].rearrange("p (t n) -> p t n", t=TT)
        tables = extra[:, :].rearrange("p (t n) -> p t n", t=2)
        turned = extra[:, 0:2 * CW].rearrange("p (b n) -> p b n", b=2)
        qT = acc[:, 0, :].rearrange("p (b h s) -> p b h s", b=2, h=GH)
        kT = acc[:, 1, :].rearrange("p (b h s) -> p b h s", b=2, h=GH)
        vv = grow[:, :].rearrange("p (b t n) -> p b t n", b=2, t=TT)
        stage = scr[:, 0:TT * CW].rearrange("p (t n) -> p t n", t=TT)
        heads = scr[:, TT * CW:2 * TT * CW].rearrange("p (t n) -> p t n", t=TT)
        normed = scr[:, 2 * TT * CW:3 * TT * CW].rearrange("p (t n) -> p t n", t=TT)
        sel = scr[0:HEADS, 3 * TT * CW:4 * TT * CW].rearrange("p (h n) -> p h n", h=HEADS)
        zs = extra[:, 0:768].rearrange("p (b n) -> p b n", b=2)
        ew = extra[:, 768:1536].rearrange("p (b n) -> p b n", b=2)
        negc = sb("negc", [HEADS, SEQ])

        raw_loaded = [sem(f"raw_loaded{i}") for i in range(RAW)]
        raw_used = sem("raw_used")
        high_ready = sem("high_ready")
        low_first = sem("low_first")
        half_used = sem("half_used")
        x_in, cst_in, dft_in, vec_in = sem("x_in"), sem("cst_in"), sem("dft_in"), sem("vec_in")
        grow_in, mask_in, sel_in = sem("grow_in"), sem("mask_in"), sem("sel_in")
        vec_turned, vec_ready = sem("vec_turned"), sem("vec_ready")
        act_link, vec_link, pool_link = sem("act_link"), sem("vec_link"), sem("pool_link")
        silu_exp = sem("silu_exp")
        acc_init = [sem(f"acc_init{v}") for v in range(6)]
        mod_read = sem("mod_read")
        mod_cols = sem("mod_cols")
        part_summed, part_read, part_cols = sem("part_summed"), sem("part_read"), sem("part_cols")
        squared = sem("squared")
        ms_ready, sd_ready, rstd_ready = sem("ms_ready"), sem("sd_ready"), sem("rstd_ready")
        yn_ready, rstd_q_ready = sem("yn_ready"), sem("rstd_q_ready")
        seq_done, seq_taken = sem("seq_done"), sem("seq_taken")
        scaled, dft_done = sem("scaled"), sem("dft_done")
        dft_high, dft_low = sem("dft_high"), sem("dft_low")
        acc_zero = sem("acc_zero")
        summed = sem("summed")
        up_taken, up_ready = sem("up_taken"), sem("up_ready")
        t_posed, t_high, t_low = sem("t_posed"), sem("t_high"), sem("t_low")
        xn_ready, n_posed = sem("xn_ready"), sem("n_posed")
        n_scaled, n_high, n_low = sem("n_scaled"), sem("n_high"), sem("n_low")
        gated = sem("gated")
        x_updated = sem("x_updated")
        qkv_taken = sem("qkv_taken")
        a_posed, a_turned = sem("a_posed"), sem("a_turned")
        f_raw, f_high, f_low = sem("f_raw"), sem("f_high"), sem("f_low")
        f_rows, f_turned = sem("f_rows"), sem("f_turned")
        f_sum, f_exp, f_logit, f_ready = sem("f_sum"), sem("f_exp"), sem("f_logit"), sem("f_ready")
        c_sum, c_ready = sem("c_sum"), sem("c_ready")
        z_ready, z_taken, z_logs = sem("z_ready"), sem("z_taken"), sem("z_logs")
        mid_in, mid_ready, mid_taken = sem("mid_in"), sem("mid_ready"), sem("mid_taken")
        fox_exp = sem("fox_exp")
        probs_ready = sem("probs_ready")
        o_ready, o_taken = sem("o_ready"), sem("o_taken")
        hms_ready, hsd_ready, mixed_ready = sem("hms_ready"), sem("hsd_ready"), sem("mixed_ready")
        m_posed, m_scaled, m_high, m_low = sem("m_posed"), sem("m_scaled"), sem("m_high"), sem("m_low")
        final_gained = sem("final_gained")
        final_first, final_second, out_done = sem("final_first"), sem("final_second"), sem("out_done")

        block = ctx.enter_context(nc.Block())

        @block.sync
        def _(eng):
            t = Tally()

            def load(src, shape=None):
                slot = t.c["raw"] % RAW
                if t.c["raw"] >= RAW or t.q is not None:
                    eng.wait_ge(raw_used, t.at("raw", 1 - RAW))
                dst = raw[:, slot, :]
                if shape is not None:
                    dst = dst.rearrange("p (k n) -> p k n", k=4)
                eng.dma_start(dst, src).then_inc(raw_loaded[slot], 16)
                t.add("raw")

            def chunk(w, row, col):
                load(w[bass.ds(row, 4 * P), bass.ds(col, CW)].rearrange("(k p) n -> p k n", p=P), 4)

            def mod_tile(unit, kk):
                load(w_mod[bass.ds(kk * P, P), unit * D:(unit + 1) * D])

            for i in range(RAW):
                if i == 2:
                    eng.wait_ge(vec_in, 16 * 8)
                mod_tile(0, i)
            for unit in range(2):
                with t.loop(eng, 1 if unit == 0 else 0, KT // RAW, raw=RAW) as q:
                    for i in range(RAW):
                        mod_tile(unit, q * RAW + i)
            for kk in range(GATE_AHEAD):
                mod_tile(2, kk)
            behind = [(2, kk) for kk in range(GATE_AHEAD, KT)] + [(3, kk) for kk in range(SHIFT_AT)]
            for ch in range(4 * NC):
                chunk(fnet_w, ch % 4 * 4 * P, ch // 4 * CW)
                if ch in FNET_AFTER:
                    mod_tile(*behind[ch - FNET_AFTER[0]])
            for kk in range(SHIFT_AT, KT):
                mod_tile(3, kk)
            with t.loop(eng, 0, KT // RAW, raw=RAW) as q:
                for i in range(RAW):
                    mod_tile(4, q * RAW + i)

            def mlp_chunk(w1, w2, q, ch):
                step, j = divmod(ch, 4)
                if step < NC:
                    chunk(w1, j * 4 * P, q * D + step * CW)
                else:
                    chunk(w2, q * D + j * 4 * P, (step - NC) * CW)

            chunk(w_mlp_in, 0, 0)
            chunk(w_mlp_in, 4 * P, 0)

            with t.loop(eng, 0, MOD_LOOPS, raw=32 + len(MOD_AFTER)) as q:
                for pos in range(32):
                    if pos < 30:
                        mlp_chunk(w_mlp_in, w_mlp_out, q, pos + 2)
                    else:
                        chunk(w_mlp_in, (pos - 30) * 4 * P, (q + 1) * D)
                    if pos in MOD_AFTER:
                        mod_tile(5, q * len(MOD_AFTER) + MOD_AFTER.index(pos))
            for q in range(MOD_LOOPS, QUARTERS):
                for ch in range(2, 32):
                    mlp_chunk(w_mlp_in, w_mlp_out, q, ch)
                for j in range(2):
                    if q < QUARTERS - 1:
                        chunk(w_mlp_in, j * 4 * P, (q + 1) * D)
                    else:
                        chunk(w_in, j * 4 * P, in_column(0, 0))
            for g in range(GROUPS):
                for r in range(3):
                    for j in range(2 if g == r == 0 else 0, 4):
                        chunk(w_in, j * 4 * P, in_column(g, r))
            for c, j in OUT_ORDER:
                chunk(w_out, j * 4 * P, c * CW)
            chunk(w_up, 0, 0)
            chunk(w_up, 4 * P, 0)
            with t.loop(eng, 0, QUARTERS - 1, raw=32) as q:
                for ch in range(2, 32):
                    mlp_chunk(w_up, w_down, q, ch)
                for j in range(2):
                    chunk(w_up, j * 4 * P, (q + 1) * D)
            for ch in range(2, 32):
                mlp_chunk(w_up, w_down, QUARTERS - 1, ch)
            outv = out.rearrange("(t p) n -> p t n", p=P)
            for part in range(2):
                piece = slice(part * D // 2, (part + 1) * D // 2)
                for tt, ready in ((1, final_second), (0, final_first)):
                    eng.wait_ge(ready, part + 1)
                    eng.dma_start(outv[:, tt, piece], acc[:, tt, piece]).then_inc(out_done, 16)
            eng.wait_ge(out_done, 16 * 4)

        @block.gpsimd
        def _(eng):
            for v in range(6):
                if v >= 2:
                    eng.wait_ge(mod_read, v if v == 5 else v - 1)
                eng.memset(mod_acc(v), 0.0).then_inc(pool_link, 1)
                eng.wait_ge(pool_link, v + 1)
                eng.dma_start(mod_acc(v)[0:1, :], b_mod[0:1, v * D:(v + 1) * D]).then_inc(acc_init[v], 16)
                if v == 3:
                    eng.wait_ge(dft_done, FG)
                    eng.dma_start(grow[:, :], norm_g[1:2, :].broadcast_to([P, D])).then_inc(grow_in, 16)
            eng.wait_ge(x_updated, TT * NC)
            eng.dma_start(grow[:, :], norm_g[3:4, :].broadcast_to([P, D])).then_inc(grow_in, 16)
            eng.dma_start(cst[:, C_SB:C_ALL], consts[:, C_SB:C_ALL]).then_inc(mask_in, 16)
            eng.dma_start(wf[:, :].rearrange("p (k n) -> p k n", k=KT),
                          w_in[:, 6 * HEADS * HD:6 * HEADS * HD + HEADS]
                          .rearrange("(k p) n -> p k n", p=P)).then_inc(f_raw, 16)
            for tt in range(TT):
                eng.dma_start(bf[:, tt * HEADS:(tt + 1) * HEADS], b_f.broadcast_to([P, HEADS])).then_inc(f_raw, 16)
            eng.wait_ge(n_posed, TT * NC)
            eng.memset(acc[:, :, :], 0.0).then_inc(acc_zero, 1)
            eng.wait_ge(mod_read, 6)
            eng.wait_ge(n_posed, 2 * TT * NC)
            eng.dma_start(sel, select).then_inc(sel_in, 16)
            eng.wait_ge(o_ready, GROUPS * GH)
            eng.dma_start(grow[:, :], g_final.broadcast_to([P, D])).then_inc(grow_in, 16)

        @block.tensor
        def _(eng):
            t = Tally()

            def half(n, hh, high, low):
                slot = t.c["half"] % LEAD
                if t.c["half"] % 2 == 0:
                    t.add("chunk")
                    eng.wait_ge(low_first, t.at("chunk", 0))
                else:
                    t.add("raw")
                    eng.wait_ge(raw_used, t.at("raw", 0))
                for tt in range(TT):
                    for kk in range(2):
                        k = 2 * hh + kk
                        wh = w_high[:, slot, kk * CW:(kk + 1) * CW]
                        wl = w_low[:, slot, kk * CW:(kk + 1) * CW]
                        ah = high[:, k, tt * P:(tt + 1) * P]
                        al = low[:, k, tt * P:(tt + 1) * P]
                        dst = lin(n)[:, tt, :]
                        eng.matmul(dst, ah, wh, start=(k == 0), stop=False)
                        eng.matmul(dst, ah, wl, start=False, stop=False)
                        last = eng.matmul(dst, al, wh, start=False, stop=(k == KT - 1))
                last.then_inc(half_used, 1)
                t.add("half")

            def sum_partitions_to_columns(v, place):
                if place:
                    eng.wait_ge(mod_cols, t.c["mod_cols"])
                for j in range(KT):
                    last = eng.matmul(ps[:, 3, place * KT + j:place * KT + j + 1],
                                      mod_acc(v)[:, j * P:(j + 1) * P], ones[:, 0:1], start=True, stop=True)
                last.then_inc(mod_read, 1)
                t.add("mod_cols")

            def sum_scale_2_by_quarters():
                for part in range(4):
                    if part < 3:
                        eng.wait_ge(part_summed, part + 1)
                    else:
                        eng.wait_ge(raw_used, t.c["raw"])
                    for j in range(4 * part, 4 * part + 4):
                        last = eng.matmul(ps[:, TURN_BANKS[4 + part], j:j + 1],
                                          mod_acc(4)[:, j * P:(j + 1) * P], ones[:, 0:1], start=True, stop=True)
                    last.then_inc(part_read if part < 3 else mod_read, 1)
                t.add("mod_cols")

            def sum_partitions_to_rows(v):
                for j in range(NC):
                    last = eng.matmul(side(j), ones, mod_acc(v)[:, j * CW:(j + 1) * CW], start=True, stop=True)
                last.then_inc(mod_read, 1)
                t.add("mod_cols")

            def turn(dst, src):
                for b in range(4):
                    last = eng.transpose(dst[:, b * P:(b + 1) * P], src[:, b * P:(b + 1) * P], ident)
                return last

            def norm_turn(first, stop):
                for i in range(first, stop):
                    j, tt = divmod(i, TT)
                    t.add("norm")
                    eng.wait_ge(xn_ready, t.c["norm"])
                    turn(ps[:, TURN_BANKS[i], :], acc[:, tt, j * CW:(j + 1) * CW]).then_inc(n_posed, 1)

            def plain_turn(first, stop):
                for i in range(first, stop):
                    j, tt = divmod(i, TT)
                    t.add("norm")
                    if t.c["norm"] > TT * NC + 4:
                        eng.wait_ge(n_scaled, t.c["norm"] - 4)
                    turn(side(i % 4), xs[:, tt, j * CW:(j + 1) * CW]).then_inc(n_posed, 1)

            def h_ready(hh):
                if hh % 2 == 0:
                    eng.wait_ge(n_low, t.c["stage"] + 2 + hh)

            def turn_hidden(tt, mods_read):
                if tt == 0:
                    eng.wait_ge(up_ready, t.at("up", 0))
                if t.c["t"] % (2 * NC):
                    eng.wait_ge(t_low, t.at("t", 0))
                elif mods_read:
                    eng.wait_ge(mod_cols, mods_read)
                turn(side(0), hidden[:, tt, :]).then_inc(t_posed, 1)
                t.add("t")

            def mlp(start, stop, mods=(), mods_read=0):
                def step(n, c, high, low, first):
                    for hh in range(HALVES):
                        first(hh)
                        half(n, hh, high, low)
                        if t.c["half"] % 2 == 0 and (4 * n + hh // 2) - 2 in mods:
                            t.add("raw")
                        if 1 <= n <= NC and hh in (1, 3):
                            turn_hidden(hh // 2, mods_read)

                with t.loop(eng, start, stop, half=64, chunk=32, raw=32 + len(mods), summed=NC, up=NC, t=2 * NC):
                    for c in range(NC):
                        if c < 2:
                            eng.wait_ge(summed, t.at("summed", c - 1))
                        else:
                            eng.wait_ge(up_taken, t.at("up", -1))
                        step(c, c, h_high, h_low, h_ready if c == 0 else lambda hh: None)
                        t.add("up")
                    for c in range(NC):
                        if c < 2:
                            eng.wait_ge(up_taken, t.at("up", c - 1))
                        else:
                            eng.wait_ge(summed, t.at("summed", -1))

                        def hidden_ready(hh):
                            if c == 0 and hh % 2 == 0:
                                eng.wait_ge(t_low, t.at("t", hh + 2 - 2 * NC) if hh < 6 else t.at("t", 0))

                        step(NC + c, c, u_high, u_low, hidden_ready)
                        t.add("summed")

            eng.wait_ge(vec_in, 16 * 8)
            eng.transpose(side(0)[:, 0:V_ALL], junk[0:V_ALL, 0:P], cst[0:V_ALL, C_ID:C_ID + V_ALL])\
               .then_inc(vec_turned, 1)
            eng.wait_ge(cst_in, 16)
            eng.wait_ge(yn_ready, TT)
            eng.wait_ge(dft_in, 16)

            def over_sequence(g):
                for d in range(2):
                    k = 2 * g + d
                    for tt in range(TT):
                        last = eng.matmul(side(2 * (g % 2) + d), acc[:, tt, k * P:(k + 1) * P],
                                          tables[:, tt, 0:2 * SEQ], start=(tt == 0), stop=(tt == 1))
                last.then_inc(seq_done, 1)

            for g in range(SEQ_AHEAD + 2):
                if g >= 2:
                    eng.wait_ge(seq_taken, g - 1)
                over_sequence(g)
            for v in range(2):
                t.add("raw", KT)
                eng.wait_ge(raw_used, t.c["raw"])
                sum_partitions_to_columns(v, v)
            for g in range(FG):
                eng.wait_ge(scaled, g + 1)
                if g == FG - 3:
                    over_sequence(FG - 1)
                if g >= 2:
                    eng.wait_ge(dft_low, g - 1)
                for e in range(2):
                    dst = lin(g)[:, 0, e * SEQ:(e + 1) * SEQ]
                    for d in range(2):
                        eng.matmul(dst, tables[:, d, e * P:(e + 1) * P], seq_dft(g)[:, d, 0:SEQ],
                                   start=(d == 0), stop=False)
                        last = eng.matmul(dst, tables[:, d, 2 * SEQ + e * P:2 * SEQ + (e + 1) * P],
                                          seq_dft(g)[:, d, SEQ:2 * SEQ], start=False, stop=(d == 1))
                last.then_inc(dft_done, 1)
            eng.wait_ge(dft_low, FG)
            t.add("raw", GATE_AHEAD)
            for c in range(NC):
                if c >= 2:
                    eng.wait_ge(summed, c - 1)
                for hh in range(HALVES):
                    half(c, hh, h_high, h_low)
                    ch = 4 * c + hh // 2
                    if hh % 2 and ch in FNET_AFTER:
                        t.add("raw")
                    if hh % 2 and ch == GATE_ROWS:
                        sum_partitions_to_rows(2)
                t.add("summed")
            t.add("raw", KT - SHIFT_AT)
            eng.wait_ge(raw_used, t.c["raw"])
            eng.wait_ge(summed, NC)
            sum_partitions_to_columns(3, 2)
            norm_turn(0, 4)
            eng.wait_ge(mod_cols, 4)
            t.add("raw", KT)
            sum_scale_2_by_quarters()
            for i in range(4, 8):
                if i < 7:
                    eng.wait_ge(part_cols, i - 3)
                else:
                    eng.wait_ge(mod_cols, 5)
                norm_turn(i, i + 1)
            mlp(0, MOD_LOOPS, MOD_AFTER)
            sum_partitions_to_rows(5)
            mlp(MOD_LOOPS, QUARTERS, mods_read=6)
            t.add("stage", TT * NC)

            def turn_updated(first, stop):
                for i in range(first, stop):
                    eng.wait_ge(x_updated, TT * NC + i + 1)
                    plain_turn(i, i + 1)

            turn_updated(0, 4)

            def forget_logits():
                eng.wait_ge(f_low, 1)
                for k in range(KT):
                    piece = slice(k * HEADS, (k + 1) * HEADS)
                    both = h_both[:, k, :, :].rearrange("p e s -> p (e s)")
                    eng.matmul(side(2)[0:HEADS, :], wf_high[:, piece], both, start=(k == 0), stop=False)
                    last = eng.matmul(side(2)[0:HEADS, 0:SEQ], wf_low[:, piece], h_high[:, k, :],
                                      start=False, stop=(k == KT - 1))
                last.then_inc(f_sum, 1)

            def forget_turn():
                eng.wait_ge(f_rows, 1)
                for tt in range(TT):
                    last = eng.transpose(side(3)[:, tt * HEADS:(tt + 1) * HEADS], negc[:, tt * P:(tt + 1) * P],
                                         cst[0:HEADS, C_ID:C_ID + HEADS])
                last.then_inc(f_turned, 1)

            def forget_sums():
                eng.wait_ge(f_ready, 1)
                lf = [fl[:, tt * HEADS:(tt + 1) * HEADS] for tt in range(TT)]
                le, one = cst[:, C_LE:C_LE + P], ones
                eng.matmul(side(3)[0:HEADS, 0:SEQ], lf[0], cst[:, C_LE:C_LE + SEQ], start=True, stop=False)
                eng.matmul(side(3)[0:HEADS, P:SEQ], lf[1], le, start=False, stop=True)
                col = side(3)[:, SEQ:SEQ + 2 * HEADS]
                eng.matmul(col[:, 0:HEADS], le, lf[0], start=True, stop=True)
                eng.matmul(col[:, HEADS:2 * HEADS], one, lf[0], start=True, stop=False)
                eng.matmul(col[:, HEADS:2 * HEADS], le, lf[1], start=False, stop=True).then_inc(c_sum, 1)

            def scores(g, i):
                n = t.c["z"]
                q_h, k_h = qT[:, g % 2, i, :], kT[:, g % 2, i, :]
                eng.wait_ge(a_turned, 4 * (g + 1))
                if n:
                    eng.wait_ge(z_taken, n)
                bank = side(1)
                if g < 2:
                    eng.matmul(bank[:, 0:SEQ], k_h[:, 0:P], q_h, start=True, stop=True)
                    eng.matmul(bank[:, SEQ:384], k_h[:, P:SEQ], q_h[:, P:SEQ], start=True, stop=True)\
                       .then_inc(z_ready, 1)
                else:
                    if g == 2 and i == 0:
                        eng.wait_ge(c_ready, 1)
                        eng.wait_ge(sel_in, 16)
                    s_h = sel[:, GH * (g - 2) + i, :]
                    eng.matmul(bank[:, 0:P], q_h[:, 0:P], k_h[:, 0:P], start=True, stop=False)
                    eng.matmul(bank[:, 0:P], s_h, negc[:, 0:P], start=False, stop=True)
                    eng.matmul(bank[:, P:384], q_h[:, P:SEQ], k_h, start=True, stop=False)
                    eng.matmul(bank[:, P:384], s_h, negc[:, :], start=False, stop=True)\
                       .then_inc(z_ready, 1)
                t.add("z")

            def middle(g, i):
                n = t.c["mid"]
                e = ew[:, n % 2, :]
                if n:
                    eng.wait_ge(mid_taken, n) if g < 2 or n == 2 * GH else eng.wait_ge(probs_ready, n)
                bank = side(2)
                if g < 2:
                    eng.wait_ge(mid_in, n + 1)
                    eng.matmul(bank[:, 0:384], cst[:, C_GE:C_GE + P], e, start=True, stop=False)
                    eng.matmul(bank[:, P:SEQ], ones, e[:, SEQ:384], start=False, stop=True)\
                       .then_inc(mid_ready, 1)
                else:
                    eng.wait_ge(fox_exp, n + 1 - 2 * GH)
                    for b in range(3):
                        last = eng.transpose(bank[:, b * P:(b + 1) * P], e[:, b * P:(b + 1) * P], ident)
                    last.then_inc(mid_ready, 1)
                t.add("mid")

            def weigh_values(g, i):
                n = t.c["o"]
                a = probs[:, n % 2, :]
                v_h = [vv[:, g % 2, tt, i * HD:(i + 1) * HD] for tt in range(TT)]
                eng.wait_ge(probs_ready, n + 1)
                if n == 0 or i == 0:
                    eng.wait_ge(qkv_taken, 3 * (g + 1))
                if n:
                    eng.wait_ge(o_taken, n)
                else:
                    eng.wait_ge(c_ready, 1)
                eng.matmul(side(3)[:, 0:HD], a[:, 0:P], v_h[0], start=True, stop=True)
                eng.matmul(side(3)[:, HD:2 * HD], a[:, P:SEQ], v_h[0], start=True, stop=False)
                eng.matmul(side(3)[:, HD:2 * HD], a[:, SEQ:384], v_h[1], start=False, stop=True)\
                   .then_inc(o_ready, 1)
                t.add("o")

            def turn_mixed(g, tt):
                if tt == 0:
                    eng.wait_ge(mixed_ready, g + 1)
                    eng.wait_ge(a_turned, min(4 * (g + 2), 4 * GROUPS))
                else:
                    eng.wait_ge(m_scaled, 2 * g + 1)
                turn(side(0), normed[:, tt, :]).then_inc(m_posed, 1)

            def attention(g, jobs):
                for job, i in jobs:
                    {"z": scores, "mid": middle, "out": weigh_values, "turn": turn_mixed}[job](g, i)

            def turn_qk(n, tt):
                g, r = divmod(n, 3)
                done = 4 * g + 2 * r + tt
                if tt == 0:
                    eng.wait_ge(qkv_taken, n + 1)
                if done:
                    eng.wait_ge(a_turned, done)
                if r == 0 and tt == 0 and g >= 2:
                    eng.wait_ge(m_scaled, 2 * (g - 1))
                turn(side(0), stage[:, tt, :]).then_inc(a_posed, 1)

            for n in range(3 * GROUPS):
                if n < 2:
                    eng.wait_ge(summed, t.c["summed"] - 1 + n)
                else:
                    eng.wait_ge(qkv_taken, n - 1)
                g, r = divmod(n, 3)
                for hh in range(HALVES):
                    if n == 0:
                        h_ready(hh)
                    half(n, hh, h_high, h_low)
                    if n == 0 and hh < 2:
                        turn_updated(2 * hh + 4, 2 * hh + 6)
                    if hh in (1, 3) and n % 3:
                        turn_qk(n - 1, hh // 2)
                    if n == 0 and hh == 7:
                        forget_logits()
                    if n == 1 and hh == 4:
                        forget_turn()
                    if n == 2 and hh == 4:
                        forget_sums()
                    if g:
                        attention(g - 1, SLOTS.get(r * HALVES + hh, ()))
            for y, (c, j) in enumerate([o for o in OUT_ORDER for _ in range(2)]):
                hh = 2 * j + y % 2
                if hh == 0:
                    if c < 2:
                        eng.wait_ge(qkv_taken, 3 * GROUPS - 1 + c)
                    else:
                        eng.wait_ge(summed, t.c["summed"] - 1)
                if y % 2 == 0 and (y < 6 or j == 3):
                    eng.wait_ge(m_low, 2 * (j + 1))
                half(c, hh, u_high, u_low)
                if hh == 7:
                    t.add("summed")
                attention(GROUPS - 1, LAST_SLOTS.get(y, ()))
                if y in PLAIN_TURNS:
                    j = PLAIN_TURNS[y]
                    eng.wait_ge(summed, t.c["summed"] - (y == 15))
                    if j == 0:
                        eng.wait_ge(o_taken, GROUPS * GH)
                        eng.wait_ge(m_scaled, TT * GROUPS)
                    plain_turn(TT * j, TT * j + TT)
            eng.wait_ge(summed, t.c["summed"])
            plain_turn(TT * (NC - 1), TT * NC)
            t.add("stage", TT * NC)
            mlp(0, QUARTERS)

        @block.scalar
        def _(eng):
            t = Tally()

            def link(ins):
                ins.then_inc(act_link, 1)
                t.add("link")
                eng.wait_ge(act_link, t.at("link", 0))

            def high_part():
                h = t.c["high"]
                slot = t.c["raw"] % RAW
                if h % 2 == 0:
                    eng.wait_ge(raw_loaded[slot], t.arrived())
                if h >= LEAD or t.q is not None:
                    eng.wait_ge(half_used, t.at("high", 1 - LEAD))
                eng.activation(w_high[:, h % LEAD, :], raw[:, slot, (h % 2) * 2 * CW:(h % 2 + 1) * 2 * CW],
                               ACT.Copy).then_inc(high_ready, 1)
                t.add("high")
                if h % 2:
                    t.add("raw")

            def square_sum(src, column):
                if t.c["squared"] or t.q is not None:
                    eng.wait_ge(squared, t.at("squared", 0))
                t.add("squared")
                eng.activation(junk[:, :], src, ACT.Square, accum_out=ssq[:, column:column + 1])\
                   .then_inc(squared, 1)

            def step_squares(target, c, done):
                eng.wait_ge(summed, done)
                for tt in range(TT):
                    square_sum(target[:, tt, c * CW:(c + 1) * CW], tt * NC + c)

            def root():
                t.add("root")
                eng.wait_ge(ms_ready, t.c["root"])
                eng.activation(sd[:, :], ms[:, :], ACT.Sqrt).then_inc(sd_ready, 1)

            def square_updated(i):
                j, tt = divmod(i, TT)
                square_sum(xs[:, tt, j * CW:(j + 1) * CW], tt * NC + j)

            def scale_turned(i, scale, shift):
                j = i // TT
                t.add("norm")
                eng.wait_ge(n_posed, t.c["norm"])
                if t.c["norm"] > 2:
                    eng.wait_ge(n_low, t.c["norm"] - 2)
                for b in range(4):
                    k = 4 * j + b
                    bank = TURN_BANKS[i] if shift is not None else 4 + i % 4
                    src, dst = ps[:, bank, b * P:(b + 1) * P], turned[:, i % 2, b * P:(b + 1) * P]
                    if shift is None:
                        last = eng.activation(dst, src, ACT.Copy, scale=scale[:, k:k + 1])
                    else:
                        last = eng.activation(dst, src, ACT.Identity, scale=scale[:, k:k + 1],
                                              bias=shift[:, k:k + 1])
                last.then_inc(n_scaled, 1)

            def residual_squares():
                for i in range(TT * NC):
                    eng.wait_ge(x_updated, i + 1)
                    square_updated(i)

            def mlp_body(target, mods=(), ahead=True, scaled=False):
                for y in range(64):
                    if y < 60 or ahead:
                        high_part()
                        if t.c["high"] % 2 == 0 and (y // 2) in mods:
                            t.add("raw")
                    c, hh = divmod(y, HALVES)
                    if 1 <= c <= NC and hh in (1, 3):
                        tt = hh // 2
                        t.add("t")
                        eng.wait_ge(t_posed, t.at("t", 0))
                        eng.activation(u_high[:, 4 * (c - 1):4 * c, tt * P:(tt + 1) * P],
                                       side(0).rearrange("p (b n) -> p b n", b=4), ACT.Copy).then_inc(t_high, 1)
                    if hh == 7:
                        t.add("done", 8)
                        eng.wait_ge(half_used, t.at("done", 0))
                        if c < NC:
                            t.add("up")
                            if scaled:
                                for tt in range(TT):
                                    last = eng.activation(relu[:, tt, :], lin(c)[:, tt, :], ACT.Relu,
                                                          scale=rstd[:, tt:tt + 1])
                                last.then_inc(up_taken, 1)
                            else:
                                eng.activation(relu, lin(c), ACT.Relu).then_inc(up_taken, 1)
                            eng.wait_ge(up_taken, t.at("up", 0))
                            eng.activation(hidden, relu, ACT.Square).then_inc(up_ready, 1)
                        else:
                            t.add("summed")
                            step_squares(target, c - NC, t.at("summed", 0))

            eng.dma_start(ident, consts[:, C_ID:C_ID + P]).then_inc(vec_in, 16)
            for src, row, rows in ((c_in, V_C, KT), (norm_g[0:1, :], V_G0, KT), (norm_g[2:3, :], V_G2, KT),
                                   (g_attn, V_GA, KT), (g_mlp, V_GM, KT), (g_out_sb, V_GO, HEADS),
                                   (g_out_fox, V_GO + HEADS, HEADS)):
                eng.dma_start(junk[row:row + rows, 0:P], src.rearrange("o (r n) -> (o r) n", n=P))\
                   .then_inc(vec_in, 16)
            eng.dma_start(cst[:, C_GE:C_SB], consts[:, C_GE:C_SB]).then_inc(cst_in, 16)
            eng.dma_start(xs[:, :, :], x.rearrange("(t p) n -> p t n", p=P)).then_inc(x_in, 16)
            eng.dma_start(extra[:, :].rearrange("p (t n) -> p t n", t=TT), dft.rearrange("(t p) n -> p t n", p=P))\
               .then_inc(dft_in, 16)
            eng.wait_ge(vec_ready, 1)
            eng.activation(silu_t[:, 0:KT], cols[:, V_C:V_C + KT], ACT.Exp, scale=-1.0).then_inc(silu_exp, 1)
            eng.wait_ge(x_in, 16)
            for i in range(TT * NC):
                tt, j = divmod(i, NC)
                square_sum(xs[:, tt, j * CW:(j + 1) * CW], i)
            root()
            eng.wait_ge(rstd_ready, 1)
            for tt in range(TT):
                eng.activation(acc[:, tt, :], xs[:, tt, :], ACT.Copy, scale=rstd[:, tt:tt + 1])\
                   .then_inc(yn_ready, 1)
            for g in range(SEQ_AHEAD):
                eng.wait_ge(seq_done, g + 1 if g < SEQ_AHEAD - 1 else g + 2)
                for d in range(2):
                    last = eng.activation(seq_dft(g)[:, d, :], side(2 * (g % 2) + d), ACT.Copy)
                last.then_inc(seq_taken, 1)
            eng.wait_ge(seq_taken, SEQ_AHEAD)
            eng.wait_ge(mod_cols, 2)

            def scale_and_shift(g):
                if g >= SEQ_AHEAD:
                    eng.wait_ge(seq_done, g + 1)
                    eng.wait_ge(dft_done, g - SEQ_AHEAD + 1)
                for d in range(2):
                    k = 2 * g + d
                    dst = seq_dft(g)[:, d, :]
                    ins = eng.activation(dst, dst if g < SEQ_AHEAD else side(2 * (g % 2) + d), ACT.Copy,
                                         scale=scale1[:, k:k + 1])
                link(ins)
                for d in range(2):
                    k = 2 * g + d
                    at0 = seq_dft(g)[:, d, 0:1]
                    last = eng.activation(at0, at0, ACT.Identity, bias=shift1[:, k:k + 1])
                last.then_inc(scaled, 1)

            scale_and_shift(0)
            for g in range(FG):
                if g + 1 < FG:
                    scale_and_shift(g + 1)
                eng.wait_ge(dft_done, g + 1)
                eng.activation(h_high[:, 2 * g:2 * g + 2, :],
                               lin(g)[:, 0, :].rearrange("p (e s) -> p e s", e=2), ACT.Copy).then_inc(dft_high, 1)
            t.add("raw", 2 * KT + GATE_AHEAD)

            def fnet_high():
                high_part()
                if t.c["high"] % 2 == 0 and t.c["high"] // 2 - 1 in FNET_AFTER:
                    t.add("raw")

            for _ in range(LEAD):
                fnet_high()
            for y in range(NC * HALVES):
                if y < NC * HALVES - LEAD:
                    fnet_high()
                if y % HALVES == 7:
                    t.add("done", 8)
                    t.add("summed")
                    step_squares(acc, y // HALVES, t.c["summed"])
            t.add("raw", KT - SHIFT_AT + KT)
            root()
            residual_squares()
            root()
            eng.wait_ge(mod_cols, 4)
            for i in range(TT * NC):
                if i % 2 == 0:
                    eng.wait_ge(part_cols, i // 2 + 1) if i < 6 else eng.wait_ge(mod_cols, 5)
                scale_turned(i, scale2, mcol[:, 2 * KT:3 * KT])
                if i % 2:
                    high_part()
            with t.loop(eng, 0, MOD_LOOPS, high=64, raw=32 + len(MOD_AFTER), t=2 * NC, done=64, up=NC, summed=NC,
                        squared=TT * NC):
                mlp_body(acc, MOD_AFTER)
            for q in range(MOD_LOOPS, QUARTERS):
                mlp_body(acc)
            root()
            for i in range(TT * NC):
                scale_turned(i, cols[:, V_GA:V_GA + KT], None)

            def take_qkv(n):
                g, r = divmod(n, 3)
                t.add("done", 8)
                eng.wait_ge(half_used, t.c["done"])
                if r < 2:
                    if n:
                        eng.wait_ge(a_posed, 4 * g + 2 * r)
                    if n == 0:
                        eng.wait_ge(rstd_q_ready, 1)
                    dst, scale = stage, rstd_q if r == 0 else rstd
                else:
                    if g >= 2:
                        eng.wait_ge(o_ready, GH * (g - 1))
                    dst, scale = vv[:, g % 2, :, :], rstd
                for tt in range(TT):
                    last = eng.activation(dst[:, tt, :], lin(n)[:, tt, :], ACT.Copy, scale=scale[:, tt:tt + 1])
                last.then_inc(qkv_taken, 1)

            def forget_high():
                eng.wait_ge(f_raw, 48)
                eng.activation(wf_high[:, :], wf[:, :], ACT.Copy).then_inc(f_high, 1)

            def forget_gate():
                eng.wait_ge(f_logit, 1)
                link(eng.activation(fe[:, :], fl[:, :], ACT.Abs))
                link(eng.activation(fe[:, :], fe[:, :], ACT.Exp, scale=-1.0))
                eng.activation(fe[:, :], fe[:, :], ACT.Ln, bias=1.0).then_inc(f_exp, 1)

            def score_logs(g, i):
                n = t.c["z"]
                t.add("z")
                z, e = zs[:, n % 2, :], ew[:, n % 2, :]
                eng.wait_ge(z_taken, n + 1)
                if g < 2:
                    link(eng.activation(e, z, ACT.Abs))
                    link(eng.activation(e, e, ACT.Exp, scale=-1.0))
                    eng.activation(e, e, ACT.Ln, bias=1.0).then_inc(z_logs, 1)
                else:
                    eng.wait_ge(mid_in, n + 1)
                    for tt, (a, b) in enumerate(((0, P), (P, 384))):
                        last = eng.activation(e[:, a:b], z[:, a:b], ACT.Exp,
                                              bias=negmax[:, tt * GH + i:tt * GH + i + 1],
                                              accum_out=psums[:, tt * GH + i:tt * GH + i + 1])
                    last.then_inc(fox_exp, 1)

            def take_middle(g, i):
                n = t.c["mid"]
                t.add("mid")
                if n >= 2:
                    eng.wait_ge(o_ready, n - 1)
                if g < 2:
                    eng.wait_ge(mid_taken, n + 1)
                    eng.activation(probs[:, n % 2, :], ew[:, n % 2, :], ACT.Exp).then_inc(probs_ready, 1)
                else:
                    eng.wait_ge(mid_ready, n + 1)
                    eng.activation(probs[:, n % 2, :], side(2)[:, 0:384], ACT.Copy).then_inc(probs_ready, 1)

            def head_root(g, i):
                if i == 3:
                    eng.wait_ge(hms_ready, g + 1)
                    eng.activation(hsd[:, :], hms[:, :], ACT.Sqrt).then_inc(hsd_ready, 1)

            def take_mixed(g, tt):
                eng.wait_ge(m_posed, 2 * g + tt + 1)
                if 2 * g + tt:
                    eng.wait_ge(m_low, 2 * g + tt)
                for b in range(4):
                    k = V_GO + 4 * g + b
                    last = eng.activation(fin[:, b * P:(b + 1) * P], side(0)[:, b * P:(b + 1) * P],
                                          ACT.Copy, scale=cols[:, k:k + 1])
                last.then_inc(m_scaled, 1)

            def attention(g, jobs):
                for job, i in jobs:
                    {"z": score_logs, "mid": take_middle, "out": head_root, "turn": take_mixed}[job](g, i)

            forget_high()
            for n in range(3 * GROUPS):
                g, r = divmod(n, 3)
                for hh in range(HALVES):
                    high_part()
                    if n == 0 and hh < 4:
                        if hh == 0:
                            eng.wait_ge(x_updated, 2 * TT * NC)
                        square_updated(2 * hh)
                        square_updated(2 * hh + 1)
                    if n == 0 and hh == 5:
                        root()
                    if hh == 7:
                        take_qkv(n)
                    if n == 1 and hh == 6:
                        forget_gate()
                    if g:
                        attention(g - 1, SLOTS.get(r * HALVES + hh, ()))
            for y, (c, j) in enumerate([o for o in OUT_ORDER for _ in range(2)]):
                high_part()
                if j == 3 and y % 2:
                    t.add("summed")
                    step_squares(xs, c, t.c["summed"])
                attention(GROUPS - 1, LAST_SLOTS.get(y, ()))
                if y in PLAIN_TURNS:
                    for tt in range(TT):
                        scale_turned(TT * PLAIN_TURNS[y] + tt, cols[:, V_GM:V_GM + KT], None)
            t.add("done", 8 * NC)
            for tt in range(TT):
                scale_turned(TT * (NC - 1) + tt, cols[:, V_GM:V_GM + KT], None)
            root()
            eng.wait_ge(rstd_ready, t.c["root"])
            with t.loop(eng, 0, QUARTERS - 1, high=64, raw=32, t=2 * NC, done=64, up=NC, summed=NC,
                        squared=TT * NC):
                mlp_body(xs, scaled=True)
            mlp_body(xs, ahead=False, scaled=True)
            root()
            eng.wait_ge(rstd_ready, t.c["root"])
            eng.wait_ge(final_gained, NC)
            for part in range(2):
                piece = acc[:, 0, part * D // 2:(part + 1) * D // 2]
                eng.activation(piece, piece, ACT.Copy, scale=rstd[:, 0:1]).then_inc(final_first, 1)

        @block.vector
        def _(eng):
            t = Tally()

            def link(ins):
                ins.then_inc(vec_link, 1)
                t.add("link")
                eng.wait_ge(vec_link, t.at("link", 0))

            def low_part():
                h = t.c["low"]
                slot = t.c["raw"] % RAW
                piece = slice((h % 2) * 2 * CW, (h % 2 + 1) * 2 * CW)
                eng.wait_ge(high_ready, t.at("low", 1))
                eng.tensor_tensor(w_low[:, h % LEAD, :], raw[:, slot, piece], w_high[:, h % LEAD, :].bitcast(f32),
                                  ALU.subtract).then_inc(raw_used if h % 2 else low_first, 1)
                t.add("low")
                if h % 2:
                    t.add("raw")

            def mod_tile(v, kk):
                slot = t.c["raw"] % RAW
                eng.wait_ge(raw_loaded[slot], t.arrived())
                if t.c["raw"]:
                    eng.wait_ge(raw_used, t.at("raw", 0))
                eng.scalar_tensor_tensor(out=mod_acc(v), in0=raw[:, slot, :], scalar=silu_c[:, bass.ds(kk, 1)],
                                         in1=mod_acc(v), op0=ALU.mult, op1=ALU.add).then_inc(raw_used, 1)
                t.add("raw")

            def mod_columns(v, place):
                eng.wait_ge(mod_read, v + 1)
                col = mcol[:, place * KT:(place + 1) * KT]
                src = ps[:, 3, place * KT:(place + 1) * KT]
                if place == 0:
                    link(eng.tensor_copy(col, src))
                    eng.tensor_scalar(shift1[:, :], col, float(SEQ), None, ALU.mult).then_inc(mod_cols, 1)
                elif place == 2:
                    eng.tensor_copy(col, src).then_inc(mod_cols, 1)
                else:
                    eng.scalar_tensor_tensor(out=scale1[:, :], in0=src, scalar=1.0, in1=cols[:, V_G0:V_G0 + KT],
                                             op0=ALU.add, op1=ALU.mult).then_inc(mod_cols, 1)

            def mod_rows(v, loads):
                eng.wait_ge(mod_read, v + 1)
                eng.wait_ge(grow_in, 16 * loads)
                for j in range(NC):
                    piece = grow[:, j * CW:(j + 1) * CW]
                    ins = eng.tensor_tensor(piece, side(j), piece, ALU.mult)
                return ins

            def mean_square():
                t.add("root")
                eng.wait_ge(squared, t.c["squared"])
                link(eng.tensor_reduce(ms[:, :], ssq[:, :].rearrange("p (t c) -> p t c", t=TT), AX.X, ALU.add))
                eng.tensor_scalar(ms[:, :], ms[:, :], 1.0 / D, EPS, ALU.mult, ALU.add).then_inc(ms_ready, 1)

            def invert():
                eng.wait_ge(sd_ready, t.c["root"])
                eng.reciprocal(rstd[:, :], sd[:, :]).then_inc(rstd_ready, 1)
                eng.wait_ge(rstd_ready, t.c["root"])

            def gate(c, dst=None):
                if dst is None:
                    eng.wait_ge(squared, t.c["squared"])
                else:
                    eng.wait_ge(summed, t.c["summed"])
                piece = acc[:, :, c * CW:(c + 1) * CW]
                row = grow[:, c * CW:(c + 1) * CW].unsqueeze(1).to_broadcast([P, TT, CW])
                eng.tensor_tensor(piece if dst is None else dst, piece, row, ALU.mult).then_inc(gated, 1)
                t.add("gated")

            def update(i, last=None):
                j, tt = divmod(i, TT)
                src = acc[:, tt, j * CW:(j + 1) * CW] if last is None or j < NC - 1 else last[:, tt, :]
                piece = xs[:, tt, j * CW:(j + 1) * CW]
                if i == 0:
                    eng.wait_ge(gated, t.c["gated"])
                eng.scalar_tensor_tensor(out=piece, in0=src, scalar=rstd[:, tt:tt + 1],
                                         in1=piece, op0=ALU.mult, op1=ALU.add).then_inc(x_updated, 1)
                t.add("squared")
                t.add("updated")

            def normalize(i):
                j, tt = divmod(i, TT)
                piece = slice(j * CW, (j + 1) * CW)
                if i == 0 and t.c["updated"]:
                    eng.wait_ge(x_updated, t.c["updated"])
                eng.tensor_scalar(acc[:, tt, piece], xs[:, tt, piece], rstd[:, tt:tt + 1], None, ALU.mult)\
                   .then_inc(xn_ready, 1)

            def split_h(i):
                j, tt = divmod(i, TT)
                t.add("norm")
                src = turned[:, i % 2, :].rearrange("p (b n) -> p b n", b=4)
                high = h_high[:, 4 * j:4 * j + 4, tt * P:(tt + 1) * P]
                eng.wait_ge(n_scaled, t.c["norm"])
                eng.tensor_copy(high, src).then_inc(n_high, 1)
                eng.wait_ge(n_high, t.c["norm"])
                eng.tensor_tensor(h_low[:, 4 * j:4 * j + 4, tt * P:(tt + 1) * P], src, high.bitcast(f32),
                                  ALU.subtract).then_inc(n_low, 1)

            def add_step(target, n, c):
                eng.wait_ge(half_used, t.at("done", 0))
                piece = (acc if target is None else target)[:, :, c * CW:(c + 1) * CW]
                if target is None:
                    eng.tensor_copy(piece, lin(n)).then_inc(summed, 1)
                else:
                    eng.tensor_tensor(piece, lin(n), piece, ALU.add).then_inc(summed, 1)
                t.add("summed")
                t.add("squared", TT)

            def gain(c):
                eng.wait_ge(summed, t.at("summed", 0))
                row = grow[:, c * CW:(c + 1) * CW].unsqueeze(1).to_broadcast([P, TT, CW])
                eng.tensor_tensor(acc[:, :, c * CW:(c + 1) * CW], xs[:, :, c * CW:(c + 1) * CW], row, ALU.mult)\
                   .then_inc(final_gained, 1)

            def mlp_body(target, q=0, mods=(), ahead=True, after=None, last=None):
                for y in range(64):
                    if y % HALVES == 7:
                        t.add("done", 8)
                        if y // HALVES >= NC:
                            add_step(target, y // HALVES, y // HALVES - NC)
                    if y == 63 and last is not None:
                        last()
                    if y < 60 or ahead:
                        low_part()
                        if t.c["low"] % 2 == 0 and (y // 2) in mods:
                            mod_tile(5, q * len(mods) + mods.index(y // 2))
                    c, hh = divmod(y, HALVES)
                    if 1 <= c <= NC and hh in (1, 3):
                        tt = hh // 2
                        t.add("t")
                        eng.wait_ge(t_high, t.at("t", 0))
                        high = u_high[:, 4 * (c - 1):4 * c, tt * P:(tt + 1) * P]
                        eng.tensor_tensor(u_low[:, 4 * (c - 1):4 * c, tt * P:(tt + 1) * P],
                                          side(0).rearrange("p (b n) -> p b n", b=4), high.bitcast(f32),
                                          ALU.subtract).then_inc(t_low, 1)
                    if after is not None and hh == 1 and c > NC:
                        after(c - 1 - NC)

            eng.wait_ge(vec_turned, 1)
            eng.tensor_copy(cols[:, :], side(0)[:, 0:V_ALL]).then_inc(vec_ready, 1)
            eng.wait_ge(silu_exp, 1)
            eng.wait_ge(vec_ready, 1)
            link(eng.tensor_scalar(silu_t[:, KT:2 * KT], silu_t[:, 0:KT], 1.0, None, ALU.add))
            link(eng.reciprocal(silu_t[:, 0:KT], silu_t[:, KT:2 * KT]))
            link(eng.tensor_tensor(silu_c[:, :], silu_t[:, 0:KT], cols[:, V_C:V_C + KT], ALU.mult))
            eng.wait_ge(acc_init[0], 16)
            for i in range(2 * RAW):
                mod_tile(0, i)
                if i == 2 * RAW - 2:
                    t.add("squared", TT * NC)
                    mean_square()
            invert()
            with t.loop(eng, 2, KT // RAW, raw=RAW) as q:
                for i in range(RAW):
                    mod_tile(0, q * RAW + i)
            eng.wait_ge(acc_init[1], 16)
            for i in range(2 * RAW):
                mod_tile(1, i)
                if i == 2 * RAW - 1:
                    mod_columns(0, 0)
            with t.loop(eng, 2, KT // RAW, raw=RAW) as q:
                for i in range(RAW):
                    mod_tile(1, q * RAW + i)
            eng.wait_ge(acc_init[2], 16)
            for i in range(GATE_AHEAD):
                mod_tile(2, i)
                if i == 2:
                    mod_columns(1, 1)
                g = i - (GATE_AHEAD - FG)
                if g >= 0:
                    eng.wait_ge(dft_high, g + 1)
                    eng.tensor_tensor(h_low[:, 2 * g:2 * g + 2, :],
                                      lin(g)[:, 0, :].rearrange("p (e s) -> p e s", e=2),
                                      h_high[:, 2 * g:2 * g + 2, :].bitcast(f32), ALU.subtract).then_inc(dft_low, 1)
            behind = [(2, kk) for kk in range(GATE_AHEAD, KT)] + [(3, kk) for kk in range(KT)]

            def next_tile():
                v, kk = behind.pop(0)
                if kk == 0:
                    eng.wait_ge(acc_init[v], 16)
                if (v, kk) == (4, KT - 1):
                    last_scale_tile()
                else:
                    mod_tile(v, kk)

            for y in range(-LEAD, NC * HALVES):
                if y < NC * HALVES - LEAD:
                    low_part()
                    ch = t.c["low"] // 2 - 1
                    if t.c["low"] % 2 == 0 and ch in FNET_AFTER:
                        next_tile()
                elif y < NC * HALVES - 1:
                    next_tile()
                if y < 0:
                    continue
                c, hh = divmod(y, HALVES)
                if hh == 7:
                    t.add("done", 8)
                    add_step(None, c, c)
                if y == 2 * GATE_ROWS + 3:
                    mod_rows(2, 1).then_inc(mod_cols, 1)
                    eng.wait_ge(mod_cols, 3)
                elif y == 2 * GATE_ROWS + 5:
                    gate(0)
                elif y == 2 * GATE_ROWS + 7:
                    gate(1)
            def last_scale_tile():
                slot = t.c["raw"] % RAW
                eng.wait_ge(raw_loaded[slot], t.arrived())
                eng.wait_ge(raw_used, t.c["raw"])
                for part in range(4):
                    piece = slice(part * CW, (part + 1) * CW)
                    sums = mod_acc(4)[:, piece]
                    eng.scalar_tensor_tensor(out=sums, in0=raw[:, slot, piece], scalar=silu_c[:, KT - 1:KT],
                                             in1=sums, op0=ALU.mult, op1=ALU.add)\
                       .then_inc(part_summed if part < 3 else raw_used, 1)
                t.add("raw")

            behind += [(4, kk) for kk in range(KT)]
            left = len(behind)
            for i in range(left):
                next_tile()
                if i == 0:
                    gate(NC - 2)
                elif i == 1:
                    gate(NC - 1)
                    mean_square()
                elif i == 2:
                    invert()
                elif 3 <= i < 11:
                    update(i - 3)
                elif i == 12:
                    mean_square()
                elif i == 13:
                    invert()
                if 13 <= i < 17:
                    for piece in range(TT):
                        normalize(TT * (i - 13) + piece)
                if i == left - KT + 1:
                    mod_columns(3, 2)
            for part in range(4):
                piece = slice(part * KT // 4, (part + 1) * KT // 4)
                eng.wait_ge(part_read, part + 1) if part < 3 else eng.wait_ge(mod_read, 5)
                eng.scalar_tensor_tensor(out=scale2[:, piece], in0=ps[:, TURN_BANKS[4 + part], piece], scalar=1.0,
                                         in1=cols[:, V_G2:V_G2 + KT][:, piece], op0=ALU.add, op1=ALU.mult)\
                   .then_inc(part_cols if part < 3 else mod_cols, 1)
            for i in range(TT * NC):
                split_h(i)
                if i % 2:
                    low_part()
            eng.wait_ge(acc_init[5], 16)
            eng.wait_ge(acc_zero, 1)
            with t.loop(eng, 0, MOD_LOOPS, low=64, raw=32 + len(MOD_AFTER), t=2 * NC, done=64, squared=TT * NC,
                        summed=NC) as q:
                mlp_body(acc, q, MOD_AFTER)
            mod_rows(5, 2).then_inc(mod_cols, 1)
            for q in range(MOD_LOOPS, QUARTERS - 1):
                mlp_body(acc)
            eng.wait_ge(mod_cols, 6)
            mlp_body(acc, after=gate, last=lambda: gate(NC - 1, gated_last))
            mean_square()
            invert()
            for i in range(4):
                update(i, gated_last)
            for i in range(0, TT * NC, 2):
                split_h(i)
                split_h(i + 1)
                if i < 4:
                    update(i + 4, gated_last)
                    update(i + 5, gated_last)

            def forget_low():
                eng.wait_ge(f_high, 1)
                eng.tensor_tensor(wf_low[:, :], wf[:, :], wf_high[:, :].bitcast(f32), ALU.subtract)\
                   .then_inc(f_low, 1)

            def forget_rows():
                eng.wait_ge(f_sum, 1)
                link(eng.tensor_copy(negc[:, :], side(2)[0:HEADS, 0:SEQ]))
                eng.tensor_tensor(negc[:, :], side(2)[0:HEADS, SEQ:2 * SEQ], negc[:, :], ALU.add)\
                   .then_inc(f_rows, 1)

            def forget_logit():
                eng.wait_ge(f_turned, 1)
                for tt in range(TT):
                    s = slice(tt * HEADS, (tt + 1) * HEADS)
                    last = eng.scalar_tensor_tensor(out=fl[:, s], in0=side(3)[:, s], scalar=rstd[:, tt:tt + 1],
                                                    in1=bf[:, s], op0=ALU.mult, op1=ALU.add)
                last.then_inc(f_logit, 1)

            def forget_gate():
                eng.wait_ge(f_exp, 1)
                eng.scalar_tensor_tensor(out=fl[:, :], in0=fl[:, :], scalar=0.0, in1=fe[:, :],
                                         op0=ALU.min, op1=ALU.subtract).then_inc(f_ready, 1)

            def forget_sums():
                eng.wait_ge(c_sum, 1)
                eng.tensor_scalar(negc[:, :], side(3)[0:HEADS, 0:SEQ], -1.0, None, ALU.mult)
                eng.tensor_copy(csum[:, :], side(3)[:, SEQ:SEQ + TT * HEADS]).then_inc(c_ready, 1)

            def turned_qk(n, tt):
                g, r = divmod(n, 3)
                t.add("a")
                eng.wait_ge(a_posed, t.c["a"])
                dst = (qT, kT)[r][:, g % 2, :, tt * P:(tt + 1) * P]
                eng.tensor_copy(dst, side(0).rearrange("p (h n) -> p h n", h=GH)).then_inc(a_turned, 1)

            def mask_scores(g, i):
                n = t.c["z"]
                t.add("z")
                z = zs[:, n % 2, :]
                eng.wait_ge(z_ready, n + 1)
                if n == 0:
                    eng.wait_ge(mask_in, 16)
                if g < 2:
                    eng.tensor_tensor(z, side(1)[:, 0:384], cst[:, C_SB:C_SB + 384], ALU.add).then_inc(z_taken, 1)
                    return
                head = GH * (g - 2) + i
                for tt, (a, b) in enumerate(((0, P), (P, 384))):
                    last = eng.scalar_tensor_tensor(
                        out=z[:, a:b], in0=side(1)[:, a:b], scalar=csum[:, tt * HEADS + head:tt * HEADS + head + 1],
                        in1=cst[:, C_FOX + a:C_FOX + b], op0=ALU.add, op1=ALU.add)
                last.then_inc(z_taken, 1)
                eng.wait_ge(z_taken, n + 1)
                for tt, (a, b) in enumerate(((0, P), (P, 384))):
                    last = eng.tensor_reduce(negmax[:, tt * GH + i:tt * GH + i + 1], z[:, a:b], AX.X, ALU.max,
                                             negate=True)
                last.then_inc(mid_in, 1)

            def keep_logs(g, i):
                n = t.c["z"] - 1
                if g < 2:
                    e = ew[:, n % 2, :]
                    eng.wait_ge(z_logs, n + 1)
                    eng.scalar_tensor_tensor(out=e, in0=zs[:, n % 2, :], scalar=0.0, in1=e, op0=ALU.max,
                                             op1=ALU.add).then_inc(mid_in, 1)

            def take_middle(g, i):
                n = t.c["mid"]
                t.add("mid")
                eng.wait_ge(mid_ready, n + 1)
                if g < 2:
                    eng.tensor_tensor(ew[:, n % 2, :], zs[:, n % 2, :], side(2)[:, 0:384], ALU.subtract)\
                       .then_inc(mid_taken, 1)

            def take_out(g, i):
                n = t.c["o"]
                t.add("o")
                eng.wait_ge(o_ready, n + 1)
                if g < 2:
                    eng.tensor_copy(heads[:, :, i * HD:(i + 1) * HD],
                                    side(3)[:, 0:TT * HD].rearrange("p (t n) -> p t n", t=TT)).then_inc(o_taken, 1)
                else:
                    for tt in range(TT):
                        s = slice(tt * GH + i, tt * GH + i + 1)
                        ins = eng.reciprocal(precip[:, s], psums[:, s])
                    link(ins)
                    for tt in range(TT):
                        last = eng.tensor_scalar(heads[:, tt, i * HD:(i + 1) * HD], side(3)[:, tt * HD:(tt + 1) * HD],
                                                 precip[:, tt * GH + i:tt * GH + i + 1], None, ALU.mult)
                    last.then_inc(o_taken, 1)
                own, squares = heads[:, :, i * HD:(i + 1) * HD], normed[:, :, i * HD:(i + 1) * HD]
                sums = hms[:, :].rearrange("p (t h) -> p t h", t=TT)[:, :, i]
                eng.wait_ge(o_taken, n + 1)
                if g and i == 0:
                    eng.wait_ge(m_posed, 2 * g)
                link(eng.tensor_tensor(squares, own, own, ALU.mult))
                link(eng.tensor_reduce(sums, squares, AX.X, ALU.add))
                if i == GH - 1:
                    flat = normed.rearrange("p t (h n) -> p (t h) n", n=HD)
                    src = heads.rearrange("p t (h n) -> p (t h) n", n=HD)
                    eng.tensor_scalar(hms[:, :], hms[:, :], 1.0 / HD, EPS, ALU.mult, ALU.add).then_inc(hms_ready, 1)
                    eng.wait_ge(hsd_ready, g + 1)
                    link(eng.reciprocal(hrs[:, :], hsd[:, :]))
                    eng.tensor_tensor(flat, src, hrs[:, :].unsqueeze(2).to_broadcast([P, TT * GH, HD]), ALU.mult)\
                       .then_inc(mixed_ready, 1)

            def take_mixed(g, tt):
                src = fin[:, :].rearrange("p (b n) -> p b n", b=4)
                high = u_high[:, 4 * g:4 * g + 4, tt * P:(tt + 1) * P]
                eng.wait_ge(m_scaled, 2 * g + tt + 1)
                eng.tensor_copy(high, src).then_inc(m_high, 1)
                eng.wait_ge(m_high, 2 * g + tt + 1)
                eng.tensor_tensor(u_low[:, 4 * g:4 * g + 4, tt * P:(tt + 1) * P], src, high.bitcast(f32),
                                  ALU.subtract).then_inc(m_low, 1)

            def attention(g, jobs):
                for job, i in jobs:
                    {"z": mask_scores, "mid": take_middle, "out": take_out, "turn": take_mixed}[job](g, i)
                for job, i in jobs:
                    if job == "z":
                        keep_logs(g, i)

            forget_low()
            for n in range(3 * GROUPS):
                g, r = divmod(n, 3)
                for hh in range(HALVES):
                    low_part()
                    if hh in (1, 3) and n % 3:
                        turned_qk(n - 1, hh // 2)
                    if n == 0 and hh == 5:
                        mean_square()
                        invert()
                        eng.tensor_scalar(rstd_q[:, :], rstd[:, :], float(HD) ** -0.5, None, ALU.mult)\
                           .then_inc(rstd_q_ready, 1)
                    if n == 1 and hh == 2:
                        forget_rows()
                    if n == 1 and hh == 5:
                        forget_logit()
                    if n == 2 and hh == 0:
                        forget_gate()
                    if n == 2 and hh == 6:
                        forget_sums()
                    if g:
                        attention(g - 1, SLOTS.get(r * HALVES + hh, ()))
            t.add("done", 8 * 3 * GROUPS)
            done = t.c["done"]
            for y, (c, j) in enumerate([o for o in OUT_ORDER for _ in range(2)]):
                if j == 3 and y % 2:
                    t.c["done"] = done + y + 1
                    add_step(xs, c, c)
                low_part()
                attention(GROUPS - 1, LAST_SLOTS.get(y, ()))
                if y in PLAIN_TURNS:
                    for tt in range(TT):
                        split_h(TT * PLAIN_TURNS[y] + tt)
            for tt in range(TT):
                split_h(TT * (NC - 1) + tt)
            mean_square()
            invert()
            with t.loop(eng, 0, QUARTERS - 1, low=64, raw=32, t=2 * NC, done=64, squared=TT * NC, summed=NC) as q:
                mlp_body(xs)
            eng.wait_ge(grow_in, 48)
            mlp_body(xs, ahead=False, after=gain, last=lambda: gain(NC - 1))
            mean_square()
            invert()
            eng.wait_ge(final_gained, NC)
            for part in range(2):
                piece = acc[:, 1, part * D // 2:(part + 1) * D // 2]
                eng.tensor_scalar(piece, piece, rstd[:, 1:2], None, ALU.mult).then_inc(final_second, 1)


def shape_constants():
    i, j = np.arange(P)[:, None], np.arange(P)[None, :]
    f = np.float32
    tri = lambda ok: np.where(ok, f(0), f(MASKED))
    zero = np.zeros((P, P), f)
    later, upto = tri(i < j), tri(j <= i)
    consts = np.concatenate([np.eye(P, dtype=f), (i >= j).astype(f), (i <= j).astype(f), np.ones((P, P), f),
                             later, zero, later, upto, zero, upto], axis=1)
    n = np.arange(SEQ)
    angle = 2.0 * np.pi * ((n[:, None] * n[None, :]) % SEQ) / SEQ
    cos, sin = np.cos(angle), np.sin(angle)
    dft = np.concatenate([cos, sin, -sin], axis=1).astype(f)
    select = np.repeat(np.eye(HEADS, dtype=f)[:, :, None], P, axis=2)
    return consts.astype(f), dft, select


def kernel(x, c, ctx, c_ctx, w_mod, b_mod, norm_g, w_mlp_in, w_mlp_out, fnet_w_out, hgrn_w_in, hgrn_lb,
           hgrn_gnorm, hgrn_w_out, diff_w_qkv, diff_lambda, diff_subln, diff_w_out, g_attn_2, w_in_2,
           b_f_2, g_out_sb_2, g_out_fox_2, w_out_2, g_mlp_2, w_up_2, w_down_2, g_final_2):
    import concourse.bacc as bacc
    from concourse.bass_utils import run_bass_kernel_spmd

    consts, dft, select = shape_constants()
    two_d = lambda a: np.ascontiguousarray(np.asarray(a)).reshape(-1, np.asarray(a).shape[-1])
    given = [("x", two_d(x)), ("c", two_d(c)), ("w_mod", two_d(w_mod)), ("b_mod", two_d(b_mod)),
             ("norm_g", two_d(norm_g)), ("w_mlp_in", two_d(w_mlp_in)), ("w_mlp_out", two_d(w_mlp_out)),
             ("fnet_w", two_d(fnet_w_out)), ("g_attn", two_d(g_attn_2)), ("w_in", two_d(w_in_2)),
             ("b_f", two_d(b_f_2)), ("g_out_sb", two_d(g_out_sb_2)), ("g_out_fox", two_d(g_out_fox_2)),
             ("w_out", two_d(w_out_2)), ("g_mlp", two_d(g_mlp_2)), ("w_up", two_d(w_up_2)),
             ("w_down", two_d(w_down_2)), ("g_final", two_d(g_final_2)), ("consts", consts), ("dft", dft),
             ("select", select)]
    nc = bacc.Bacc("TRN2", target_bir_lowering=False, num_devices=1)
    arrays, args = {}, []
    for name, a in given:
        arrays[f"in_{name}"] = a
        args.append(nc.dram_tensor(f"in_{name}", a.shape, mybir.dt.from_np(a.dtype), kind="ExternalInput").ap())
    args.append(nc.dram_tensor("out_x", (SEQ, D), mybir.dt.float32, kind="ExternalOutput").ap())
    program(nc, *args)
    r = run_bass_kernel_spmd(nc, [arrays], core_ids=[0])
    return r.results[0]["out_x"].reshape(1, SEQ, D)
```
